# Optimizing a Trainium2 kernel written in Bass

```python
import jax
import jax.numpy as jnp
from jax import lax
import numpy as np

D_MODEL = 1024
BATCH = 1
SEQ = 256
DEPTH = 2

CHUNK = 64
Q_BLOCK = 128
N_HEADS = 4
HEAD_DIM = 128
BRANCH_W = N_HEADS * HEAD_DIM
RET_DK = HEAD_DIM
RET_DV = HEAD_DIM
GLA_DK = HEAD_DIM // 2
GLA_DV = HEAD_DIM
GLA_LOWRANK = 16
GLA_TAU = 16.0
FOX_D = HEAD_DIM
N_BRANCH = 3
D_FF = 2816
CONV_W = 3
ROPE_BASE = 10000.0
EPS = 1e-6

IN_SPLITS = (
    N_HEADS * RET_DK, N_HEADS * RET_DK, N_HEADS * RET_DV, N_HEADS * RET_DV,
    N_HEADS * GLA_DK, N_HEADS * GLA_DK, N_HEADS * GLA_DV, GLA_LOWRANK, N_HEADS * GLA_DV,
    N_HEADS * FOX_D, N_HEADS * FOX_D, N_HEADS * FOX_D, N_HEADS,
)
IN_W = sum(IN_SPLITS)


F32 = jnp.float32

def rms_norm(x, g):
    xf = x.astype(F32)
    y = xf * lax.rsqrt(jnp.mean(xf * xf, axis=-1, keepdims=True) + EPS)
    return (y * g).astype(x.dtype)

def head_group_norm(x, g):
    xf = x.astype(F32)
    mu = jnp.mean(xf, axis=-1, keepdims=True)
    xc = xf - mu
    return xc * lax.rsqrt(jnp.mean(xc * xc, axis=-1, keepdims=True) + EPS) * g

def modulate(h, shift, scale):
    return h * (1.0 + scale[:, None, :]) + shift[:, None, :]

def rotary(x, pos):
    half = x.shape[-1] // 2
    inv_freq = ROPE_BASE ** (-jnp.arange(half, dtype=F32) / half)
    ang = pos[:, None] * inv_freq[None, :]
    cos = jnp.cos(ang)[None, :, None, :]
    sin = jnp.sin(ang)[None, :, None, :]
    x1, x2 = x[..., :half], x[..., half:]
    return jnp.concatenate([x1 * cos - x2 * sin, x1 * sin + x2 * cos], axis=-1)

def retention(q, k, v):
    b, s, h, dk = q.shape
    dv = v.shape[-1]
    n = s // CHUNK
    pos = jnp.arange(s, dtype=F32)
    q = rotary(q.astype(F32), pos)
    k = rotary(k.astype(F32), pos) * dk ** -0.5
    v = v.astype(F32)
    log_g = jnp.log1p(-jnp.exp2(-5.0 - jnp.arange(h, dtype=F32)))
    idx = jnp.arange(CHUNK, dtype=F32)
    d_intra = jnp.exp(jnp.abs(idx[:, None] - idx[None, :])[None] * log_g[:, None, None])
    qc = q.reshape(b, n, CHUNK, h, dk)
    kc = k.reshape(b, n, CHUNK, h, dk)
    vc = v.reshape(b, n, CHUNK, h, dv)
    scores = jnp.einsum('bnihd,bnjhd->bnhij', qc, kc) * d_intra
    o_intra = jnp.einsum('bnhij,bnjhe->bnihe', scores, vc)
    k_w = jnp.exp((CHUNK - 1.0 - idx)[:, None] * log_g[None, :])
    kv = jnp.einsum('bnjhd,bnjhe->nbhde', kc * k_w[:, :, None], vc)
    g_chunk = jnp.exp(CHUNK * log_g)[None, :, None, None]

    def step(r, kv_n):
        return g_chunk * r + kv_n, r

    _, r_prev = lax.scan(step, jnp.zeros((b, h, dk, dv), F32), kv)
    q_w = jnp.exp((idx + 1.0)[:, None] * log_g[None, :])
    o_cross = jnp.einsum('bnihd,nbhde->bnihe', qc * q_w[:, :, None], r_prev)
    return (o_intra + o_cross).reshape(b, s, h, dv)

def gla(q, k, v, log_a):
    b, s, h, dk = q.shape
    dv = v.shape[-1]
    n = s // CHUNK
    qc = (q.astype(F32) * dk ** -0.5).reshape(b, n, CHUNK, h, dk)
    kc = k.astype(F32).reshape(b, n, CHUNK, h, dk)
    vc = v.astype(F32).reshape(b, n, CHUNK, h, dv)
    la = log_a.astype(F32).reshape(b, n, CHUNK, h, dk)
    b_cum = jnp.cumsum(la, axis=2)
    b_end = b_cum[:, :, -1:]
    kv = jnp.einsum('bnjhd,bnjhe->nbhde', kc * jnp.exp(b_end - b_cum), vc)
    a = jnp.exp(b_end[:, :, 0]).transpose(1, 0, 2, 3)

    def step(st, inp):
        a_n, kv_n = inp
        st = a_n[..., None] * st + kv_n
        return st, st

    _, s_all = lax.scan(step, jnp.zeros((b, h, dk, dv), F32), (a, kv))
    o = jnp.einsum('bnihd,nbhde->bnihe', qc, s_all)
    return o.reshape(b, s, h, dv)

def forgetting_attention(q, k, v, f_logit):
    b, s, h, d = q.shape
    log_f = jax.nn.log_sigmoid(f_logit.astype(F32))
    cum = jnp.cumsum(log_f, axis=1).transpose(0, 2, 1)
    outs = []
    for blk in range(s // Q_BLOCK):
        q0 = blk * Q_BLOCK
        q1 = q0 + Q_BLOCK
        logits = jnp.einsum('bihd,bjhd->bhij', q[:, q0:q1], k[:, :q1]).astype(F32) * d ** -0.5
        logits = logits + cum[:, :, q0:q1, None] - cum[:, :, None, :q1]
        mask = jnp.arange(q0, q1)[:, None] >= jnp.arange(q1)[None, :]
        p = jax.nn.softmax(jnp.where(mask, logits, -jnp.inf), axis=-1).astype(v.dtype)
        outs.append(jnp.einsum('bhij,bjhe->bihe', p, v[:, :q1]))
    return jnp.concatenate(outs, axis=1)

def causal_dwconv(u, w, bias):
    s = u.shape[1]
    up = jnp.pad(u, ((0, 0), (CONV_W - 1, 0), (0, 0)))
    out = bias
    for j in range(CONV_W):
        out = out + w[j] * up[:, j:j + s]
    return out

def hybrid_layer(x, c_act, norm1_g, norm2_g, w_ada, b_ada, w_in, w_gla_a2, b_gla_a, b_fox_f,
                 ret_norm_g, gla_norm_g, q_norm_g, k_norm_g, w_br, w_mg, b_mg, w_o,
                 w_up, w_conv, b_conv, w_down):
    b, s = x.shape[0], x.shape[1]
    mod = c_act @ w_ada + b_ada
    shift1, scale1, gate1, shift2, scale2, gate2 = jnp.split(mod, 6, axis=-1)

    h = modulate(rms_norm(x, norm1_g), shift1, scale1)
    split_points = np.cumsum(IN_SPLITS)[:-1].tolist()
    (rq, rk, rv, rg, gq, gk, gv, glr, gg, fq, fk, fv, ff) = jnp.split(h @ w_in, split_points, axis=-1)

    def heads(t, d):
        return t.reshape(b, s, N_HEADS, d)

    ret = retention(heads(rq, RET_DK), heads(rk, RET_DK), heads(rv, RET_DV))
    ret = head_group_norm(ret, ret_norm_g.reshape(N_HEADS, RET_DV)).reshape(b, s, BRANCH_W)
    ret = jax.nn.silu(rg) * ret

    log_a = jax.nn.log_sigmoid((glr @ w_gla_a2 + b_gla_a).astype(F32)) / GLA_TAU
    gla_o = gla(heads(gq, GLA_DK), heads(gk, GLA_DK), heads(gv, GLA_DV), heads(log_a, GLA_DK))
    gla_o = rms_norm(gla_o, gla_norm_g).reshape(b, s, BRANCH_W)
    gla_o = jax.nn.silu(gg) * gla_o

    fox_o = forgetting_attention(rms_norm(heads(fq, FOX_D), q_norm_g),
                                 rms_norm(heads(fk, FOX_D), k_norm_g),
                                 heads(fv, FOX_D), ff + b_fox_f).reshape(b, s, BRANCH_W)

    branches = jnp.stack([ret, gla_o, fox_o], axis=2).astype(h.dtype)
    y_br = jnp.einsum('bsnw,nwd->bsnd', branches, w_br)
    gates = jax.nn.sigmoid(h @ w_mg + b_mg).reshape(b, s, N_BRANCH, D_MODEL)
    mixed = jnp.sum(gates * y_br, axis=2) @ w_o
    x = x + (gate1[:, None, :] * mixed).astype(x.dtype)

    h2 = modulate(rms_norm(x, norm2_g), shift2, scale2)
    u, g = jnp.split(h2 @ w_up, 2, axis=-1)
    u = causal_dwconv(u, w_conv, b_conv)
    y = (jax.nn.silu(u) * g) @ w_down
    x = x + (gate2[:, None, :] * y).astype(x.dtype)
    return x

def first_inputs(seed: int = 0) -> dict:
    key = jax.random.key(seed)
    ks = jax.random.split(key, 24)

    def nrm(k, shape, scale):
        return jax.random.normal(k, shape, F32) * scale

    L, D = DEPTH, D_MODEL
    return {
        'x': nrm(ks[0], (BATCH, SEQ, D), 1.0),
        'c': nrm(ks[1], (BATCH, D), 1.0),
        'norm1_g': 1.0 + nrm(ks[2], (L, D), 0.02),
        'norm2_g': 1.0 + nrm(ks[3], (L, D), 0.02),
        'w_ada': nrm(ks[4], (L, D, 6 * D), 0.5 * D ** -0.5),
        'b_ada': nrm(ks[5], (L, 6 * D), 0.02),
        'w_in': nrm(ks[6], (L, D, IN_W), D ** -0.5),
        'w_gla_a2': nrm(ks[7], (L, GLA_LOWRANK, N_HEADS * GLA_DK), GLA_LOWRANK ** -0.5),
        'b_gla_a': nrm(ks[8], (L, N_HEADS * GLA_DK), 0.1),
        'b_fox_f': 1.0 + nrm(ks[9], (L, N_HEADS), 0.1),
        'ret_norm_g': 1.0 + nrm(ks[10], (L, N_HEADS * RET_DV), 0.02),
        'gla_norm_g': 1.0 + nrm(ks[11], (L, GLA_DV), 0.02),
        'q_norm_g': 1.0 + nrm(ks[12], (L, FOX_D), 0.02),
        'k_norm_g': 1.0 + nrm(ks[13], (L, FOX_D), 0.02),
        'w_br': nrm(ks[14], (L, N_BRANCH, BRANCH_W, D), BRANCH_W ** -0.5),
        'w_mg': nrm(ks[15], (L, D, N_BRANCH * D), D ** -0.5),
        'b_mg': nrm(ks[16], (L, N_BRANCH * D), 0.02),
        'w_o': nrm(ks[17], (L, D, D), D ** -0.5),
        'w_up': nrm(ks[18], (L, D, 2 * D_FF), D ** -0.5),
        'w_conv': nrm(ks[19], (L, CONV_W, D_FF), CONV_W ** -0.5),
        'b_conv': nrm(ks[20], (L, D_FF), 0.02),
        'w_down': nrm(ks[21], (L, D_FF, D), D_FF ** -0.5),
    }

def first_block(x, c, norm1_g, norm2_g, w_ada, b_ada, w_in, w_gla_a2, b_gla_a, b_fox_f,
              ret_norm_g, gla_norm_g, q_norm_g, k_norm_g, w_br, w_mg, b_mg, w_o,
              w_up, w_conv, b_conv, w_down):
    c_act = jax.nn.silu(c)
    for l in range(DEPTH):
        x = hybrid_layer(x, c_act, norm1_g[l], norm2_g[l], w_ada[l], b_ada[l], w_in[l],
                         w_gla_a2[l], b_gla_a[l], b_fox_f[l], ret_norm_g[l], gla_norm_g[l],
                         q_norm_g[l], k_norm_g[l], w_br[l], w_mg[l], b_mg[l], w_o[l],
                         w_up[l], w_conv[l], b_conv[l], w_down[l])
    return x


D_PLE = 256
N_EVEN = (DEPTH + 1) // 2
N_ODD = DEPTH // 2
A_HEADS = 8
A_KV_HEADS = 2
A_GROUP = A_HEADS // A_KV_HEADS
A_HEAD_DIM = 64
A_WIDTH = A_HEADS * A_HEAD_DIM
A_KV_WIDTH = A_KV_HEADS * A_HEAD_DIM
A_WINDOW = 128
A_PREV_CHUNKS = A_WINDOW // CHUNK
B_WIDTH = 512
B_BLOCKS = 8
B_BLOCK = B_WIDTH // B_BLOCKS
B_CONV = 4
RG_C = 8.0
AB_PROJ = A_WIDTH + 2 * A_KV_WIDTH + 2 * B_WIDTH
C_HEADS = 8
C_HEAD_DIM = 128
C_WIDTH = C_HEADS * C_HEAD_DIM
C_CONV = 4
C_PROJ = 4 * C_WIDTH + 2 * C_HEADS
DN_ALPHA = (2.0 * DEPTH) ** 0.25
DN_BETA = (8.0 * DEPTH) ** -0.25
LN_EPS = 1e-5
NORM_EPS = 1e-6
NEG = -1e30


def layer_norm(x, g, b):
    xf = x.astype(jnp.float32)
    mu = jnp.mean(xf, -1, keepdims=True)
    var = jnp.mean(jnp.square(xf - mu), -1, keepdims=True)
    return ((xf - mu) * lax.rsqrt(var + LN_EPS) * g + b).astype(x.dtype)

def swiglu(x, wg, wu, wd):
    return (jax.nn.silu(x @ wg) * (x @ wu)) @ wd

def causal_dwconv_2(x, w):
    k, s = w.shape[0], x.shape[1]
    xp = jnp.pad(x, ((0, 0), (k - 1, 0), (0, 0)))
    y = xp[:, 0:s] * w[0]
    for j in range(1, k):
        y = y + xp[:, j:j + s] * w[j]
    return y

def chunk_band(t, n_prev):
    b, s = t.shape[:2]
    nc = s // CHUNK
    pad = n_prev * CHUNK
    tp = jnp.pad(t, ((0, 0), (pad, 0), (0, 0), (0, 0)))
    return jnp.concatenate(
        [tp[:, j * CHUNK:j * CHUNK + s].reshape(b, nc, CHUNK, *t.shape[2:]) for j in range(n_prev + 1)],
        axis=2)

def alibi_slopes(n):
    return 2.0 ** (-8.0 * jnp.arange(1, n + 1, dtype=jnp.float32) / n)

def sliding_window_sink_attention(q, k, v, sinks):
    b, s = q.shape[:2]
    nc = s // CHUNK
    pad = A_PREV_CHUNKS * CHUNK
    nk = pad + CHUNK
    qb = q.reshape(b, nc, CHUNK, A_KV_HEADS, A_GROUP, A_HEAD_DIM)
    kb = chunk_band(k, A_PREV_CHUNKS)
    vb = chunk_band(v, A_PREV_CHUNKS)
    sc = jnp.einsum('bnckgd,bnskd->bnkgcs', qb, kb).astype(jnp.float32) * (A_HEAD_DIM ** -0.5)
    dist = jnp.abs(jnp.arange(CHUNK)[:, None] + pad - jnp.arange(nk)[None, :]).astype(jnp.float32)
    slopes = alibi_slopes(A_HEADS).reshape(A_KV_HEADS, A_GROUP)
    valid = (jnp.arange(nc)[:, None] * CHUNK + jnp.arange(nk)[None, :] - pad) >= 0
    sc = sc - slopes[:, :, None, None] * dist
    sc = jnp.where(valid[None, :, None, None, None, :], sc, NEG)
    sink = sinks.astype(jnp.float32).reshape(A_KV_HEADS, A_GROUP)[:, :, None]
    m = jnp.maximum(sc.max(-1), sink)
    pr = jnp.exp(sc - m[..., None])
    den = pr.sum(-1) + jnp.exp(sink - m)
    o = jnp.einsum('bnkgcs,bnskd->bnckgd', pr / den[..., None], vb.astype(jnp.float32))
    return o.reshape(b, s, A_WIDTH).astype(q.dtype)

def rg_lru(x, w_a, b_a, w_x, b_x, lam):
    xb = x.reshape(*x.shape[:2], B_BLOCKS, B_BLOCK)
    r = jax.nn.sigmoid(jnp.einsum('bshi,hij->bshj', xb, w_a).reshape(x.shape) + b_a)
    i = jax.nn.sigmoid(jnp.einsum('bshi,hij->bshj', xb, w_x).reshape(x.shape) + b_x)
    log_a = (-RG_C * r * jax.nn.softplus(-lam)).astype(jnp.float32)
    a = jnp.exp(log_a)
    u = jnp.sqrt(-jnp.expm1(2.0 * log_a)) * (i * x).astype(jnp.float32)

    def combine(c1, c2):
        a1, b1 = c1
        a2, b2 = c2
        return a1 * a2, a2 * b1 + b2

    _, h = lax.associative_scan(combine, (a, u), axis=1)
    return h.astype(x.dtype)

def mixer_ab(x, w_in, sinks, conv_w, conv_b, w_a, b_a, w_x, b_x, lam, w_out):
    b, s = x.shape[:2]
    proj = x @ w_in
    o1 = A_WIDTH
    o2 = o1 + A_KV_WIDTH
    o3 = o2 + A_KV_WIDTH
    o4 = o3 + B_WIDTH
    q = proj[..., :o1].reshape(b, s, A_HEADS, A_HEAD_DIM)
    k = proj[..., o1:o2].reshape(b, s, A_KV_HEADS, A_HEAD_DIM)
    v = proj[..., o2:o3].reshape(b, s, A_KV_HEADS, A_HEAD_DIM)
    bx = proj[..., o3:o4]
    bg = proj[..., o4:]
    ya = sliding_window_sink_attention(q, k, v, sinks)
    bx = causal_dwconv_2(bx, conv_w) + conv_b
    yb = rg_lru(bx, w_a, b_a, w_x, b_x, lam) * jax.nn.gelu(bg)
    return jnp.concatenate([ya, yb], axis=-1) @ w_out

def gated_delta_rule(q, k, v, g, beta):
    f32 = jnp.float32
    b, s, h, dk = q.shape
    dv = v.shape[-1]
    nc = s // CHUNK

    def to_chunks(t):
        return t.astype(f32).reshape(b, nc, CHUNK, h, -1).transpose(1, 0, 3, 2, 4)

    q = to_chunks(q) * (dk ** -0.5)
    k = to_chunks(k)
    v = to_chunks(v)
    g = g.astype(f32).reshape(b, nc, CHUNK, h).transpose(1, 0, 3, 2)
    beta = beta.astype(f32).reshape(b, nc, CHUNK, h).transpose(1, 0, 3, 2)
    gc = jnp.cumsum(g, axis=-1)
    tril = jnp.tril(jnp.ones((CHUNK, CHUNK), bool))
    strict = jnp.tril(jnp.ones((CHUNK, CHUNK), bool), -1)
    diff = gc[..., :, None] - gc[..., None, :]
    decay = jnp.where(tril, jnp.exp(jnp.where(tril, diff, 0.0)), 0.0)
    kb = k * beta[..., None]
    lmat = jnp.where(strict, jnp.einsum('nbhid,nbhjd->nbhij', kb, k) * decay, 0.0)
    amat = lmat + jnp.eye(CHUNK, dtype=f32)
    u = lax.linalg.triangular_solve(amat, v * beta[..., None], left_side=True, lower=True, unit_diagonal=True)
    w = lax.linalg.triangular_solve(amat, kb * jnp.exp(gc)[..., None], left_side=True, lower=True, unit_diagonal=True)
    attn = jnp.einsum('nbhid,nbhjd->nbhij', q, k) * decay
    qg = q * jnp.exp(gc)[..., None]
    kdec = k * jnp.exp(gc[..., -1:] - gc)[..., None]
    glast = jnp.exp(gc[..., -1])

    def step(state, xs):
        qg_n, kdec_n, w_n, u_n, attn_n, gl_n = xs
        v_new = u_n - jnp.einsum('bhcd,bhde->bhce', w_n, state)
        o = jnp.einsum('bhcd,bhde->bhce', qg_n, state) + jnp.einsum('bhij,bhje->bhie', attn_n, v_new)
        state = state * gl_n[..., None, None] + jnp.einsum('bhcd,bhce->bhde', kdec_n, v_new)
        return state, o

    s0 = jnp.zeros((b, h, dk, dv), f32)
    _, o = lax.scan(step, s0, (qg, kdec, w, u, attn, glast))
    return o.transpose(1, 0, 3, 2, 4).reshape(b, s, h, dv)

def mixer_c(x, w_in, conv_w, a_log, dt_bias, norm_g, w_out):
    b, s = x.shape[:2]
    proj = x @ w_in
    qkv = jax.nn.silu(causal_dwconv_2(proj[..., :3 * C_WIDTH], conv_w))
    z = proj[..., 3 * C_WIDTH:4 * C_WIDTH].reshape(b, s, C_HEADS, C_HEAD_DIM)
    b_logit = proj[..., 4 * C_WIDTH:4 * C_WIDTH + C_HEADS]
    a_in = proj[..., 4 * C_WIDTH + C_HEADS:]
    q = qkv[..., :C_WIDTH].reshape(b, s, C_HEADS, C_HEAD_DIM).astype(jnp.float32)
    k = qkv[..., C_WIDTH:2 * C_WIDTH].reshape(b, s, C_HEADS, C_HEAD_DIM).astype(jnp.float32)
    v = qkv[..., 2 * C_WIDTH:].reshape(b, s, C_HEADS, C_HEAD_DIM)
    q = q * lax.rsqrt(jnp.sum(q * q, -1, keepdims=True) + NORM_EPS)
    k = k * lax.rsqrt(jnp.sum(k * k, -1, keepdims=True) + NORM_EPS)
    beta = jax.nn.sigmoid(b_logit.astype(jnp.float32))
    g = -jnp.exp(a_log.astype(jnp.float32)) * jax.nn.softplus((a_in + dt_bias).astype(jnp.float32))
    o = gated_delta_rule(q, k, v, g, beta)
    o = o * lax.rsqrt(jnp.mean(o * o, -1, keepdims=True) + NORM_EPS) * norm_g
    o = (o * jax.nn.silu(z.astype(jnp.float32))).astype(x.dtype)
    return o.reshape(b, s, C_WIDTH) @ w_out

def second_inputs(seed: int = 0) -> dict:
    key = jax.random.key(seed)
    ks = iter(jax.random.split(key, 48))
    f32 = jnp.float32

    def nrm(shape, scale):
        return jax.random.normal(next(ks), shape, f32) * scale

    d = D_MODEL
    x = nrm((BATCH, SEQ, d), 1.0)
    p = nrm((DEPTH, BATCH, SEQ, D_PLE), 1.0)
    ffn1_wg = nrm((DEPTH, d, D_FF), d ** -0.5)
    ffn1_wu = nrm((DEPTH, d, D_FF), d ** -0.5)
    ffn1_wd = nrm((DEPTH, D_FF, d), DN_BETA * D_FF ** -0.5)
    ffn2_wg = nrm((DEPTH, d, D_FF), d ** -0.5)
    ffn2_wu = nrm((DEPTH, d, D_FF), d ** -0.5)
    ffn2_wd = nrm((DEPTH, D_FF, d), DN_BETA * D_FF ** -0.5)
    ln_g = 1.0 + nrm((DEPTH, 3, d), 0.02)
    ln_b = nrm((DEPTH, 3, d), 0.02)
    ple_wg = nrm((DEPTH, d, d), d ** -0.5)
    ple_bg = nrm((DEPTH, d), 0.02)
    ple_wp = nrm((DEPTH, D_PLE, d), D_PLE ** -0.5)
    ab_w_in = nrm((N_EVEN, d, AB_PROJ), d ** -0.5)
    a_sinks = nrm((N_EVEN, A_HEADS), 0.5)
    b_conv_w = nrm((N_EVEN, B_CONV, B_WIDTH), B_CONV ** -0.5)
    b_conv_b = nrm((N_EVEN, B_WIDTH), 0.02)
    b_wa = nrm((N_EVEN, B_BLOCKS, B_BLOCK, B_BLOCK), B_BLOCK ** -0.5)
    b_ba = nrm((N_EVEN, B_WIDTH), 0.02)
    b_wx = nrm((N_EVEN, B_BLOCKS, B_BLOCK, B_BLOCK), B_BLOCK ** -0.5)
    b_bx = nrm((N_EVEN, B_WIDTH), 0.02)
    a_c = jax.random.uniform(next(ks), (N_EVEN, B_WIDTH), f32, 0.9, 0.999)
    a0 = a_c ** (1.0 / RG_C)
    b_lam = jnp.log(a0) - jnp.log1p(-a0)
    ab_w_out = nrm((N_EVEN, A_WIDTH + B_WIDTH, d), DN_BETA * (A_WIDTH + B_WIDTH) ** -0.5)
    c_w_in = nrm((N_ODD, d, C_PROJ), d ** -0.5)
    c_conv_w = nrm((N_ODD, C_CONV, 3 * C_WIDTH), C_CONV ** -0.5)
    c_a_log = jnp.log(jax.random.uniform(next(ks), (N_ODD, C_HEADS), f32, 1.0, 16.0))
    dt = jnp.exp(jax.random.uniform(next(ks), (N_ODD, C_HEADS), f32, np.log(1e-3), np.log(1e-1)))
    c_dt_bias = dt + jnp.log(-jnp.expm1(-dt))
    c_norm_g = 1.0 + nrm((N_ODD, C_HEAD_DIM), 0.02)
    c_w_out = nrm((N_ODD, C_WIDTH, d), DN_BETA * C_WIDTH ** -0.5)
    return {'x': x, 'p': p,
            'ffn1_wg': ffn1_wg, 'ffn1_wu': ffn1_wu, 'ffn1_wd': ffn1_wd,
            'ffn2_wg': ffn2_wg, 'ffn2_wu': ffn2_wu, 'ffn2_wd': ffn2_wd,
            'ln_g': ln_g, 'ln_b': ln_b,
            'ple_wg': ple_wg, 'ple_bg': ple_bg, 'ple_wp': ple_wp,
            'ab_w_in': ab_w_in, 'a_sinks': a_sinks,
            'b_conv_w': b_conv_w, 'b_conv_b': b_conv_b,
            'b_wa': b_wa, 'b_ba': b_ba, 'b_wx': b_wx, 'b_bx': b_bx, 'b_lam': b_lam,
            'ab_w_out': ab_w_out,
            'c_w_in': c_w_in, 'c_conv_w': c_conv_w, 'c_a_log': c_a_log, 'c_dt_bias': c_dt_bias,
            'c_norm_g': c_norm_g, 'c_w_out': c_w_out}

def second_block(x, p, ffn1_wg, ffn1_wu, ffn1_wd, ffn2_wg, ffn2_wu, ffn2_wd, ln_g, ln_b,
              ple_wg, ple_bg, ple_wp, ab_w_in, a_sinks, b_conv_w, b_conv_b,
              b_wa, b_ba, b_wx, b_bx, b_lam, ab_w_out,
              c_w_in, c_conv_w, c_a_log, c_dt_bias, c_norm_g, c_w_out):
    for i in range(DEPTH):
        j = i // 2
        x = layer_norm(DN_ALPHA * x + 0.5 * swiglu(x, ffn1_wg[i], ffn1_wu[i], ffn1_wd[i]), ln_g[i, 0], ln_b[i, 0])
        if i % 2 == 0:
            y = mixer_ab(x, ab_w_in[j], a_sinks[j], b_conv_w[j], b_conv_b[j],
                         b_wa[j], b_ba[j], b_wx[j], b_bx[j], b_lam[j], ab_w_out[j])
        else:
            y = mixer_c(x, c_w_in[j], c_conv_w[j], c_a_log[j], c_dt_bias[j], c_norm_g[j], c_w_out[j])
        x = layer_norm(DN_ALPHA * x + y, ln_g[i, 1], ln_b[i, 1])
        x = layer_norm(DN_ALPHA * x + 0.5 * swiglu(x, ffn2_wg[i], ffn2_wu[i], ffn2_wd[i]), ln_g[i, 2], ln_b[i, 2])
        x = x + jax.nn.sigmoid(x @ ple_wg[i] + ple_bg[i]) * (p[i] @ ple_wp[i])
    return x


def setup_inputs(seed=0):
    out = dict(first_inputs(seed))
    for name, value in second_inputs(seed + 1).items():
        if name != "x":
            out[name + "_2"] = value
    return out


def reference(
    x, c, norm1_g, norm2_g, w_ada, b_ada, w_in, w_gla_a2, b_gla_a, b_fox_f, ret_norm_g,
    gla_norm_g, q_norm_g, k_norm_g, w_br, w_mg, b_mg, w_o, w_up, w_conv, b_conv, w_down, p_2,
    ffn1_wg_2, ffn1_wu_2, ffn1_wd_2, ffn2_wg_2, ffn2_wu_2, ffn2_wd_2, ln_g_2, ln_b_2, ple_wg_2,
    ple_bg_2, ple_wp_2, ab_w_in_2, a_sinks_2, b_conv_w_2, b_conv_b_2, b_wa_2, b_ba_2, b_wx_2,
    b_bx_2, b_lam_2, ab_w_out_2, c_w_in_2, c_conv_w_2, c_a_log_2, c_dt_bias_2, c_norm_g_2,
    c_w_out_2,
):
    x = first_block(
        x, c, norm1_g, norm2_g, w_ada, b_ada, w_in, w_gla_a2, b_gla_a, b_fox_f, ret_norm_g,
        gla_norm_g, q_norm_g, k_norm_g, w_br, w_mg, b_mg, w_o, w_up, w_conv, b_conv, w_down,
    )
    return second_block(
        x, p_2, ffn1_wg_2, ffn1_wu_2, ffn1_wd_2, ffn2_wg_2, ffn2_wu_2, ffn2_wd_2, ln_g_2,
        ln_b_2, ple_wg_2, ple_bg_2, ple_wp_2, ab_w_in_2, a_sinks_2, b_conv_w_2, b_conv_b_2,
        b_wa_2, b_ba_2, b_wx_2, b_bx_2, b_lam_2, ab_w_out_2, c_w_in_2, c_conv_w_2, c_a_log_2,
        c_dt_bias_2, c_norm_g_2, c_w_out_2,
    )


_drawn_inputs = setup_inputs


def setup_inputs(seed=0):
    import zlib

    import numpy as np

    out = dict(_drawn_inputs(seed))
    spreads = {}
    factors = {'norm1_g': 6.695,
     'norm2_g': 7.818,
     'b_gla_a': 8.0,
     'b_fox_f': 8.0,
     'ret_norm_g': 8.0,
     'gla_norm_g': 8.0,
     'q_norm_g': 8.0,
     'k_norm_g': 8.0,
     'b_mg': 8.0,
     'b_conv': 8.0,
     'ple_bg_2': 8.0,
     'a_sinks_2': 8.0,
     'b_conv_b_2': 4.963,
     'b_ba_2': 64.0,
     'b_bx_2': 49.691,
     'c_norm_g_2': 25.766}
    for name, (base, spread) in spreads.items():
        noise = np.random.default_rng([zlib.crc32(name.encode()), seed]).standard_normal(out[name].shape)
        drawn = base * np.exp(spread * noise) if base else spread * noise
        out[name] = jnp.asarray(drawn.astype(out[name].dtype))
    for name, factor in factors.items():
        out[name] = (out[name] * factor).astype(out[name].dtype)
    return out
```

```python
import math
from contextlib import ExitStack

import numpy as np
import concourse.bass as bass
from concourse import mybir

P = 128
T = 256
D = 1024
KD = D // P
DEPTH = 2
FF = 2816
KF = FF // P
HEADS = 4
CH = 64
TT = T // P
EPS = 1e-6
LN_EPS = 1e-5
ALPHA = (2.0 * DEPTH) ** 0.25
NEG = -1e30
A_HEADS = 8
C_HEADS = 8
LEVELS = 7

TILE = P * P
DMA_TILES = 16
CUT_TILES = 8
RAW_SLOTS = 3
CUT_SLOTS = 4
AHEAD = CUT_SLOTS - 2

F32 = mybir.dt.float32
F32R = mybir.dt.float32r
ACT = mybir.ActivationFunctionType
ALU = mybir.AluOpType
AX = mybir.AxisListType


def sections():
    out = []
    for l in range(DEPTH):
        out.append((f"ada{l}", KD, range(0, 16), "raw"))
        out.append((f"small{l}", KD, range(1), "m"))
        for n in ("rq", "rk"):
            out.append((f"{n}{l}", KD, range(4), "m"))
        out.append((f"rv{l}", KD, range(4), "k"))
        out.append((f"rg{l}", KD, range(4), "m"))
        out.append((f"gq{l}", KD, range(2), "m"))
        out.append((f"gk{l}", KD, range(2), "m"))
        out.append((f"gv{l}", KD, range(4), "k"))
        out.append((f"gg{l}", KD, range(4), "m"))
        for n in ("fq", "fk"):
            out.append((f"{n}{l}", KD, range(4), "m"))
        out.append((f"fv{l}", KD, range(4), "k"))
        for m in range(0, 24, 2):
            out.append((f"mg{l}", KD, range(m, m + 2), "m"))
        out.append((f"ada{l}", KD, range(16, 48), "raw"))
        for m in range(0, KD, 2):
            for n in range(3):
                out.append((f"br{l}_{n}", 4, range(m, m + 2), "m"))
        out.append((f"wo{l}", KD, range(KD), "m"))
        for m in range(0, KF, 2):
            out.append((f"up{l}", KD, range(m, m + 2), "m"))
            out.append((f"up{l}", KD, range(KF + m, KF + m + 2), "m"))
        out.append((f"down{l}", KF, range(KD), "m"))
    for l in range(DEPTH):
        for f in (1, 2):
            for m in range(0, KF, 2):
                out.append((f"f{f}g{l}", KD, range(m, m + 2), "m"))
                out.append((f"f{f}u{l}", KD, range(m, m + 2), "m"))
            out.append((f"f{f}d{l}", KF, range(KD), "m"))
            if f == 1 and l == 0:
                out.append(("aq", KD, range(4), "m"))
                out.append(("ak", KD, range(1), "m"))
                out.append(("av", KD, range(1), "k"))
                out.append(("abx", KD, range(4), "m"))
                out.append(("abg", KD, range(4), "m"))
                out.append(("abo", KD, range(KD), "m"))
            if f == 1 and l == 1:
                out.append(("cab", KD, range(1), "m"))
                for n in ("cq", "ck", "cv"):
                    out.append((n, KD, range(KD), "m"))
                out.append(("cz", KD, range(KD), "m"))
                out.append(("cwo", KD, range(KD), "m"))
        out.append((f"pp{l}", 2, range(KD), "m"))
        out.append((f"pg{l}", KD, range(KD), "m"))
    return out


def weight_order():
    order, raw = [], None
    for name, nk, ms, how in sections():
        if raw is not None and raw != (how == "raw"):
            order += [None] * (-len(order) % DMA_TILES)
        raw = how == "raw"
        if how == "k":
            order += [(name, k, m, True) for k in range(nk) for m in ms]
        else:
            order += [(name, k, m, not raw) for m in ms for k in range(nk)]
    return order + [None] * (-len(order) % DMA_TILES)


def vector_columns():
    sizes = [("c", KD)]
    for l in range(DEPTH):
        sizes += [(f"b_ada{l}", 48), (f"norm1_g{l}", KD), (f"norm2_g{l}", KD), (f"b_gla{l}", 2),
                  (f"b_fox{l}", 1), (f"ret_g{l}", 4), (f"gla_g{l}", 1), (f"q_g{l}", 1),
                  (f"k_g{l}", 1), (f"b_mg{l}", 24), (f"w_conv{l}", 3 * KF), (f"b_conv{l}", KF),
                  (f"ple_b{l}", KD)]
        for i in range(3):
            sizes += [(f"ln_g{l}{i}", KD), (f"ln_b{l}{i}", KD)]
    sizes += [("sinks", A_HEADS), ("b_conv_w", 16), ("b_conv_b", 4), ("b_ba", 4), ("b_bx", 4),
              ("b_lam", 4), ("c_conv_w", 4 * 24), ("c_a_log", 1), ("c_dt", 1), ("c_g", 1)]
    out, at = {}, 0
    for n, s in sizes:
        out[n] = (at, s)
        at += s
    return out, at


BASE = [("ident", P), ("mean_d", P), ("mean_h", P), ("center", P), ("resets", T)]
TAB1 = [("swap", P), ("cos", T), ("sin", T), ("decay", HEADS * 384), ("gla", 384), ("causal", T),
        ("sel", HEADS * P)]
TABA = [("bias", A_HEADS * T)]
TABC = [("causal_t", P), ("strict", P), ("level", LEVELS * P), ("sel_c", C_HEADS * P)]


def widths(table):
    return sum(w for _, w in table)


def columns(table):
    out, at = {}, 0
    for n, w in table:
        out[n] = (at, w)
        at += w
    return out


class Engine:

    def __init__(self, sem):
        self.sem, self.count, self.steps, self.passed = sem, 0, [], {}

    def wait(self, *marks):
        for mark in marks:
            if mark is None:
                continue
            if isinstance(mark, list):
                self.wait(*mark)
            elif self.passed.get(id(mark[0]), 0) < mark[1]:
                self.passed[id(mark[0])] = mark[1]
                self.steps.append(("wait", mark[0], mark[1]))

    def do(self, what, *after, mark=True):
        self.wait(*after)
        self.steps.append(("do", what, self.sem if mark else None))
        if mark:
            self.count += 1
            return (self.sem, self.count)
        return None

    def last(self):
        return (self.sem, self.count) if self.count else None

    def emit(self, eng):
        for kind, a, b in self.steps:
            if kind == "wait":
                eng.wait_ge(a, b)
            elif kind == "dma":
                a(eng).then_inc(b, 16)
            elif b is None:
                a(eng)
            else:
                a(eng).then_inc(b, 1)


def build(nc, ins, out_ap, stages):
    order = weight_order()
    vec_at, n_vec = vector_columns()
    ctx = ExitStack()
    with ctx:
        def sb(name, shape, dt=F32):
            return ctx.enter_context(nc.sbuf_tensor(name, shape, dt))

        def semaphore(name):
            return ctx.enter_context(nc.semaphore(name))

        pe, act, dve, pool, sp = (Engine(semaphore(f"{n}_done")) for n in ("pe", "act", "dve", "pool", "sp"))

        x_t = sb("x_t", [P, KD, T])
        h_hi = sb("h_hi", [P, KD, T], F32R)
        h_lo = sb("h_lo", [P, KD, T], F32R)
        g_hi = sb("g_hi", [P, KF, T], F32R)
        g_lo = sb("g_lo", [P, KF, T], F32R)
        raw = [sb(f"raw{i}", [P, DMA_TILES, P]) for i in range(RAW_SLOTS)]
        cut_hi = [sb(f"cut_hi{i}", [P, CUT_TILES, P], F32R) for i in range(CUT_SLOTS)]
        cut_lo = [sb(f"cut_lo{i}", [P, CUT_TILES, P], F32R) for i in range(CUT_SLOTS)]
        vec = sb("vec", [P, n_vec])
        base = sb("base", [P, widths(BASE)])
        mod = sb("mod", [P, 48])
        col = sb("col", [P, 64])
        WORK = 19900
        work = sb("work", [P, WORK])
        psum = [ctx.enter_context(nc.psum_tensor(f"psum{i}", [P, 512], F32)) for i in range(8)]

        base_at = columns(BASE)

        def B(name):
            a, w = base_at[name]
            return base[:, a:a + w]

        def V(name, i=0, n=1, rows=P):
            a, _ = vec_at[name]
            return vec[0:rows, a + i:a + i + n]

        class Bank:
            def __init__(self, t):
                self.t, self.free = t, []

            def halves(self):
                return self.t[:, :].rearrange("p (a t) -> p a t", a=2)

        banks = [Bank(t) for t in psum]
        turn = [0]

        def take():
            b = banks[turn[0] % len(banks)]
            turn[0] += 1
            marks, b.free = b.free, []
            pe.wait(marks)
            return b

        raw_ready = [semaphore(f"raw_ready{i}") for i in range(RAW_SLOTS)]
        n_loads = len(order) // DMA_TILES
        load_free = [None] * n_loads
        cut_mark = {}
        cut_free = {}
        state = {"loads": 0, "cuts": 0, "pos": 0}
        cuts_per_load = DMA_TILES // CUT_TILES
        stream = ins["stream"]

        def start_loads(upto):
            while state["loads"] <= min(upto, n_loads - 1):
                s = state["loads"]
                if s >= RAW_SLOTS:
                    sp.wait(load_free[s - RAW_SLOTS])
                sp.steps.append(("dma", lambda e, s=s: e.dma_start(
                    raw[s % RAW_SLOTS][:, :, :], stream[s]), raw_ready[s % RAW_SLOTS]))
                state["loads"] += 1

        def load_mark(s):
            return (raw_ready[s % RAW_SLOTS], 16 * (s // RAW_SLOTS + 1))

        def is_split(s):
            first = order[s * DMA_TILES]
            return first[3]

        def cut(g):
            s, half = divmod(g, cuts_per_load)
            if is_split(s):
                src = raw[s % RAW_SLOTS][:, half * CUT_TILES:(half + 1) * CUT_TILES, :]
                hi, lo = cut_hi[g % CUT_SLOTS], cut_lo[g % CUT_SLOTS]
                m = act.do(lambda e: e.activation(hi[:, :, :], src, ACT.Copy),
                           load_mark(s), cut_free.get(g - CUT_SLOTS))
                cut_mark[g] = dve.do(lambda e: e.tensor_tensor(
                    lo[:, :, :], src, hi[:, :, :].bitcast(F32), ALU.subtract), m)
                if half == cuts_per_load - 1:
                    load_free[s] = cut_mark[g]
                    start_loads(s + RAW_SLOTS)

        def cut_upto(g):
            while state["cuts"] <= min(g, n_loads * cuts_per_load - 1):
                cut(state["cuts"])
                state["cuts"] += 1

        start_loads(RAW_SLOTS - 1)

        class Weight:
            pass

        def weight(name, k, m, n=1):
            p = state["pos"]
            while order[p] is None:
                p += 1
            assert order[p][:3] == (name, k, m), (order[p], name, k, m)
            w = Weight()
            g = p // CUT_TILES
            s = p // DMA_TILES
            w.split = order[p][3]
            i = p % CUT_TILES
            w.group, w.load = g, s
            if w.split:
                cut_upto(g + AHEAD)
                w.hi = cut_hi[g % CUT_SLOTS][:, i:i + n, :].rearrange("p a b -> p (a b)")
                w.lo = cut_lo[g % CUT_SLOTS][:, i:i + n, :].rearrange("p a b -> p (a b)")
                w.ready = cut_mark[g]
            else:
                i = p % DMA_TILES
                cut_upto((s + 1) * cuts_per_load - 1)
                w.f32 = raw[s % RAW_SLOTS][:, i:i + n, :].rearrange("p a b -> p (a b)")
                w.ready = load_mark(s)
            nxt = p + n
            while nxt < len(order) and order[nxt] is None:
                nxt += 1
            w.ends_group = nxt // CUT_TILES != g
            w.ends_load = nxt // DMA_TILES != s
            state["pos"] = p + n
            return w

        def used(w, mark):
            if w.split and w.ends_group:
                cut_free[w.group] = mark
            if not w.split and w.ends_load:
                load_free[w.load] = mark
                start_loads(w.load + RAW_SLOTS)

        def matmul(out, lhsT, rhs, start, stop, *after, mark=False):
            return pe.do(lambda e: e.matmul(out, lhsT, rhs, start=start, stop=stop), *after, mark=mark)

        class Pair:

            def __init__(self, hi, lo, first=0):
                self.hi, self.lo, self.first, self.ready = hi, lo, first, {}

            def part(self, lo, k, a=0, b=T):
                t = self.lo if lo else self.hi
                return t[:, self.first + k, a:b]

            def split(self, value, k, n, *after):
                f = self.first + k
                hi, lo = self.hi[:, f:f + n, :], self.lo[:, f:f + n, :]
                m = A(hi, value, ACT.Copy, *after)
                m = TTn(lo, value, hi.bitcast(F32), ALU.subtract, m)
                for i in range(k, k + n):
                    self.ready[i] = m
                return m

        h_pair = Pair(h_hi, h_lo)

        def three(out, w, pair, k, start, stop, swap, n_cols=None):
            parts = [(w.hi, 0), (w.hi, 1), (w.lo, 0)]
            for i, (wt, lo) in enumerate(parts):
                s, e_ = start and i == 0, stop and i == 2
                if swap is None:
                    yield wt, pair.part(lo, k), out, s, e_
                else:
                    yield pair.part(lo, k, swap * P, (swap + 1) * P), wt, out, s, e_

        def project(sec, pair, nk, ms, evacuate):
            ms = list(ms)
            for i in range(0, len(ms), 2):
                two = ms[i:i + 2]
                b = take()
                for j, m in enumerate(two):
                    out = b.halves()[:, j, :]
                    for k in range(nk):
                        w = weight(sec, k, m)
                        steps = list(three(out, w, pair, k, k == 0, k == nk - 1, None))
                        for n, (l, r, o, s, e_) in enumerate(steps):
                            end = n == 2 and (k == nk - 1 or w.ends_group)
                            mk = matmul(o, l, r, s, e_, w.ready, pair.ready[k], mark=end)
                        if mk is not None:
                            used(w, mk)
                evacuate(two, b, mk)

        def project_tokens(sec, pair, n_cols, evacuate):
            bs = [take() for _ in range(TT)]
            for k in range(KD):
                w = weight(sec, k, 0, n_cols // P)
                for t in range(TT):
                    steps = list(three(bs[t].t[:, 0:n_cols], w, pair, k, k == 0, k == KD - 1, t))
                    for n, (l, r, o, s, e_) in enumerate(steps):
                        mk = matmul(o, l, r, s, e_, w.ready, pair.ready[k],
                                    mark=n == 2 and (k == KD - 1 or t == TT - 1))
                    if k == KD - 1:
                        bs[t].done = mk
                w_pos = state["pos"]
                if n_cols // P > 1:
                    state["pos"] = w_pos
                used(w, mk)
            for t in range(TT):
                evacuate(t, bs[t], bs[t].done)

        def fence():
            marks = [e.last() for e in (pe, act, dve, pool)]
            for e in (act, dve, pool):
                e.wait(*marks)

        class Area:
            def __init__(self, at=0):
                self.at = at

            def get(self, *shape):
                n = math.prod(shape)
                assert self.at + n <= WORK, (self.at, n)
                a = work[:, self.at:self.at + n]
                self.at += n
                if len(shape) == 2:
                    a = a.rearrange("p (a b) -> p a b", a=shape[0])
                if len(shape) == 3:
                    a = a.rearrange("p (a b c) -> p a b c", a=shape[0], b=shape[1])
                return a

        s_in = semaphore("inputs_ready")
        s_tab = semaphore("tables_ready")
        n_tab = [0]

        def load_in(dst, src):
            pool.steps.append(("dma", lambda e: e.dma_start(dst, src), s_in))

        load_in(vec[:, :], ins["vec"])
        load_in(base[:, :], ins["base"])
        load_in(x_t[:, :, :], ins["xT"])
        inputs = (s_in, 48)
        for e in (pe, act, dve, pool):
            e.wait(inputs)

        def load_table(dst, src):
            n_tab[0] += 16
            pool.steps.append(("dma", lambda e: e.dma_start(dst, src), s_tab))
            return (s_tab, n_tab[0])

        before = {}

        def behind(engine, what, *after):
            before[engine.sem.name] = m = engine.do(what, before.get(engine.sem.name), *after)
            return m

        def A(out, in_, f, *after, bias=0.0, scale=1.0):
            return behind(act, lambda e: e.activation(out, in_, f, bias=bias, scale=scale), *after)

        def TTn(out, a, b, op, *after):
            return behind(dve, lambda e: e.tensor_tensor(out, a, b, op), *after)

        def TS(out, a, s1, op0, *after, s2=None, op1=None):
            if op1 is None:
                return behind(dve, lambda e: e.tensor_scalar(out, a, s1, None, op0), *after)
            return behind(dve, lambda e: e.tensor_scalar(out, a, s1, s2, op0, op1), *after)

        def STT(out, a, s, b, op0, op1, *after):
            return behind(dve, lambda e: e.scalar_tensor_tensor(out, a, s, b, op0, op1), *after)

        def RED(out, in_, op, *after):
            return behind(dve, lambda e: e.tensor_reduce(out, in_, AX.X, op), *after)

        def RCP(out, in_, *after):
            return behind(dve, lambda e: e.reciprocal(out, in_), *after)

        def SCAN(out, a, b, *after):
            return behind(dve, lambda e: e.tensor_tensor_scan(out, a, b, 0.0, ALU.mult, ALU.add), *after)

        def SET(out, value, *after):
            return behind(dve, lambda e: e.memset(out, value), *after)

        eps_col = {}

        def const_col(value):
            if value not in eps_col:
                i = 60 + len(eps_col)
                eps_col[value] = (col[:, i:i + 1], SET(col[:, i:i + 1], value))
            return eps_col[value]

        for v in (EPS, LN_EPS, 1.0):
            const_col(v)
        act.wait(dve.last())

        def bc(ap, n):
            p, w = ap.shape
            return ap.unsqueeze(1).to_broadcast([p, n, w])

        def bl(ap, n):
            p, w = ap.shape
            return ap.unsqueeze(2).to_broadcast([p, w, n])

        def feature_mean(src, tmp, *after):
            r = RED(tmp, src.rearrange("p k t -> p t k"), ALU.add, *after)
            b = take()
            mk = matmul(b.t[:, 0:T], B("mean_d"), tmp, True, True, r, mark=True)
            return b, mk

        def inverse_root(b, out, mk, eps, n=T, scale=1.0):
            e_col, e_mk = const_col(eps)
            m = A(out, b.t[:, 0:n], ACT.Sqrt, mk, bias=e_col, scale=scale)
            b.free = [m]
            return RCP(out, out, m)

        def modulated_norm(gain, shift):
            fence()
            ar = Area()
            sq, tmp, rs, t1 = ar.get(KD, T), ar.get(T), ar.get(T), ar.get(KD, T)
            m = A(sq, x_t[:, :, :], ACT.Square)
            b, mk = feature_mean(sq, tmp, m)
            r = inverse_root(b, rs, mk, EPS)
            for k in range(KD):
                m = STT(t1[:, k, :], x_t[:, k, :], gain[:, k:k + 1], rs, ALU.mult, ALU.mult, r)
                m = A(h_hi[:, k, :], t1[:, k, :], ACT.Identity, m, bias=shift[:, k:k + 1])
                h_pair.ready[k] = STT(h_lo[:, k, :], t1[:, k, :], shift[:, k:k + 1],
                                      h_hi[:, k, :].bitcast(F32), ALU.add, ALU.subtract, m)

        def make_pair_of_x(scaled=True):
            for k in range(KD):
                h_pair.split(x_t[:, k:k + 1, :], k, 1)
                if scaled:
                    A(x_t[:, k:k + 1, :], x_t[:, k:k + 1, :], ACT.Copy, dve.last(), scale=ALPHA)

        def layer_norm(l, i, scaled=True):
            fence()
            ar = Area()
            xc, sq, tmp, rs = ar.get(KD, T), ar.get(KD, T), ar.get(T), ar.get(T)
            b, mk = feature_mean(x_t[:, :, :], tmp)
            m = TTn(xc, x_t[:, :, :], bc(b.t[:, 0:T], KD), ALU.subtract, mk)
            b.free = [m]
            m = A(sq, xc, ACT.Square, m)
            b, mk = feature_mean(sq, tmp, m)
            r = inverse_root(b, rs, mk, LN_EPS)
            for k in range(KD):
                m = STT(xc[:, k, :], xc[:, k, :], V(f"ln_g{l}{i}", k), rs, ALU.mult, ALU.mult, r)
                m = A(x_t[:, k, :], xc[:, k, :], ACT.Identity, m, bias=V(f"ln_b{l}{i}", k))
                m = A(h_hi[:, k, :], x_t[:, k, :], ACT.Copy, m)
                h_pair.ready[k] = m = TTn(h_lo[:, k, :], x_t[:, k, :], h_hi[:, k, :].bitcast(F32),
                                          ALU.subtract, m)
                if scaled:
                    A(x_t[:, k, :], x_t[:, k, :], ACT.Copy, m, scale=ALPHA)

        def down(sec, pair, nk, residual):
            def evacuate(two, b, mk):
                b.free = [residual(two, b, mk)]
            project(sec, pair, nk, range(KD), evacuate)

        def add_gated(gate):
            def residual(two, b, mk):
                for j, m in enumerate(two):
                    r = STT(x_t[:, m, :], b.halves()[:, j, :], gate[:, m:m + 1], x_t[:, m, :],
                            ALU.mult, ALU.add, mk)
                return r
            return residual

        def add_scaled(scale):
            def residual(two, b, mk):
                return STT(x_t[:, two[0]:two[0] + 2, :], b.halves(), scale,
                           x_t[:, two[0]:two[0] + 2, :], ALU.mult, ALU.add, mk, act.last())
            return residual

        def swiglu(secg, secu, secd, residual):
            pair = Pair(g_hi, g_lo)
            ar = Area()
            silu = [ar.get(2, T) for _ in range(2)]
            val = [ar.get(2, T) for _ in range(2)]
            done = [None, None]
            for n, m in enumerate(range(0, KF, 2)):
                hold = {}

                def gate_out(two, b, mk, n=n, hold=hold):
                    hold["m"] = A(silu[n % 2], b.halves(), ACT.Silu, mk, done[n % 2])
                    b.free = [hold["m"]]

                def up_out(two, b, mk, n=n, m=m, hold=hold):
                    v = TTn(val[n % 2], silu[n % 2], b.halves(), ALU.mult, mk, hold["m"])
                    b.free = [v]
                    done[n % 2] = pair.split(val[n % 2], m, 2, v)

                project(secg, h_pair, KD, range(m, m + 2), gate_out)
                project(secu, h_pair, KD, range(m, m + 2), up_out)
            down(secd, pair, KF, residual)

        def conv_ffn(l, gate):
            fence()
            pair = Pair(g_hi, g_lo)
            ar = Area()
            pad = [ar.get(2, T + 2) for _ in range(2)]
            con = [ar.get(2, T) for _ in range(2)]
            val = [ar.get(2, T) for _ in range(2)]
            zeroed = [SET(p[:, :, 0:2], 0.0) for p in pad]
            done = [zeroed[1], zeroed[1]]
            for n, m in enumerate(range(0, KF, 2)):
                hold = {}
                pd, cv, vl = pad[n % 2], con[n % 2], val[n % 2]

                def u_out(two, b, mk, n=n, pd=pd, cv=cv, hold=hold):
                    a = A(pd[:, :, 2:T + 2], b.halves(), ACT.Copy, mk, done[n % 2])
                    for j, f in enumerate(two):
                        b.free = [A(cv[:, j, :], b.halves()[:, j, :], ACT.Identity,
                                    bias=V(f"b_conv{l}", f), scale=V(f"w_conv{l}", 2 * KF + f))]
                    c = b.free[0]
                    for j, f in enumerate(two):
                        c1 = STT(cv[:, j, :], pd[:, j, 1:T + 1], V(f"w_conv{l}", KF + f), cv[:, j, :],
                                 ALU.mult, ALU.add, c)
                        c2 = STT(cv[:, j, :], pd[:, j, 0:T], V(f"w_conv{l}", f), cv[:, j, :],
                                 ALU.mult, ALU.add, c1)
                    hold["m"] = A(cv, cv, ACT.Silu, c2)

                def g_out(two, b, mk, n=n, m=m, cv=cv, vl=vl, hold=hold):
                    v = TTn(vl, cv, b.halves(), ALU.mult, mk, hold["m"])
                    b.free = [v]
                    done[n % 2] = pair.split(vl, m, 2, v)

                project(f"up{l}", h_pair, KD, range(m, m + 2), u_out)
                project(f"up{l}", h_pair, KD, range(KF + m, KF + m + 2), g_out)
            down(f"down{l}", pair, KF, add_gated(gate))

        def to(out, f=ACT.Copy, bias=0.0, scale=1.0):
            def evacuate(two, b, mk):
                b.free = [A(out[:, two[0]:two[0] + len(two), :], b.halves()[:, 0:len(two), :], f, mk,
                            bias=bias, scale=scale)]
            return evacuate

        def to_tokens(out, n_cols):
            def evacuate(t, b, mk):
                b.free = [A(out[:, t, 0:n_cols], b.t[:, 0:n_cols], ACT.Copy, mk)]
            return evacuate

        def weave(main, filler):
            for _ in main:
                next(filler, None)
            for _ in filler:
                pass

        def log_sigmoid(out, z, t1, t2, *after):
            m = A(t1, z, ACT.Abs, *after)
            m = A(t1, t1, ACT.Exp, m, scale=-1.0)
            m = A(t1, t1, ACT.Ln, m, bias=const_col(1.0)[0][0:t1.shape[0], :])
            m2 = TS(t2, z, 0.0, ALU.min)
            return TTn(out, t2, t1, ALU.subtract, m, m2)

        def head_norm(src, tmp, rs, heads, eps, *after, scale=1.0):
            m = A(tmp, src, ACT.Square, *after)
            last = []
            for h in range(0, heads, 2):
                b = take()
                mk = matmul(b.t[:, :], B("mean_h"), tmp[:, h:h + 2, :].rearrange("p a t -> p (a t)"),
                            True, True, m, mark=True)
                s = A(rs[:, h:h + 2, :], b.halves(), ACT.Sqrt, mk, bias=const_col(eps)[0], scale=scale)
                b.free = [s]
                last.append(RCP(rs[:, h:h + 2, :], rs[:, h:h + 2, :], s))
            return last[-1]

        def values_times_scores(vals, sc, out, heads, *after):
            for h in range(heads):
                if h % 2 == 0:
                    b = take()
                o = b.halves()[:, h % 2, :]
                matmul(o, vals(h, 0), sc[:, h, 0:T], True, False, *after)
                mk = matmul(o[:, P:T], vals(h, 1), sc[:, h, T:T + P], False, True, mark=True)
                if h % 2 == 1:
                    out(h - 1, b, mk)

        def softmax_attention(heads, it, scores, bias, scale, S, E, small, sc, sink=None):
            W = P * (it + 1)
            per = 4 if it == 0 else 2
            Sv = S[:, 0:heads * W].rearrange("p (h w) -> p h w", h=heads)
            Ev = E[:, 0:heads * W].rearrange("p (h w) -> p h w", h=heads)
            for h0 in range(0, heads, per):
                b = take()
                v = b.t[:, :].rearrange("p (h w) -> p h w", h=per)
                for h in range(h0, h0 + per):
                    mk = scores(h, v[:, h - h0, :], W)
                m = STT(Sv[:, h0:h0 + per, :], v, scale, bias(h0, per, W), ALU.mult, ALU.add, mk,
                        act.last())
                b.free = [m]
                yield
            mx, sm, ex = (small[:, i * heads:(i + 1) * heads] for i in range(3))
            m = RED(mx, Sv, ALU.max, m)
            if sink is not None:
                m = TTn(mx, mx, sink, ALU.max, m)
                m1 = TTn(ex, sink, mx, ALU.subtract, m)
                mex = A(ex, ex, ACT.Exp, m1)
            m = TTn(Sv, Sv, bl(mx, W), ALU.subtract, m)
            m = A(Ev, Sv, ACT.Exp, m)
            yield
            m = RED(sm, Ev, ALU.add, m)
            if sink is not None:
                m = TTn(sm, sm, ex, ALU.add, m, mex)
            m = RCP(sm, sm, m)
            m = TTn(Ev, Ev, bl(sm, W), ALU.mult, m)
            yield
            pieces = [(h, jt) for jt in range(it + 1) for h in range(heads)]
            for i in range(0, len(pieces), 4):
                b = take()
                for n, (h, jt) in enumerate(pieces[i:i + 4]):
                    o, s_ = b.t[:, n * P:(n + 1) * P], Ev[:, h, jt * P:(jt + 1) * P]
                    mk = pe.do(lambda e, o=o, s_=s_: e.transpose(o, s_, B("ident")), m)
                h, jt = pieces[i]
                c0 = T if jt == 1 else it * P
                b.free = [A(sc[:, h:h + 4, c0:c0 + P], b.t[:, :].rearrange("p (h w) -> p h w", h=4),
                            ACT.Copy, mk)]
                yield

        def modulation(l, first, n):
            b = take()
            for i in range(n):
                for k in range(KD):
                    w = weight(f"ada{l}", k, first + i)
                    end = w.ends_load or (k == KD - 1 and i == n - 1)
                    mk = matmul(b.t[:, i:i + 1], w.f32, c_act[:, k:k + 1], k == 0, k == KD - 1,
                                w.ready, c_ready, mark=end)
                    if mk is not None:
                        used(w, mk)
                yield
            m = TTn(mod[:, first:first + n], b.t[:, 0:n], V(f"b_ada{l}", first, n), ALU.add, mk)
            b.free = [m]
            if first == 0:
                g = STT(col[:, 8:16], mod[:, 8:16], 1.0, V(f"norm1_g{l}", 0, KD), ALU.add, ALU.mult, m)
            else:
                g = STT(col[:, 16:24], mod[:, 32:40], 1.0, V(f"norm2_g{l}", 0, KD), ALU.add, ALU.mult, m)

        c_act = col[:, 0:KD]
        c_ready = A(c_act, V("c", 0, KD), ACT.Silu)

        def mixer_one(l):
            fence()
            ar = Area()
            tab = ar.get(widths(TAB1))
            ready = load_table(tab, ins["tab1"])
            at = columns(TAB1)

            def C(name):
                a, w = at[name]
                return tab[:, a:a + w]

            wa2 = ar.get(256)
            ready = load_table(wa2[0:48, :], ins[f"wa2_{l}"])
            r_at = ar.at
            rq, rk, rv, rg = ar.get(4, T), ar.get(4, T), ar.get(2, 512), ar.get(4, T)
            gq, gk, gv, gg = ar.get(2, T), ar.get(2, T), ar.get(2, 512), ar.get(4, T)
            kw_next = ar.get(3, 2, T)
            kw = [gk] + [kw_next[:, n, :, :] for n in range(3)]
            r_end = ar.at
            fq, fk, fv = ar.get(4, T), ar.get(4, T), ar.get(2, 512)
            t_a, t_b, t_c = ar.get(1024), ar.get(1024), ar.get(1536)
            rows = ar.get(T)
            rows2 = ar.get(T)
            small = ar.get(64)
            ar2 = Area(r_at)
            gates = ar2.get(24, T)
            assert ar2.at <= r_end

            def four(x):
                return x[:, 0:1024].rearrange("p (h t) -> p h t", h=4)

            branch = [Pair(g_hi, g_lo, 4 * n) for n in range(3)]
            sc = t_c.rearrange("p (h w) -> p h w", h=4)
            proj = lambda n, ms, ev: project(f"{n}{l}", h_pair, KD, ms, ev)

            def small_out(two, b, mk):
                b.free = [A(rows[0:48, :], b.t[0:48, 0:T], ACT.Copy, mk)]
            proj("small", range(1), small_out)
            proj("rq", range(4), to(rq))
            proj("rk", range(4), to(rk))
            project_tokens(f"rv{l}", h_pair, 512, to_tokens(rv, 512))
            proj("rg", range(4), to(rg, ACT.Silu))
            for e in (pe, act, dve):
                e.wait(ready)

            def finish(o, gate, gain, pair, src_mark, center, eps, bufs):
                tmp, rs = bufs
                r = head_norm(o, tmp, rs, 4, eps, src_mark)
                for h in range(4):
                    m = STT(o[:, h, :], o[:, h, :], gain(h), rs[:, h, :], ALU.mult, ALU.mult, r)
                m = TTn(o, o, gate, ALU.mult, m)
                for h in range(0, 4, 2):
                    pair.split(o[:, h:h + 2, :], h, 2, m)

            def retention():
                t1 = four(t_a)
                for x, s in ((rq, 1.0), (rk, P ** -0.5)):
                    last = None
                    for h in range(0, 4, 2):
                        b = take()
                        mk = matmul(b.t[:, :], C("swap"), x[:, h:h + 2, :].rearrange("p a t -> p (a t)"),
                                    True, True, act.last(), mark=True)
                        m = STT(t1[:, h:h + 2, :], b.halves(), s, bc(C("sin"), 2), ALU.mult, ALU.mult, mk)
                        b.free = [m]
                        m = STT(x[:, h:h + 2, :], x[:, h:h + 2, :], s, bc(C("cos"), 2), ALU.mult, ALU.mult, m)
                        last = TTn(x[:, h:h + 2, :], x[:, h:h + 2, :], t1[:, h:h + 2, :], ALU.add, m)
                    yield
                dec = C("decay").rearrange("p (h w) -> p h w", h=4)
                for h in range(4):
                    b = take()
                    matmul(b.t[:, 0:T], rk[:, h, 0:P], rq[:, h, :], True, True, last)
                    mk = matmul(b.t[:, T:T + P], rk[:, h, P:T], rq[:, h, P:T], True, True, mark=True)
                    m = TTn(sc[:, h, :], b.t[:, 0:T + P], dec[:, h, :], ALU.mult, mk)
                    b.free = [m]
                    if h % 2:
                        yield
                o = four(t_a)
                marks = []

                def out(h, b, mk):
                    a = A(o[:, h:h + 2, :], b.halves(), ACT.Copy, mk, dve.last())
                    b.free = [a]
                    marks.append(a)
                values_times_scores(lambda h, t: rv[:, t, h * P:(h + 1) * P], sc, out, 4, m)
                yield
                for h in range(0, 4, 2):
                    b = take()
                    mk = matmul(b.t[:, :], B("center"), o[:, h:h + 2, :].rearrange("p a t -> p (a t)"),
                                True, True, marks[-1], mark=True)
                    a = A(o[:, h:h + 2, :], b.halves(), ACT.Copy, mk)
                    b.free = [a]
                yield
                finish(o, rg, lambda h: V(f"ret_g{l}", h), branch[0], a, True, EPS,
                       (four(t_b), four(t_c)))
                yield

            def gla_proj():
                proj("gq", range(2), to(gq))
                yield
                proj("gk", range(2), to(gk))
                yield
                project_tokens(f"gv{l}", h_pair, 512, to_tokens(gv, 512))
                yield
                proj("gg", range(2), to(gg, ACT.Silu))
                yield
                proj("gg", range(2, 4), to(gg, ACT.Silu))
                yield

            def fox_proj():
                for n, x in (("fq", fq), ("fk", fk)):
                    proj(n, range(2), to(x))
                    yield
                    proj(n, range(2, 4), to(x))
                    yield
                project_tokens(f"fv{l}", h_pair, 512, to_tokens(fv, 512))
                yield

            def gla():
                la = t_a[:, 0:512].rearrange("p (a t) -> p a t", a=2)
                t2 = t_a[:, 512:1024].rearrange("p (a t) -> p a t", a=2)
                t3 = t_b[:, 0:512].rearrange("p (a t) -> p a t", a=2)
                b = take()
                for j in range(2):
                    mk = matmul(b.halves()[:, j, :], wa2[32:48, j * P:(j + 1) * P], rows[32:48, :],
                                True, True, act.last(), mark=True)
                for j in range(2):
                    m = TS(la[:, j, :], b.halves()[:, j, :], V(f"b_gla{l}", j), ALU.add, mk, act.last())
                b.free = [m]
                m = log_sigmoid(la, la, t3, t2, m)
                m = TS(la, la, 1.0 / 16.0, ALU.mult, m)
                cum = t2
                for j in range(2):
                    m2 = SCAN(cum[:, j, :], B("resets"), la[:, j, :], m)
                ends = small[:, 0:8].rearrange("p (a n) -> p a n", a=2)
                for j in range(2):
                    c4 = cum[:, j, :].rearrange("p (n i) -> p n i", n=4)
                    m = TTn(t3[:, j, :].rearrange("p (n i) -> p n i", n=4),
                            c4[:, :, CH - 1:CH].to_broadcast([P, 4, CH]), c4, ALU.subtract, m2)
                    m = A(ends[:, j, :].unsqueeze(2), c4[:, :, CH - 1:CH], ACT.Exp, m)
                m = A(t3, t3, ACT.Exp, m)
                yield
                m = TTn(kw[0], gk, t3, ALU.mult, m)
                for n in range(1, 4):
                    for j in range(2):
                        m2 = TS(kw[n][:, j, 0:n * CH], kw[n - 1][:, j, 0:n * CH], ends[:, j, n:n + 1],
                                ALU.mult, m)
                        m3 = TS(kw[n][:, j, n * CH:T], kw[0][:, j, n * CH:T], 1.0, ALU.mult, m)
                    m = m3
                yield
                mask = C("gla")
                for h in range(4):
                    j, lo = h // 2, (h % 2) * 64
                    b = take()
                    for n in range(4):
                        q_ = gq[lo:lo + 64, j, n * CH:(n + 1) * CH]
                        mk = matmul(b.t[:, n * CH:(n + 1) * CH], kw[n][lo:lo + 64, j, 0:P], q_,
                                    True, True, m, mark=n < 2)
                        if n >= 2:
                            c = T + (n - 2) * CH
                            mk = matmul(b.t[:, c:c + CH], kw[n][lo:lo + 64, j, P:T], q_, True, True,
                                        mark=True)
                    s = TTn(sc[:, h, :], b.t[:, 0:T + P], mask, ALU.mult, mk, act.last())
                    b.free = [s]
                    if h % 2:
                        yield
                o = four(t_a)
                marks = []

                def out(h, b, mk):
                    a = A(o[:, h:h + 2, :], b.halves(), ACT.Copy, mk, dve.last())
                    b.free = [a]
                    marks.append(a)
                values_times_scores(lambda h, t: gv[:, t, h * P:(h + 1) * P], sc, out, 4, s)
                yield
                finish(o, gg, lambda h: V(f"gla_g{l}", 0), branch[1], marks[-1], False, EPS,
                       (four(t_b), four(t_c)))
                yield

            def fox():
                lf, t1 = t_a[0:4, 0:T], t_a[0:4, T:2 * T]
                m = TS(lf, rows[0:4, :], V(f"b_fox{l}", rows=4), ALU.add, act.last(), pe.last())
                m = log_sigmoid(lf, lf, t1, rows2[0:4, :], m)
                ones = t_b[0:4, 0:T]
                m = SET(ones, 1.0, m)
                cum, ncum = rows[0:4, :], rows2[0:4, :]
                m = SCAN(cum, ones, lf, m)
                c_m = TS(ncum, cum, -1.0, ALU.mult, m)
                yield
                for x, g, s in ((fq, f"q_g{l}", P ** -0.5), (fk, f"k_g{l}", 1.0)):
                    tmp, rs = four(t_b), four(t_c)
                    r = head_norm(x, tmp, rs, 4, EPS, dve.last())
                    m = STT(x, x, V(g), rs, ALU.mult, ALU.mult, r)
                    if s != 1.0:
                        m = TS(x, x, s, ALU.mult, m)
                    yield
                sel = C("sel").rearrange("p (h w) -> p h w", h=HEADS)
                fence()
                for it in range(TT):
                    def scores(h, o, W, it=it):
                        for c in range(0, W, P):
                            w_ = slice(c, c + P)
                            matmul(o[:, w_], fq[:, h, it * P:(it + 1) * P], fk[:, h, w_], True, False, m, c_m)
                            matmul(o[:, w_], sel[0:4, h, :], ncum[:, w_], False, False)
                            mk = matmul(o[:, w_], cum[:, it * P:(it + 1) * P], sel[0:4, h, :],
                                        False, True, mark=True)
                        return mk

                    def bias(h0, per, W):
                        return bc(C("causal")[:, T - W:T], per)
                    yield from softmax_attention(4, it, scores, bias, 1.0, t_a, t_b, small, sc)
                o = four(t_a)

                def out(h, b, mk):
                    a = A(o[:, h:h + 2, :], b.halves(), ACT.Copy, mk, dve.last())
                    b.free = [a]
                    branch[2].split(o[:, h:h + 2, :], h, 2, a)
                values_times_scores(lambda h, t: fv[:, t, h * P:(h + 1) * P], sc, out, 4, act.last())
                yield

            def gate_proj(free):
                def out(two, b, mk):
                    for j, m in enumerate(two):
                        a = A(gates[:, m, :], b.halves()[:, j, :], ACT.Sigmoid, mk, free,
                              bias=V(f"b_mg{l}", m))
                    b.free = [a]
                for m in range(0, 24, 2):
                    proj("mg", range(m, m + 2), out)
                    yield
                yield from modulation(l, 16, 32)

            weave(retention(), gla_proj())
            weave(gla(), fox_proj())
            weave(fox(), gate_proj([pe.last(), dve.last(), act.last()]))

            mixed = Pair(g_hi, g_lo, 12)
            for m in range(0, KD, 2):
                acc, t1 = four(t_a)[:, 0:2, :], four(t_a)[:, 2:4, :]
                for n in range(3):
                    def out(two, b, mk, n=n, m=m):
                        g = gates[:, n * KD + m:n * KD + m + 2, :]
                        dst = acc if n == 0 else t1
                        r = TTn(dst, b.halves(), g, ALU.mult, mk, dve.last(), act.last())
                        b.free = [r]
                        if n:
                            TTn(acc, acc, t1, ALU.add, r)
                    project(f"br{l}_{n}", branch[n], 4, range(m, m + 2), out)
                mixed.split(acc, m, 2, dve.last())
            down(f"wo{l}", mixed, KD, add_gated(mod[:, 16:24]))

        def mixer_ab():
            fence()
            ar = Area()
            tab = ar.get(widths(TABA))
            ready = load_table(tab, ins["taba"])
            wg = ar.get(8, P)
            ready = load_table(wg, ins["rgw"])
            q, k, v = ar.get(4, T), ar.get(T), ar.get(2, P)
            bg = ar.get(4, T)
            pad = ar.get(4, T + 3)
            cv, ga, gi = ar.get(4, T), ar.get(4, T), ar.get(4, T)
            S, E, small, sc = ar.get(2048), ar.get(2048), ar.get(64), ar.get(8, 384)
            yb = Pair(g_hi, g_lo, 4)
            ya = Pair(g_hi, g_lo, 0)
            z = SET(pad[:, :, 0:3], 0.0)
            project("aq", h_pair, KD, range(4), to(q))
            project("ak", h_pair, KD, range(1), to(k.unsqueeze(1)))
            project_tokens("av", h_pair, P, to_tokens(v, P))
            for e in (pe, act, dve):
                e.wait(ready)
            bias_t = tab.rearrange("p (h w) -> p h w", h=A_HEADS)
            vq = act.last()

            def attention():
                for it in range(TT):
                    def scores(h, o, W, it=it):
                        lo = (h // 4) * 64
                        return matmul(o, q[lo:lo + 64, h % 4, it * P:(it + 1) * P], k[lo:lo + 64, 0:W],
                                      True, True, vq, mark=True)

                    def bias(h0, per, W):
                        return bias_t[:, h0:h0 + per, T - W:T]
                    yield from softmax_attention(8, it, scores, bias, 64 ** -0.5, S, E, small, sc,
                                                 sink=V("sinks", 0, 8))
                val = S[:, 0:1024].rearrange("p (h t) -> p h t", h=4)

                def out(h, b, mk):
                    lo = (h // 4) * 64
                    a = A(val[lo:lo + 64, h % 4:h % 4 + 2, :], b.halves()[lo:lo + 64, :, :], ACT.Copy, mk,
                          dve.last())
                    b.free = [a]
                values_times_scores(lambda h, t: v[:, t, :], sc, out, 8, act.last())
                for h in range(0, 4, 2):
                    ya.split(val[:, h:h + 2, :], h, 2, act.last())
                yield

            def rg_out(two, b, mk):
                b.free = [A(pad[:, two[0]:two[0] + 2, 3:T + 3], b.halves(), ACT.Copy, mk, z)]

            def recurrence():
                project("abx", h_pair, KD, range(2), rg_out)
                yield
                project("abx", h_pair, KD, range(2, 4), rg_out)
                yield
                project("abg", h_pair, KD, range(2), to(bg, ACT.Gelu_apprx_tanh))
                yield
                project("abg", h_pair, KD, range(2, 4), to(bg, ACT.Gelu_apprx_tanh))
                yield
                for j in range(4):
                    m = TS(cv[:, j, :], pad[:, j, 0:T], V("b_conv_w", j), ALU.mult, act.last(),
                           s2=V("b_conv_b", j), op1=ALU.add)
                    for t in range(1, 4):
                        m = STT(cv[:, j, :], pad[:, j, t:t + T], V("b_conv_w", 4 * t + j), cv[:, j, :],
                                ALU.mult, ALU.add, m)
                for w0, dst, bias in ((0, ga, "b_ba"), (4, gi, "b_bx")):
                    for j in range(0, 4, 2):
                        b = take()
                        for i in range(2):
                            mk = matmul(b.halves()[:, i, :], wg[:, w0 + j + i, :], cv[:, j + i, :],
                                        True, True, m, mark=True)
                        for i in range(2):
                            a = A(dst[:, j + i, :], b.halves()[:, i, :], ACT.Sigmoid, mk,
                                  bias=V(bias, j + i))
                        b.free = [a]
                    yield
                y, s_, s2, acc = (col[:, 24 + 4 * i:28 + 4 * i] for i in range(4))
                lam = V("b_lam", 0, 4)
                m = A(y, lam, ACT.Abs, m)
                m = A(y, y, ACT.Exp, m, scale=-1.0)
                m = TS(s_, y, 2.0, ALU.add, m)
                m = RCP(s_, s_, m)
                m = TTn(s_, s_, y, ALU.mult, m)
                m = TTn(s2, s_, s_, ALU.mult, m)
                m = SET(acc, 2.0 / 19, m)
                for n in range(17, 0, -2):
                    m = TTn(acc, acc, s2, ALU.mult, m)
                    m = TS(acc, acc, 2.0 / n, ALU.add, m)
                m = TTn(acc, acc, s_, ALU.mult, m)
                m = TS(y, lam, -1.0, ALU.mult, m, s2=0.0, op1=ALU.max)
                m = TTn(acc, acc, y, ALU.add, m)
                m = TS(acc, acc, 8.0, ALU.mult, m)
                yield
                for j in range(4):
                    m2 = TS(ga[:, j, :], ga[:, j, :], acc[:, j:j + 1], ALU.mult, m, act.last())
                th = pad[:, :, 0:T]
                m3 = A(th, ga, ACT.Tanh, m2)
                m2 = A(ga, ga, ACT.Exp, m3, scale=-1.0)
                m = TTn(gi, gi, cv, ALU.mult, m3)
                m = TS(cv, th, 1.0, ALU.add, m)
                m = RCP(cv, cv, m)
                m = TTn(cv, cv, th, ALU.mult, m)
                m = A(cv, cv, ACT.Sqrt, m, scale=2.0)
                m = TTn(gi, gi, cv, ALU.mult, m)
                for j in range(4):
                    m4 = SCAN(cv[:, j, :], ga[:, j, :], gi[:, j, :], m, m2)
                m = TTn(cv, cv, bg, ALU.mult, m4)
                for h in range(0, 4, 2):
                    yb.split(cv[:, h:h + 2, :], h, 2, m)
                yield

            weave(attention(), recurrence())
            both = Pair(g_hi, g_lo, 0)
            for i in range(4):
                both.ready[i], both.ready[4 + i] = ya.ready[i], yb.ready[i]
            down("abo", both, KD, add_scaled(1.0))

        def mixer_c():
            fence()
            ar = Area()
            tab = ar.get(widths(TABC))
            ready = load_table(tab, ins["tabc"])
            at = columns(TABC)

            def C(name):
                a, w = at[name]
                return tab[:, a:a + w]

            qkv = [ar.get(8, T) for _ in range(3)]
            q, k, v = qkv
            rows = ar.get(4, T)
            cols = ar.get(48)
            st = ar.get(8, P)
            conv_at = ar.at
            pad = [ar.get(2, T + 3) for _ in range(2)]
            con = [ar.get(2, T) for _ in range(2)]
            rs = ar.get(8, T)
            sq = ar.get(8, T)
            zeroed = [SET(p[:, :, 0:3], 0.0) for p in pad][1]

            def small_out(two, b, mk):
                b.free = [A(rows[0:8, 0, :], b.t[0:8, 0:T], ACT.Sigmoid, mk)]
                e_ = A(rows[0:8, 1, :], b.t[32:40, 0:T], ACT.Copy)
                b.free = [e_]
                TS(rows[0:8, 1, :], rows[0:8, 1, :], V("c_dt", rows=8), ALU.add, e_)
            project("cab", h_pair, KD, range(1), small_out)
            for e in (pe, act, dve):
                e.wait(ready)
            n = 0
            free = [zeroed, zeroed]
            for part, sec in enumerate(("cq", "ck", "cv")):
                def out(two, b, mk, part=part):
                    i = (two[0] // 2) % 2
                    pd, cn, dst = pad[i], con[i], qkv[part]
                    a = A(pd[:, :, 3:T + 3], b.halves(), ACT.Copy, mk, free[i])
                    b.free = [a]
                    for j, f in enumerate(two):
                        c0 = part * 8 + f
                        m = A(cn[:, j, :], pd[:, j, 3:T + 3], ACT.Identity, a, scale=V("c_conv_w", 72 + c0))
                    for j, f in enumerate(two):
                        c0 = part * 8 + f
                        for t in range(2, -1, -1):
                            m = STT(cn[:, j, :], pd[:, j, t:t + T], V("c_conv_w", 24 * t + c0),
                                    cn[:, j, :], ALU.mult, ALU.add, m)
                    free[i] = A(dst[:, two[0]:two[0] + 2, :], cn, ACT.Silu, m)
                project(sec, h_pair, KD, range(KD), out)
            a_, g_, t1, gc = rows[0:8, 1, :], rows[0:8, 2, :], rows[0:8, 3, :], rows[0:8, 1, :]
            m = A(g_, a_, ACT.Abs, dve.last())
            m = A(g_, g_, ACT.Exp, m, scale=-1.0)
            m = A(g_, g_, ACT.Ln, m, bias=const_col(1.0)[0][0:8, :])
            m1 = A(col[0:8, 40:41], V("c_a_log", rows=8), ACT.Exp)
            m = TS(t1, a_, 0.0, ALU.max, m, m1)
            m = TTn(g_, g_, t1, ALU.add, m)
            m = TS(g_, g_, col[0:8, 40:41], ALU.mult, m, s2=-1.0, op1=ALU.mult)
            m = SET(sq[0:8, 0, 0:P], 1.0, m)
            for t in range(TT):
                m = SCAN(gc[:, t * P:(t + 1) * P], sq[0:8, 0, 0:P], g_[:, t * P:(t + 1) * P], m)
            eg = rows[0:8, 2, :]
            m_eg = A(eg, gc, ACT.Exp, m)
            ngc = rows[0:8, 3, :]
            m_row = TS(ngc, gc, -1.0, ALU.mult, m)
            beta = rows[0:8, 0, :]
            for x, s in ((q, P ** -0.5), (k, 1.0)):
                r = head_norm(x, sq, rs, 8, EPS, dve.last(), scale=float(P))
                m_x = STT(x, x, s, rs, ALU.mult, ALU.mult, r)
            fence()
            ar.at = conv_at
            kb, dec, att, U, X, Xt, T1, vt = (ar.get(8, P) for _ in range(8))
            qg = ar.get(8, P)
            ekd = ar.get(P)
            sel = C("sel_c").rearrange("p (h w) -> p h w", h=8)
            levels = C("level").rearrange("p (n w) -> p n w", n=LEVELS)
            egc, bec, ekc = cols[:, 0:8], cols[:, 8:16], cols[:, 16:24]
            o_t = q

            def heads4(fn, consume, *after):
                marks = []
                for h0 in (0, 4):
                    b = take()
                    for h in range(h0, h0 + 4):
                        mk = fn(h, b.t[:, (h - h0) * P:(h - h0 + 1) * P], *after)
                    c = consume(slice(h0, h0 + 4), b.t[:, :].rearrange("p (h w) -> p h w", h=4), mk)
                    b.free = [c]
                    marks.append(c)
                return marks

            def mm(lhsT, rhs):
                return lambda h, o, *after: matmul(o, lhsT(h), rhs(h), True, True, *after, mark=True)

            for t in range(TT):
                tk = slice(t * P, (t + 1) * P)
                m = TS(ekd[0:8, :], gc[:, tk], gc[:, (t + 1) * P - 1:(t + 1) * P], ALU.subtract,
                       m_row, pe.last(), s2=-1.0, op1=ALU.mult)
                m = A(ekd[0:8, :], ekd[0:8, :], ACT.Exp, m)
                b = take()
                for i, src in enumerate((eg[:, tk], beta[:, tk], ekd[0:8, :])):
                    o = b.t[:, 8 * i:8 * i + 8]
                    mk = pe.do(lambda e, o=o, src=src: e.transpose(o, src, B("ident")[0:8, 0:8]), m, m_eg)
                m_c = A(cols[:, 0:24], b.t[:, 0:24], ACT.Copy, mk, dve.last())
                b.free = [m_c]
                ms = heads4(mm(lambda h: sel[0:8, h, :], lambda h: beta[:, tk]),
                            lambda s, p, mk: TTn(kb[:, s, :], k[:, s, tk], p, ALU.mult, mk), m_x)
                m_kb = ms[-1]
                def diff(h, o, *after):
                    matmul(o, sel[0:8, h, :], gc[:, tk], True, False, *after)
                    return matmul(o, ngc[:, tk], sel[0:8, h, :], False, True, mark=True)
                ms = heads4(diff, lambda s, p, mk: TTn(dec[:, s, :], p, bc(C("causal_t"), 4), ALU.add, mk),
                            m_row)
                m = A(dec, dec, ACT.Exp, ms[-1])
                heads4(mm(lambda h: k[:, h, tk], lambda h: q[:, h, tk]),
                       lambda s, p, mk: TTn(att[:, s, :], p, dec[:, s, :], ALU.mult, mk, m), m_kb)
                m_s = TTn(dec, dec, bc(C("strict"), 8), ALU.mult, dve.last())
                heads4(mm(lambda h: k[:, h, tk], lambda h: kb[:, h, :]),
                       lambda s, p, mk: TTn(U[:, s, :], p, dec[:, s, :], ALU.mult, mk, m_s), m_kb)
                m_att = dve.last()
                if t == 1:
                    heads4(mm(lambda h: sel[0:8, h, :], lambda h: eg[:, tk]),
                           lambda s, p, mk: TTn(qg[:, s, :], q[:, s, tk], p, ALU.mult, mk), m_eg)
                Um = dec
                m = TTn(Um, U, bc(levels[:, 0, :], 8), ALU.mult, m_att)
                m_xt = TTn(Xt, bc(B("ident"), 8), Um, ALU.subtract, m)

                def tr(src):
                    def fn(h, o, *after):
                        of = src(h)
                        return pe.do(lambda e: e.transpose(o, of, B("ident")), *after)
                    return fn
                m_X = heads4(tr(lambda h: Xt[:, h, :]),
                             lambda s, p, mk: A(X[:, s, :], p, ACT.Copy, mk, dve.last()), m_xt)[-1]
                for n in range(1, LEVELS):
                    m = TTn(Um, U, bc(levels[:, n, :], 8), ALU.mult, dve.last(), pe.last())
                    ms = heads4(mm(lambda h: Um[:, h, :], lambda h: X[:, h, :]),
                                lambda s, p, mk: A(T1[:, s, :], p, ACT.Copy, mk), m, m_X, dve.last())
                    if n < LEVELS - 1:
                        m_p = []
                        bs = []
                        for h0 in (0, 4):
                            b = take()
                            for h in range(h0, h0 + 4):
                                mk = matmul(b.t[:, (h - h0) * P:(h - h0 + 1) * P], Xt[:, h, :],
                                            T1[:, h, :], True, True, ms, m_xt, mark=True)
                            bs.append((b, mk))
                    m_xt2 = heads4(mm(lambda h: T1[:, h, :], lambda h: Xt[:, h, :]),
                                   lambda s, p, mk: TTn(Xt[:, s, :], Xt[:, s, :], p, ALU.subtract, mk),
                                   ms)
                    m_xt = m_xt2[-1]
                    if n < LEVELS - 1:
                        for i, (b, mk) in enumerate(bs):
                            s = slice(4 * i, 4 * i + 4)
                            m_X = TTn(X[:, s, :], X[:, s, :], b.t[:, :].rearrange("p (h w) -> p h w", h=4),
                                      ALU.subtract, mk)
                            b.free = [m_X]
                m_v = heads4(tr(lambda h: v[:, h, tk]),
                             lambda s, p, mk: A(vt[:, s, :], p, ACT.Copy, mk, dve.last()))[-1]
                if t == 1:
                    ms = heads4(mm(lambda h: k[:, h, tk], lambda h: st[:, h, :]),
                                lambda s, p, mk: TTn(T1[:, s, :], p, bl(egc[:, s], P), ALU.mult, mk, pe.last()),
                                m_st)
                    m_v = TTn(vt, vt, T1, ALU.subtract, ms[-1], m_v)
                m_v = TTn(vt, vt, bl(bec, P), ALU.mult, m_v)
                m_n = heads4(mm(lambda h: Xt[:, h, :], lambda h: vt[:, h, :]),
                             lambda s, p, mk: A(T1[:, s, :], p, ACT.Copy, mk, dve.last()), m_v, m_xt)[-1]
                if t == 0:
                    m_k = heads4(tr(lambda h: k[:, h, tk]),
                                 lambda s, p, mk: A(U[:, s, :], p, ACT.Copy, mk, dve.last()))[-1]
                    m = TTn(vt, T1, bl(ekc, P), ALU.mult, m_n, pe.last())
                    m_st = heads4(mm(lambda h: U[:, h, :], lambda h: vt[:, h, :]),
                                  lambda s, p, mk: A(st[:, s, :], p, ACT.Copy, mk), m_k, m)[-1]

                def outp(h, o, *after):
                    mk = matmul(o, T1[:, h, :], att[:, h, :], True, t == 0, *after, mark=t == 0)
                    if t == 1:
                        mk = matmul(o, st[:, h, :], qg[:, h, :], False, True, mark=True)
                    return mk
                heads4(outp, lambda s, p, mk: A(o_t[:, s, tk], p, ACT.Copy, mk), m_n, m_att, dve.last())
            fence()
            ar.at = conv_at
            rs, sq, zb = ar.get(8, T), ar.get(8, T), ar.get(8, T)
            r = head_norm(o_t, sq, rs, 8, EPS)
            m = STT(o_t, o_t, V("c_g"), rs, ALU.mult, ALU.mult, r)
            pair = Pair(g_hi, g_lo, 0)

            def z_out(two, b, mk):
                a = A(zb[:, two[0]:two[0] + 2, :], b.halves(), ACT.Silu, mk)
                b.free = [a]
                g = TTn(o_t[:, two[0]:two[0] + 2, :], o_t[:, two[0]:two[0] + 2, :],
                        zb[:, two[0]:two[0] + 2, :], ALU.mult, a, m)
                pair.split(o_t[:, two[0]:two[0] + 2, :], two[0], 2, g)
            project("cz", h_pair, KD, range(KD), z_out)
            down("cwo", pair, KD, add_scaled(1.0))

        def ple(l):
            fence()
            ar = Area()
            pt, pv, sg = ar.get(2, T), ar.get(8, T), [ar.get(2, T) for _ in range(2)]
            ready = load_table(pt, ins[f"p{l}"])
            pair = Pair(g_hi, g_lo, 0)
            pair.split(pt, 0, 2, ready)
            project(f"pp{l}", pair, 2, range(KD), to(pv))

            def out(two, b, mk):
                s = sg[(two[0] // 2) % 2]
                for j, m in enumerate(two):
                    a = A(s[:, j, :], b.halves()[:, j, :], ACT.Sigmoid, mk, dve.last(),
                          bias=V(f"ple_b{l}", m))
                b.free = [a]
                r = TTn(s, s, pv[:, two[0]:two[0] + 2, :], ALU.mult, a)
                TTn(x_t[:, two[0]:two[0] + 2, :], x_t[:, two[0]:two[0] + 2, :], s, ALU.add, r)
            project(f"pg{l}", h_pair, KD, range(KD), out)

        plan = []
        for l in range(DEPTH):
            def first(l=l):
                for _ in modulation(l, 0, 16):
                    pass
                modulated_norm(col[:, 8:16], mod[:, 0:8])
                mixer_one(l)

            def second(l=l):
                modulated_norm(col[:, 16:24], mod[:, 24:32])
                conv_ffn(l, mod[:, 40:48])
            plan += [first, second]
        for l in range(DEPTH):
            def ffn(l=l, f=1, i=0):
                if f == 1:
                    fence()
                    make_pair_of_x()
                swiglu(f"f{f}g{l}", f"f{f}u{l}", f"f{f}d{l}", add_scaled(0.5))
                layer_norm(l, i, scaled=f == 1)

            def mix(l=l):
                (mixer_ab if l == 0 else mixer_c)()
                layer_norm(l, 1)
            plan += [ffn, mix, lambda l=l, ffn=ffn: ffn(l, 2, 2), lambda l=l: ple(l)]
        for step in plan[:stages]:
            step()
        s_out = semaphore("output_written")
        sp.wait(dve.last(), act.last())
        sp.steps.append(("dma", lambda e: e.dma_start(out_ap, x_t[:, :, :]), s_out))
        sp.steps.append(("wait", s_out, 16))

        block = ctx.enter_context(nc.Block())

        @block.sync
        def _(e):
            sp.emit(e)

        @block.gpsimd
        def _(e):
            pool.emit(e)

        @block.scalar
        def _(e):
            act.emit(e)

        @block.vector
        def _(e):
            dve.emit(e)

        @block.tensor
        def _(e):
            pe.emit(e)


def pack_vectors(i):
    at, n = vector_columns()
    out = np.zeros((P, n), np.float32)

    def put(name, v):
        a, w = at[name]
        v = np.asarray(v).reshape(-1)
        if v.size < P:
            out[:v.size, a] = v
        else:
            out[:, a:a + w] = v.reshape(w, P).T
    put("c", i["c"])
    for l in range(DEPTH):
        for name, src in (("b_ada", "b_ada"), ("norm1_g", "norm1_g"), ("norm2_g", "norm2_g"),
                          ("b_gla", "b_gla_a"), ("b_fox", "b_fox_f"), ("ret_g", "ret_norm_g"),
                          ("gla_g", "gla_norm_g"), ("q_g", "q_norm_g"), ("k_g", "k_norm_g"),
                          ("b_mg", "b_mg"), ("w_conv", "w_conv"), ("b_conv", "b_conv"),
                          ("ple_b", "ple_bg_2")):
            put(f"{name}{l}", i[src][l])
        for j in range(3):
            put(f"ln_g{l}{j}", i["ln_g_2"][l, j])
            put(f"ln_b{l}{j}", i["ln_b_2"][l, j])
    a, w = at["sinks"]
    out[:, a:a + w] = np.asarray(i["a_sinks_2"])[0]
    for name, src in (("b_conv_w", "b_conv_w_2"), ("b_conv_b", "b_conv_b_2"), ("b_ba", "b_ba_2"),
                      ("b_bx", "b_bx_2"), ("b_lam", "b_lam_2"), ("c_conv_w", "c_conv_w_2"),
                      ("c_a_log", "c_a_log_2"), ("c_dt", "c_dt_bias_2"), ("c_g", "c_norm_g_2")):
        put(name, i[src][0])
    return out


def matrices(i):
    out = {}
    splits = [512, 512, 512, 512, 256, 256, 512, 16, 512, 512, 512, 512, 4]
    edges = np.cumsum([0] + splits)
    for l in range(DEPTH):
        w = i["w_in"][l]
        parts = [w[:, a:b] for a, b in zip(edges[:-1], edges[1:])]
        for name, part in zip(("rq", "rk", "rv", "rg", "gq", "gk", "gv", "lr", "gg", "fq", "fk", "fv", "ff"), parts):
            out[f"{name}{l}"] = part
        small = np.zeros((D, P), np.float32)
        small[:, 0:4] = out[f"ff{l}"]
        small[:, 32:48] = out[f"lr{l}"]
        out[f"small{l}"] = small
        out[f"ada{l}"] = i["w_ada"][l]
        out[f"mg{l}"] = i["w_mg"][l]
        for n in range(3):
            out[f"br{l}_{n}"] = i["w_br"][l, n]
        out[f"wo{l}"], out[f"up{l}"], out[f"down{l}"] = i["w_o"][l], i["w_up"][l], i["w_down"][l]
        for f in (1, 2):
            out[f"f{f}g{l}"], out[f"f{f}u{l}"], out[f"f{f}d{l}"] = (
                i[f"ffn{f}_wg_2"][l], i[f"ffn{f}_wu_2"][l], i[f"ffn{f}_wd_2"][l])
        out[f"pg{l}"], out[f"pp{l}"] = i["ple_wg_2"][l], i["ple_wp_2"][l]
    w = i["ab_w_in_2"][0]
    heads = np.array([h for c in range(4) for h in (c, c + 4)])
    perm = (heads[:, None] * 64 + np.arange(64)[None, :]).reshape(-1)
    out["aq"], out["ak"], out["av"] = w[:, perm], w[:, 512:640], w[:, 640:768]
    out["abx"], out["abg"] = w[:, 768:1280], w[:, 1280:1792]
    out["abo"] = i["ab_w_out_2"][0][np.concatenate([perm, np.arange(512, 1024)])]
    w = i["c_w_in_2"][0]
    for n, name in enumerate(("cq", "ck", "cv", "cz")):
        out[name] = w[:, n * D:(n + 1) * D]
    small = np.zeros((D, P), np.float32)
    small[:, 0:8], small[:, 32:40] = w[:, 4096:4104], w[:, 4104:4112]
    out["cab"] = small
    out["cwo"] = i["c_w_out_2"][0]
    return out


def pack_stream(i):
    order, mats = weight_order(), matrices(i)
    out = np.zeros((len(order) // DMA_TILES, P, DMA_TILES, P), np.float32)
    for n, t in enumerate(order):
        if t is not None:
            name, k, m, _ = t
            out[n // DMA_TILES, :, n % DMA_TILES, :] = mats[name][k * P:(k + 1) * P, m * P:(m + 1) * P]
    return out


def lay(table, parts):
    out = np.zeros((P, widths(table)), np.float32)
    for name, (a, w) in columns(table).items():
        v = parts[name]
        out[:v.shape[0], a:a + w] = v.reshape(v.shape[0], w)
    return out


def tables():
    i, j, t = np.arange(P), np.arange(P), np.arange(T)
    eye = np.eye(P)
    base = lay(BASE, {"ident": eye, "mean_d": np.full((P, P), 1.0 / D), "mean_h": np.full((P, P), 1.0 / P),
                      "center": eye - 1.0 / P, "resets": np.tile((t % CH != 0) * 1.0, (P, 1))})
    half = P // 2
    freq = (10000.0 ** (-np.arange(half, dtype=np.float32) / half)).astype(np.float32)
    ang = (t.astype(np.float32)[None, :] * freq[:, None]).astype(np.float32)
    cos, sin = np.cos(ang), np.sin(ang)
    swap = np.zeros((P, P))
    swap[(i + half) % P, i] = 1.0
    decay = np.zeros((P, HEADS, 384))
    gla = np.zeros((P, 384))
    for jt in range(TT):
        key, qs = jt * P + i[:, None], t[None, jt * P:]
        seen = key // CH <= qs // CH
        at = slice(0, T) if jt == 0 else slice(T, 384)
        for h in range(HEADS):
            lg = np.log1p(-(2.0 ** (-5.0 - h)))
            decay[:, h, at] = np.where(seen, np.exp(np.abs(qs - key) * lg), 0.0)
        gla[:, at] = seen * 64 ** -0.5
    causal = np.concatenate([np.zeros((P, P)), np.where(i[:, None] >= j[None, :], 0.0, NEG)], 1)
    sel = np.zeros((P, C_HEADS, P))
    for h in range(C_HEADS):
        sel[h, h, :] = 1.0
    tab1 = lay(TAB1, {"swap": swap, "cos": np.concatenate([cos, cos]), "sin": np.concatenate([-sin, sin]),
                      "decay": decay, "gla": gla, "causal": causal, "sel": sel[:, :HEADS]})
    bias = np.zeros((P, A_HEADS, T))
    qi = P + i[:, None]
    kj = t[None, :]
    near = (kj // CH <= qi // CH) & (kj // CH >= qi // CH - 2)
    for h in range(A_HEADS):
        bias[:, h] = np.where(near, -(2.0 ** -(h + 1.0)) * np.abs(qi - kj), NEG)
    taba = lay(TABA, {"bias": bias})
    level = np.zeros((P, LEVELS, P))
    for n in range(LEVELS):
        s = 2 ** n
        level[:, n] = (j[None, :] // (2 * s) == i[:, None] // (2 * s)) & (i[:, None] % (2 * s) < s) & (
            j[None, :] % (2 * s) >= s)
    tabc = lay(TABC, {"causal_t": np.where(i[:, None] <= j[None, :], 0.0, NEG),
                      "strict": (i[:, None] < j[None, :]) * 1.0, "level": level, "sel_c": sel})
    return {"base": base, "tab1": tab1, "taba": taba, "tabc": tabc}


def arrays_of(i):
    def blocks(x):
        f = x.shape[1]
        return np.ascontiguousarray(x.T.reshape(f // P, P, T).transpose(1, 0, 2))
    out = {"stream": pack_stream(i), "vec": pack_vectors(i), "xT": blocks(i["x"][0])}
    out.update(tables())
    rgw = np.zeros((P, 8, P), np.float32)
    for n, name in enumerate(("b_wa_2", "b_wx_2")):
        w = i[name][0]
        for b in range(8):
            s = slice((b % 2) * 64, (b % 2) * 64 + 64)
            rgw[s, 4 * n + b // 2, s] = w[b]
    out["rgw"] = rgw
    for l in range(DEPTH):
        a = np.zeros((48, 256), np.float32)
        a[32:48] = i["w_gla_a2"][l]
        out[f"wa2_{l}"] = a
        out[f"p{l}"] = blocks(i["p_2"][l, 0])
    return out


def make(nc, arrays, stages=None):
    ins = {n: nc.dram_tensor(f"in_{n}", a.shape, F32, kind="ExternalInput").ap() for n, a in arrays.items()}
    out = nc.dram_tensor("out", (P, KD, T), F32, kind="ExternalOutput").ap()
    build(nc, ins, out, stages)


def kernel(**inputs):
    import concourse.bacc as _bacc
    from concourse.bass_utils import run_bass_kernel_spmd as _run
    arrays = arrays_of({n: np.asarray(a) for n, a in inputs.items()})
    nc = _bacc.Bacc("TRN2", target_bir_lowering=False, num_devices=1)
    make(nc, arrays)
    r = _run(nc, [{f"in_{n}": a for n, a in arrays.items()}], core_ids=[0])
    got = np.asarray(r.results[0]["out"])
    return np.ascontiguousarray(got.transpose(1, 0, 2).reshape(D, T).T).reshape(1, T, D)
```

```python
import math
from contextlib import ExitStack

import numpy as np
import concourse.bass as bass
from concourse import mybir

P = 128
T = 256
D = 1024
KD = D // P
DEPTH = 2
FF = 2816
KF = FF // P
HEADS = 4
CH = 64
TT = T // P
EPS = 1e-6
LN_EPS = 1e-5
ALPHA = (2.0 * DEPTH) ** 0.25
NEG = -1e30
A_HEADS = 8
C_HEADS = 8
LEVELS = 7

TILE = P * P
DMA_TILES = 16
CUT_TILES = 8
RAW_SLOTS = 3
CUT_SLOTS = 4
AHEAD = CUT_SLOTS - 2

F32 = mybir.dt.float32
F32R = mybir.dt.float32r
ACT = mybir.ActivationFunctionType
ALU = mybir.AluOpType
AX = mybir.AxisListType


def ada_beside_gates(m):
    return range(16 + m, 18 + m) if m < 16 else range(32 + 2 * (m - 16), 36 + 2 * (m - 16))


def sections():
    out = []
    for l in range(DEPTH):
        if l == 0:
            out.append((f"ada{l}", KD, range(0, 16), "raw"))
        out.append((f"small{l}", KD, range(1), "m"))
        for n in ("rq", "rk"):
            out.append((f"{n}{l}", KD, range(4), "m"))
        out.append((f"rv{l}", KD, range(4), "k"))
        out.append((f"rg{l}", KD, range(4), "m"))
        out.append((f"gq{l}", KD, range(2), "m"))
        out.append((f"gk{l}", KD, range(2), "m"))
        out.append((f"gv{l}", KD, range(4), "k"))
        out.append((f"gg{l}", KD, range(4), "m"))
        for n in ("fq", "fk"):
            out.append((f"{n}{l}", KD, range(4), "m"))
        out.append((f"fv{l}", KD, range(4), "k"))
        for m in range(0, 24, 2):
            out.append((f"mg{l}", KD, range(m, m + 2), "m"))
            out.append((f"ada{l}", KD, ada_beside_gates(m), "raw"))
        for m in range(0, KD, 2):
            for n in range(3):
                out.append((f"br{l}_{n}", 4, range(m, m + 2), "m"))
        out.append((f"wo{l}", KD, range(KD), "m"))
        for m in range(0, KF, 2):
            out.append((f"up{l}", KD, range(m, m + 2), "m"))
            out.append((f"up{l}", KD, range(KF + m, KF + m + 2), "m"))
            if l + 1 < DEPTH and m < 16:
                out.append((f"ada{l + 1}", KD, range(m, m + 2), "raw"))
        out.append((f"down{l}", KF, range(KD), "m"))
    for l in range(DEPTH):
        for f in (1, 2):
            for m in range(0, KF, 2):
                out.append((f"f{f}g{l}", KD, range(m, m + 2), "m"))
                out.append((f"f{f}u{l}", KD, range(m, m + 2), "m"))
            out.append((f"f{f}d{l}", KF, range(KD), "m"))
            if f == 1 and l == 0:
                out.append(("aq", KD, range(4), "m"))
                out.append(("ak", KD, range(1), "m"))
                out.append(("av", KD, range(1), "k"))
                out.append(("abx", KD, range(4), "m"))
                out.append(("abg", KD, range(4), "m"))
                out.append(("abo", KD, range(KD), "m"))
            if f == 1 and l == 1:
                out.append(("cab", KD, range(1), "m"))
                for n in ("cq", "ck", "cv"):
                    out.append((n, KD, range(KD), "m"))
                out.append(("cz", KD, range(KD), "m"))
                out.append(("cwo", KD, range(KD), "m"))
        out.append((f"pp{l}", 2, range(KD), "m"))
        out.append((f"pg{l}", KD, range(KD), "m"))
    return out


def weight_order():
    order, raw = [], None
    for name, nk, ms, how in sections():
        if raw is not None and raw != (how == "raw"):
            order += [None] * (-len(order) % DMA_TILES)
        raw = how == "raw"
        if how == "k":
            order += [(name, k, m, True) for k in range(nk) for m in ms]
        else:
            order += [(name, k, m, not raw) for m in ms for k in range(nk)]
    return order + [None] * (-len(order) % DMA_TILES)


def vector_columns():
    sizes = []
    for l in range(DEPTH):
        sizes += [(f"b_ada{l}", 48), (f"norm1_g{l}", KD), (f"norm2_g{l}", KD), (f"b_gla{l}", 2),
                  (f"b_fox{l}", 1), (f"ret_g{l}", 4), (f"gla_g{l}", 1), (f"q_g{l}", 1),
                  (f"k_g{l}", 1), (f"b_mg{l}", 24), (f"w_conv{l}", 3 * KF), (f"b_conv{l}", KF),
                  (f"ple_b{l}", KD)]
        for i in range(3):
            sizes += [(f"ln_g{l}{i}", KD), (f"ln_b{l}{i}", KD)]
    sizes += [("sinks", A_HEADS), ("b_conv_w", 16), ("b_conv_b", 4), ("b_ba", 4), ("b_bx", 4),
              ("b_lam", 4), ("c_conv_w", 4 * 24), ("c_a_log", 1), ("c_dt", 1), ("c_g", 1)]
    out, at = {}, 0
    for n, s in sizes:
        out[n] = (at, s)
        at += s
    return out, at


BASE = [("ident", P), ("mean_d", P), ("pick", 16), ("center", P), ("resets", T)]
TAB1 = [("swap", P), ("cos", T), ("sin", T), ("decay", HEADS * 384), ("gla", 384), ("causal", T),
        ("sel", HEADS * P)]
TABA = [("bias", A_HEADS * T)]
TABC = [("causal_t", P), ("strict", P), ("level", LEVELS * P), ("sel_c", C_HEADS * P)]


def widths(table):
    return sum(w for _, w in table)


def columns(table):
    out, at = {}, 0
    for n, w in table:
        out[n] = (at, w)
        at += w
    return out


class Engine:

    def __init__(self, sem):
        self.sem, self.count, self.steps, self.passed = sem, 0, [], {}

    def wait(self, *marks):
        for mark in marks:
            if mark is None:
                continue
            if isinstance(mark, list):
                self.wait(*mark)
            elif self.passed.get(id(mark[0]), 0) < mark[1]:
                self.passed[id(mark[0])] = mark[1]
                self.steps.append(("wait", mark[0], mark[1]))

    def do(self, what, *after, mark=True):
        self.wait(*after)
        self.steps.append(("do", what, self.sem if mark else None))
        if mark:
            self.count += 1
            return (self.sem, self.count)
        return None

    def last(self):
        return (self.sem, self.count) if self.count else None

    def emit(self, eng):
        for kind, a, b in self.steps:
            if kind == "wait":
                eng.wait_ge(a, b)
            elif kind == "dma":
                a(eng).then_inc(b, 16)
            elif b is None:
                a(eng)
            else:
                a(eng).then_inc(b, 1)


def build(nc, ins, out_ap, stages):
    order = weight_order()
    vec_at, n_vec = vector_columns()
    ctx = ExitStack()
    with ctx:
        def sb(name, shape, dt=F32):
            return ctx.enter_context(nc.sbuf_tensor(name, shape, dt))

        def semaphore(name):
            return ctx.enter_context(nc.semaphore(name))

        pe, act, dve, pool, sp = (Engine(semaphore(f"{n}_done")) for n in ("pe", "act", "dve", "pool", "sp"))

        x_t = sb("x_t", [P, KD, T])
        h_hi = sb("h_hi", [P, KD, T], F32R)
        h_lo = sb("h_lo", [P, KD, T], F32R)
        g_hi = sb("g_hi", [P, KF, T], F32R)
        g_lo = sb("g_lo", [P, KF, T], F32R)
        raw = [sb(f"raw{i}", [P, DMA_TILES, P]) for i in range(RAW_SLOTS)]
        cut_hi = [sb(f"cut_hi{i}", [P, CUT_TILES, P], F32R) for i in range(CUT_SLOTS)]
        cut_lo = [sb(f"cut_lo{i}", [P, CUT_TILES, P], F32R) for i in range(CUT_SLOTS)]
        vec = sb("vec", [P, n_vec])
        base = sb("base", [P, widths(BASE)])
        mod = sb("mod", [P, 48])
        col = sb("col", [P, 64])
        WORK = 19900
        work = sb("work", [P, WORK])
        psum = [ctx.enter_context(nc.psum_tensor(f"psum{i}", [P, 512], F32)) for i in range(8)]

        base_at = columns(BASE)

        def B(name):
            a, w = base_at[name]
            return base[:, a:a + w]

        def V(name, i=0, n=1, rows=P):
            a, _ = vec_at[name]
            return vec[0:rows, a + i:a + i + n]

        class Bank:
            def __init__(self, t):
                self.t, self.free = t, []

            def halves(self):
                return self.t[:, :].rearrange("p (a t) -> p a t", a=2)

        banks = [Bank(t) for t in psum]
        turn = [0]

        def take():
            b = banks[turn[0] % len(banks)]
            turn[0] += 1
            marks, b.free = b.free, []
            pe.wait(marks)
            return b

        raw_ready = [semaphore(f"raw_ready{i}") for i in range(RAW_SLOTS)]
        n_loads = len(order) // DMA_TILES
        load_free = [None] * n_loads
        cut_mark = {}
        cut_free = {}
        state = {"loads": 0, "cuts": 0, "pos": 0}
        cuts_per_load = DMA_TILES // CUT_TILES
        stream = ins["stream"]

        def start_loads(upto):
            while state["loads"] <= min(upto, n_loads - 1):
                s = state["loads"]
                if s >= RAW_SLOTS:
                    sp.wait(load_free[s - RAW_SLOTS])
                sp.steps.append(("dma", lambda e, s=s: e.dma_start(
                    raw[s % RAW_SLOTS][:, :, :], stream[s]), raw_ready[s % RAW_SLOTS]))
                state["loads"] += 1

        def load_mark(s):
            return (raw_ready[s % RAW_SLOTS], 16 * (s // RAW_SLOTS + 1))

        def is_split(s):
            first = order[s * DMA_TILES]
            return first[3]

        def cut(g):
            s, half = divmod(g, cuts_per_load)
            if is_split(s):
                src = raw[s % RAW_SLOTS][:, half * CUT_TILES:(half + 1) * CUT_TILES, :]
                hi, lo = cut_hi[g % CUT_SLOTS], cut_lo[g % CUT_SLOTS]
                m = act.do(lambda e: e.activation(hi[:, :, :], src, ACT.Copy),
                           load_mark(s), cut_free.get(g - CUT_SLOTS))
                cut_mark[g] = dve.do(lambda e: e.tensor_tensor(
                    lo[:, :, :], src, hi[:, :, :].bitcast(F32), ALU.subtract), m)
                if half == cuts_per_load - 1:
                    load_free[s] = cut_mark[g]
                    start_loads(s + RAW_SLOTS)

        def cut_upto(g):
            while state["cuts"] <= min(g, n_loads * cuts_per_load - 1):
                cut(state["cuts"])
                state["cuts"] += 1

        start_loads(RAW_SLOTS - 1)

        class Weight:
            pass

        def weight(name, k, m, n=1):
            p = state["pos"]
            while order[p] is None:
                p += 1
            assert order[p][:3] == (name, k, m), (order[p], name, k, m)
            w = Weight()
            g = p // CUT_TILES
            s = p // DMA_TILES
            w.split = order[p][3]
            i = p % CUT_TILES
            w.group, w.load = g, s
            if w.split:
                cut_upto(g + AHEAD)
                w.hi = cut_hi[g % CUT_SLOTS][:, i:i + n, :].rearrange("p a b -> p (a b)")
                w.lo = cut_lo[g % CUT_SLOTS][:, i:i + n, :].rearrange("p a b -> p (a b)")
                w.ready = cut_mark[g]
            else:
                i = p % DMA_TILES
                cut_upto((s + 1) * cuts_per_load - 1)
                w.raw = raw[s % RAW_SLOTS][:, i:i + n, :].rearrange("p a b -> p (a b)")
                w.ready = load_mark(s)
            nxt = p + n
            while nxt < len(order) and order[nxt] is None:
                nxt += 1
            w.ends_group = nxt // CUT_TILES != g
            w.ends_load = nxt // DMA_TILES != s
            state["pos"] = p + n
            return w

        def used(w, mark):
            if w.split and w.ends_group:
                cut_free[w.group] = mark
            if not w.split and w.ends_load:
                load_free[w.load] = mark
                start_loads(w.load + RAW_SLOTS)

        def matmul(out, lhsT, rhs, start, stop, *after, mark=False):
            return pe.do(lambda e: e.matmul(out, lhsT, rhs, start=start, stop=stop), *after, mark=mark)

        class Pair:

            def __init__(self, hi, lo, first=0):
                self.hi, self.lo, self.first, self.ready = hi, lo, first, {}

            def part(self, lo, k, a=0, b=T):
                t = self.lo if lo else self.hi
                return t[:, self.first + k, a:b]

            def split(self, value, k, n, *after):
                f = self.first + k
                hi, lo = self.hi[:, f:f + n, :], self.lo[:, f:f + n, :]
                m = A(hi, value, ACT.Copy, *after)
                m = TTn(lo, value, hi.bitcast(F32), ALU.subtract, m)
                for i in range(k, k + n):
                    self.ready[i] = m
                return m

        h_pair = Pair(h_hi, h_lo)

        def three(out, w, pair, k, start, stop, swap, n_cols=None):
            parts = [(w.hi, 0), (w.hi, 1), (w.lo, 0)]
            for i, (wt, lo) in enumerate(parts):
                s, e_ = start and i == 0, stop and i == 2
                if swap is None:
                    yield wt, pair.part(lo, k), out, s, e_
                else:
                    yield pair.part(lo, k, swap * P, (swap + 1) * P), wt, out, s, e_

        late = []

        def flush(keep=0):
            while len(late) > keep:
                late.pop(0)()

        def project(sec, pair, nk, ms, evacuate):
            ms = list(ms)
            for i in range(0, len(ms), 2):
                two = ms[i:i + 2]
                b = take()
                for j, m in enumerate(two):
                    out = b.halves()[:, j, :]
                    for k in range(nk):
                        if k not in pair.ready:
                            flush()
                        w = weight(sec, k, m)
                        steps = list(three(out, w, pair, k, k == 0, k == nk - 1, None))
                        for n, (l, r, o, s, e_) in enumerate(steps):
                            end = n == 2 and (k == nk - 1 or w.ends_group)
                            mk = matmul(o, l, r, s, e_, w.ready, pair.ready[k], mark=end)
                        if mk is not None:
                            used(w, mk)
                flush()
                late.append(lambda two=two, b=b, mk=mk: evacuate(two, b, mk))

        def project_tokens(sec, pair, n_cols, evacuate):
            bs = [take() for _ in range(TT)]
            for k in range(KD):
                w = weight(sec, k, 0, n_cols // P)
                for t in range(TT):
                    steps = list(three(bs[t].t[:, 0:n_cols], w, pair, k, k == 0, k == KD - 1, t))
                    for n, (l, r, o, s, e_) in enumerate(steps):
                        mk = matmul(o, l, r, s, e_, w.ready, pair.ready[k],
                                    mark=n == 2 and (k == KD - 1 or t == TT - 1))
                    if k == KD - 1:
                        bs[t].done = mk
                w_pos = state["pos"]
                if n_cols // P > 1:
                    state["pos"] = w_pos
                used(w, mk)
            flush()
            for t in range(TT):
                late.append(lambda t=t: evacuate(t, bs[t], bs[t].done))

        def fence():
            flush()
            marks = [e.last() for e in (pe, act, dve, pool)]
            for e in (act, dve, pool):
                e.wait(*marks)

        class Area:
            def __init__(self, at=0):
                self.at = at

            def get(self, *shape):
                n = math.prod(shape)
                assert self.at + n <= WORK, (self.at, n)
                a = work[:, self.at:self.at + n]
                self.at += n
                if len(shape) == 2:
                    a = a.rearrange("p (a b) -> p a b", a=shape[0])
                if len(shape) == 3:
                    a = a.rearrange("p (a b c) -> p a b c", a=shape[0], b=shape[1])
                return a

        s_in = semaphore("inputs_ready")
        s_tab = semaphore("tables_ready")
        n_tab = [0]

        def load_in(dst, src):
            pool.steps.append(("dma", lambda e: e.dma_start(dst, src), s_in))

        c_row = work[:, WORK - D:WORK]
        load_in(c_row, ins["c_row"])
        load_in(vec[:, :], ins["vec"])
        load_in(base[:, :], ins["base"])
        load_in(x_t[:, :, :], ins["xT"])
        inputs = (s_in, 64)
        for e in (pe, act, dve, pool):
            e.wait(inputs)

        def load_table(dst, src):
            n_tab[0] += 16
            pool.steps.append(("dma", lambda e: e.dma_start(dst, src), s_tab))
            return (s_tab, n_tab[0])

        before = {}

        def behind(engine, what, *after):
            before[engine.sem.name] = m = engine.do(what, before.get(engine.sem.name), *after)
            return m

        def A(out, in_, f, *after, bias=0.0, scale=1.0):
            return behind(act, lambda e: e.activation(out, in_, f, bias=bias, scale=scale), *after)

        def TTn(out, a, b, op, *after):
            return behind(dve, lambda e: e.tensor_tensor(out, a, b, op), *after)

        def TS(out, a, s1, op0, *after, s2=None, op1=None):
            if op1 is None:
                return behind(dve, lambda e: e.tensor_scalar(out, a, s1, None, op0), *after)
            return behind(dve, lambda e: e.tensor_scalar(out, a, s1, s2, op0, op1), *after)

        def STT(out, a, s, b, op0, op1, *after):
            return behind(dve, lambda e: e.scalar_tensor_tensor(out, a, s, b, op0, op1), *after)

        def RED(out, in_, op, *after):
            return behind(dve, lambda e: e.tensor_reduce(out, in_, AX.X, op), *after)

        def RCP(out, in_, *after):
            return behind(dve, lambda e: e.reciprocal(out, in_), *after)

        def SCAN(out, a, b, *after):
            return behind(dve, lambda e: e.tensor_tensor_scan(out, a, b, 0.0, ALU.mult, ALU.add), *after)

        def SET(out, value, *after):
            return behind(dve, lambda e: e.memset(out, value), *after)

        eps_col = {}

        def const_col(value):
            if value not in eps_col:
                i = 60 + len(eps_col)
                eps_col[value] = (col[:, i:i + 1], SET(col[:, i:i + 1], value))
            return eps_col[value]

        for v in (EPS, LN_EPS, 1.0):
            const_col(v)
        act.wait(dve.last())

        def bc(ap, n):
            p, w = ap.shape
            return ap.unsqueeze(1).to_broadcast([p, n, w])

        def bl(ap, n):
            p, w = ap.shape
            return ap.unsqueeze(2).to_broadcast([p, w, n])

        stat = work[:, WORK - 2048:WORK - 1536].rearrange("p (a t) -> p a t", a=2)
        stat_sq = work[:, WORK - 1536:WORK - 1024].rearrange("p (a t) -> p a t", a=2)

        def sum_x(two, mark):
            x = x_t[:, two[0]:two[0] + 2, :]
            if two[0] == 0:
                TS(stat, x, 1.0, ALU.mult, mark)
            else:
                TTn(stat, stat, x, ALU.add, mark)

        def sum_squares(two, mark):
            x = x_t[:, two[0]:two[0] + 2, :]
            if two[0] == 0:
                A(stat, x, ACT.Square, mark, dve.last(), pe.last())
            else:
                m = A(stat_sq, x, ACT.Square, mark, dve.last())
                TTn(stat, stat, stat_sq, ALU.add, m)

        def pair_of_x(two, mark):
            x = x_t[:, two[0]:two[0] + 2, :]
            h_pair.split(x, two[0], 2, mark, pe.last())
            A(x, x, ACT.Copy, dve.last(), scale=ALPHA)

        def mean_of_stat():
            m = TTn(stat[:, 0, :], stat[:, 0, :], stat[:, 1, :], ALU.add, act.last())
            b = take()
            mk = matmul(b.t[:, 0:T], B("mean_d"), stat[:, 0, :], True, True, m, mark=True)
            return b, mk

        def inverse_root(b, out, mk, eps, n=T, scale=1.0):
            m = A(out, b.t[:, 0:n], ACT.Sqrt, mk, bias=const_col(eps)[0], scale=scale)
            b.free = [m]
            return RCP(out, out, m)

        def modulated_norm(gain, shift, r=None):
            fence()
            ar = Area(8192)
            rs, t1 = ar.get(T), ar.get(KD, T)
            b, mk = mean_of_stat()
            r = inverse_root(b, rs, mk, EPS)
            for k in range(KD):
                m = STT(t1[:, k, :], x_t[:, k, :], gain[:, k:k + 1], rs, ALU.mult, ALU.mult, r)
                m = A(h_hi[:, k, :], t1[:, k, :], ACT.Identity, m, bias=shift[:, k:k + 1])
                h_pair.ready[k] = STT(h_lo[:, k, :], t1[:, k, :], shift[:, k:k + 1],
                                      h_hi[:, k, :].bitcast(F32), ALU.add, ALU.subtract, m)

        def layer_norm(l, i, pair, factor, meanwhile=None):
            flush()
            ar = Area(8192)
            xc, sq, rs = ar.get(KD, T), ar.get(KD, T), ar.get(T)
            b, mk = mean_of_stat()
            if meanwhile is not None:
                meanwhile()
            v = take()
            for k in range(0, KD, 2):
                m = TTn(xc[:, k:k + 2, :], x_t[:, k:k + 2, :], bc(b.t[:, 0:T], 2), ALU.subtract, mk,
                        act.last())
                sm = A(sq[:, k:k + 2, :], xc[:, k:k + 2, :], ACT.Square, m)
                for j in range(k, k + 2):
                    mv = matmul(v.t[:, 0:T], B("mean_d"), sq[:, j, :], j == 0, j == KD - 1, sm, mark=True)
            b.free = [m]
            flush()
            r = inverse_root(v, rs, mv, LN_EPS)
            gain, shift = (lambda k: V(f"ln_g{l}{i}", k)), (lambda k: V(f"ln_b{l}{i}", k))
            for k in range(KD):
                m = STT(xc[:, k, :], xc[:, k, :], gain(k), rs, ALU.mult, ALU.mult, r)
                hi, lo = pair.hi[:, pair.first + k, :], pair.lo[:, pair.first + k, :]
                m = A(hi, xc[:, k, :], ACT.Identity, m, pe.last(), bias=shift(k))
                pair.ready[k] = STT(lo, xc[:, k, :], shift(k), hi.bitcast(F32), ALU.add,
                                    ALU.subtract, m)
            if factor != 1.0:
                scaled = TS(col[:, 48:56], V(f"ln_b{l}{i}", 0, KD), factor, ALU.mult)
            for k in range(KD):
                bias = shift(k) if factor == 1.0 else col[:, 48 + k:49 + k]
                A(x_t[:, k, :], xc[:, k, :], ACT.Identity, dve.last(), bias=bias, scale=factor)

        def down(sec, pair, nk, residual, after):
            def evacuate(two, b, mk):
                m = residual(two, b, mk)
                b.free = [m]
                if after is not None:
                    after(two, m)
            if after is pair_of_x:
                h_pair.ready.clear()
            project(sec, pair, nk, range(KD), evacuate)

        def add_gated(gate):
            def residual(two, b, mk):
                for j, m in enumerate(two):
                    r = STT(x_t[:, m, :], b.halves()[:, j, :], gate[:, m:m + 1], x_t[:, m, :],
                            ALU.mult, ALU.add, mk)
                return r
            return residual

        def add_scaled(scale):
            def residual(two, b, mk):
                return STT(x_t[:, two[0]:two[0] + 2, :], b.halves(), scale,
                           x_t[:, two[0]:two[0] + 2, :], ALU.mult, ALU.add, mk, act.last())
            return residual

        def swiglu(secg, secu, secd, residual, after, before_down=None):
            pair = Pair(g_hi, g_lo)
            ar = Area()
            silu = [ar.get(2, T) for _ in range(2)]
            val = [ar.get(2, T) for _ in range(2)]
            done = [None, None]
            for n, m in enumerate(range(0, KF, 2)):
                hold = {}

                def gate_out(two, b, mk, n=n, hold=hold):
                    hold["m"] = A(silu[n % 2], b.halves(), ACT.Silu, mk, done[n % 2])
                    b.free = [hold["m"]]

                def up_out(two, b, mk, n=n, m=m, hold=hold):
                    v = TTn(val[n % 2], silu[n % 2], b.halves(), ALU.mult, mk, hold["m"])
                    b.free = [v]
                    done[n % 2] = pair.split(val[n % 2], m, 2, v)

                project(secg, h_pair, KD, range(m, m + 2), gate_out)
                project(secu, h_pair, KD, range(m, m + 2), up_out)
            if before_down is not None:
                flush()
                before_down()
            down(secd, pair, KF, residual, after)

        def conv_ffn(l, gate, after):
            fence()
            pair = Pair(g_hi, g_lo)
            ar = Area()
            pad = [ar.get(2, T + 2) for _ in range(2)]
            con = [ar.get(2, T) for _ in range(2)]
            val = [ar.get(2, T) for _ in range(2)]
            zeroed = [SET(p[:, :, 0:2], 0.0) for p in pad]
            done = [zeroed[1], zeroed[1]]
            for n, m in enumerate(range(0, KF, 2)):
                hold = {}
                pd, cv, vl = pad[n % 2], con[n % 2], val[n % 2]

                def u_out(two, b, mk, n=n, pd=pd, cv=cv, hold=hold):
                    a = A(pd[:, :, 2:T + 2], b.halves(), ACT.Copy, mk, done[n % 2])
                    for j, f in enumerate(two):
                        b.free = [A(cv[:, j, :], b.halves()[:, j, :], ACT.Identity,
                                    bias=V(f"b_conv{l}", f), scale=V(f"w_conv{l}", 2 * KF + f))]
                    c = b.free[0]
                    for j, f in enumerate(two):
                        c1 = STT(cv[:, j, :], pd[:, j, 1:T + 1], V(f"w_conv{l}", KF + f), cv[:, j, :],
                                 ALU.mult, ALU.add, c)
                        c2 = STT(cv[:, j, :], pd[:, j, 0:T], V(f"w_conv{l}", f), cv[:, j, :],
                                 ALU.mult, ALU.add, c1)
                    hold["m"] = A(cv, cv, ACT.Silu, c2)

                def g_out(two, b, mk, n=n, m=m, cv=cv, vl=vl, hold=hold):
                    v = TTn(vl, cv, b.halves(), ALU.mult, mk, hold["m"])
                    b.free = [v]
                    done[n % 2] = pair.split(vl, m, 2, v)

                project(f"up{l}", h_pair, KD, range(m, m + 2), u_out)
                project(f"up{l}", h_pair, KD, range(KF + m, KF + m + 2), g_out)
                if l + 1 < DEPTH and m < 16:
                    modulate(l + 1, range(m, m + 2))
            down(f"down{l}", pair, KF, add_gated(gate), after)

        def to(out, f=ACT.Copy, bias=0.0, scale=1.0):
            def evacuate(two, b, mk):
                b.free = [A(out[:, two[0]:two[0] + len(two), :], b.halves()[:, 0:len(two), :], f, mk,
                            bias=bias, scale=scale)]
            return evacuate

        def to_tokens(out, n_cols):
            def evacuate(t, b, mk):
                b.free = [A(out[:, t, 0:n_cols], b.t[:, 0:n_cols], ACT.Copy, mk)]
            return evacuate

        def weave(main, filler):
            for _ in main:
                next(filler, None)
            for _ in filler:
                pass
            flush()

        def log_sigmoid(out, z, t1, t2, *after):
            m = A(t1, z, ACT.Abs, *after)
            m = A(t1, t1, ACT.Exp, m, scale=-1.0)
            m = A(t1, t1, ACT.Ln, m, bias=const_col(1.0)[0][0:t1.shape[0], :])
            m2 = TS(t2, z, 0.0, ALU.min)
            return TTn(out, t2, t1, ALU.subtract, m, m2)

        def head_norm(src, tmp, small, heads, eps, sel, *after, scale=1.0):
            m = A(tmp, src, ACT.Square, *after)
            b = take()
            for h in range(heads):
                mk = matmul(b.t[0:heads, 0:T], B("pick")[:, 8 - h:8 - h + heads], tmp[:, h, :],
                            h == 0, h == heads - 1, m, mark=True)
            rows = small[0:heads, 0:T]
            m = A(rows, b.t[0:heads, 0:T], ACT.Sqrt, mk, bias=const_col(eps)[0][0:heads, :], scale=scale)
            b.free = [m]
            m = RCP(rows, rows, m)

            def spread(h):
                b = take()
                for j in range(2):
                    mk = matmul(b.halves()[:, j, :], sel[0:heads, h + j, :], rows, True, True, m, mark=True)
                return b, mk
            return spread

        def values_times_scores(vals, sc, out, heads, *after):
            for h in range(heads):
                if h % 2 == 0:
                    b = take()
                o = b.halves()[:, h % 2, :]
                matmul(o, vals(h, 0), sc[:, h, 0:T], True, False, *after)
                mk = matmul(o[:, P:T], vals(h, 1), sc[:, h, T:T + P], False, True, mark=True)
                if h % 2 == 1:
                    out(h - 1, b, mk)

        def softmax_attention(heads, it, scores, bias, scale, S, E, small, sc, sink=None):
            W = P * (it + 1)
            per = 4 if it == 0 else 2
            Sv = S[:, 0:heads * W].rearrange("p (h w) -> p h w", h=heads)
            Ev = E[:, 0:heads * W].rearrange("p (h w) -> p h w", h=heads)
            for h0 in range(0, heads, per):
                b = take()
                v = b.t[:, :].rearrange("p (h w) -> p h w", h=per)
                for h in range(h0, h0 + per):
                    mk = scores(h, v[:, h - h0, :], W)
                m = STT(Sv[:, h0:h0 + per, :], v, scale, bias(h0, per, W), ALU.mult, ALU.add, mk,
                        act.last())
                b.free = [m]
                yield
            mx, sm, ex = (small[:, i * heads:(i + 1) * heads] for i in range(3))
            m = RED(mx, Sv, ALU.max, m)
            if sink is not None:
                m = TTn(mx, mx, sink, ALU.max, m)
                m1 = TTn(ex, sink, mx, ALU.subtract, m)
                mex = A(ex, ex, ACT.Exp, m1)
            m = TTn(Sv, Sv, bl(mx, W), ALU.subtract, m)
            m = A(Ev, Sv, ACT.Exp, m)
            yield
            m = RED(sm, Ev, ALU.add, m)
            if sink is not None:
                m = TTn(sm, sm, ex, ALU.add, m, mex)
            m = RCP(sm, sm, m)
            m = TTn(Ev, Ev, bl(sm, W), ALU.mult, m)
            yield
            pieces = [(h, jt) for jt in range(it + 1) for h in range(heads)]
            for i in range(0, len(pieces), 4):
                b = take()
                for n, (h, jt) in enumerate(pieces[i:i + 4]):
                    o, s_ = b.t[:, n * P:(n + 1) * P], Ev[:, h, jt * P:(jt + 1) * P]
                    mk = pe.do(lambda e, o=o, s_=s_: e.transpose(o, s_, B("ident")), m)
                h, jt = pieces[i]
                c0 = T if jt == 1 else it * P
                b.free = [A(sc[:, h:h + 4, c0:c0 + P], b.t[:, :].rearrange("p (h w) -> p h w", h=4),
                            ACT.Copy, mk)]
                yield

        c_ready = A(c_row, c_row, ACT.Silu)

        def modulate(l, blocks):
            for m in blocks:
                w = weight(f"ada{l}", 0, m, KD)
                mk = behind(dve, lambda e, w=w, m=m: e.tensor_tensor_reduce(
                    out=w.raw, in0=w.raw, in1=c_row, scale=1.0, scalar=0.0, op0=ALU.mult,
                    op1=ALU.add, accum_out=mod[:, m:m + 1]), w.ready, c_ready)
                used(w, mk)

        def modulated(l, first, n):
            m = TTn(mod[:, first:first + n], mod[:, first:first + n], V(f"b_ada{l}", first, n), ALU.add)
            if first == 0:
                STT(col[:, 8:16], mod[:, 8:16], 1.0, V(f"norm1_g{l}", 0, KD), ALU.add, ALU.mult, m)
            else:
                STT(col[:, 16:24], mod[:, 32:40], 1.0, V(f"norm2_g{l}", 0, KD), ALU.add, ALU.mult, m)

        def mixer_one(l):
            fence()
            ar = Area()
            tab = ar.get(widths(TAB1))
            ready = load_table(tab, ins["tab1"])
            at = columns(TAB1)

            def C(name):
                a, w = at[name]
                return tab[:, a:a + w]

            wa2 = ar.get(256)
            ready = load_table(wa2[0:48, :], ins[f"wa2_{l}"])
            r_at = ar.at
            rq, rk, rv, rg = ar.get(4, T), ar.get(4, T), ar.get(2, 512), ar.get(4, T)
            gq, gk, gv, gg = ar.get(2, T), ar.get(2, T), ar.get(2, 512), ar.get(4, T)
            kw_next = work[:, r_at:r_at + 3 * 512].rearrange("p (n a t) -> p n a t", n=3, a=2)
            kw = [gk] + [kw_next[:, n, :, :] for n in range(3)]
            r_end = ar.at
            fq, fk, fv = ar.get(4, T), ar.get(4, T), ar.get(2, 512)
            t_a, t_b, t_c = ar.get(1024), ar.get(1024), ar.get(1536)
            rows = ar.get(T)
            rows2 = ar.get(T)
            small = ar.get(64)
            ar2 = Area(r_at)
            gates = ar2.get(24, T)
            assert ar2.at <= r_end

            def four(x):
                return x[:, 0:1024].rearrange("p (h t) -> p h t", h=4)

            sel = C("sel").rearrange("p (h w) -> p h w", h=HEADS)
            branch = [Pair(g_hi, g_lo, 4 * n) for n in range(3)]
            sc = t_c.rearrange("p (h w) -> p h w", h=4)
            proj = lambda n, ms, ev: project(f"{n}{l}", h_pair, KD, ms, ev)

            def small_out(two, b, mk):
                b.free = [A(rows[0:48, :], b.t[0:48, 0:T], ACT.Copy, mk)]
            proj("small", range(1), small_out)
            proj("rq", range(4), to(rq))
            proj("rk", range(4), to(rk))
            project_tokens(f"rv{l}", h_pair, 512, to_tokens(rv, 512))
            proj("rg", range(4), to(rg, ACT.Silu))
            flush()
            for e in (pe, act, dve):
                e.wait(ready)

            def finish(o, gate, gain, pair, src_mark, center, eps, bufs):
                tmp, rs = bufs
                spread = head_norm(o, tmp, rs, 4, eps, sel, src_mark)
                for h in range(0, 4, 2):
                    b, mk = spread(h)
                    for j in range(2):
                        m = STT(o[:, h + j, :], o[:, h + j, :], gain(h + j), b.halves()[:, j, :],
                                ALU.mult, ALU.mult, mk)
                    b.free = [m]
                    m = TTn(o[:, h:h + 2, :], o[:, h:h + 2, :], gate[:, h:h + 2, :], ALU.mult, m)
                    pair.split(o[:, h:h + 2, :], h, 2, m)

            def retention():
                t1 = four(t_a)
                for x, s in ((rq, 1.0), (rk, P ** -0.5)):
                    last = None
                    for h in range(0, 4, 2):
                        b = take()
                        mk = matmul(b.t[:, :], C("swap"), x[:, h:h + 2, :].rearrange("p a t -> p (a t)"),
                                    True, True, act.last(), mark=True)
                        m = STT(t1[:, h:h + 2, :], b.halves(), s, bc(C("sin"), 2), ALU.mult, ALU.mult, mk)
                        b.free = [m]
                        m = STT(x[:, h:h + 2, :], x[:, h:h + 2, :], s, bc(C("cos"), 2), ALU.mult, ALU.mult, m)
                        last = TTn(x[:, h:h + 2, :], x[:, h:h + 2, :], t1[:, h:h + 2, :], ALU.add, m)
                    yield
                dec = C("decay").rearrange("p (h w) -> p h w", h=4)
                for h in range(4):
                    b = take()
                    matmul(b.t[:, 0:T], rk[:, h, 0:P], rq[:, h, :], True, True, last)
                    mk = matmul(b.t[:, T:T + P], rk[:, h, P:T], rq[:, h, P:T], True, True, mark=True)
                    m = TTn(sc[:, h, :], b.t[:, 0:T + P], dec[:, h, :], ALU.mult, mk)
                    b.free = [m]
                    if h % 2:
                        yield
                o = four(t_a)
                marks = []

                def out(h, b, mk):
                    a = A(o[:, h:h + 2, :], b.halves(), ACT.Copy, mk, dve.last())
                    b.free = [a]
                    marks.append(a)
                values_times_scores(lambda h, t: rv[:, t, h * P:(h + 1) * P], sc, out, 4, m)
                yield
                for h in range(0, 4, 2):
                    b = take()
                    mk = matmul(b.t[:, :], B("center"), o[:, h:h + 2, :].rearrange("p a t -> p (a t)"),
                                True, True, marks[-1], mark=True)
                    a = A(o[:, h:h + 2, :], b.halves(), ACT.Copy, mk)
                    b.free = [a]
                yield
                finish(o, rg, lambda h: V(f"ret_g{l}", h), branch[0], a, True, EPS,
                       (four(t_b), t_c))
                yield

            def gla_proj():
                proj("gq", range(2), to(gq))
                yield
                proj("gk", range(2), to(gk))
                yield
                project_tokens(f"gv{l}", h_pair, 512, to_tokens(gv, 512))
                yield
                proj("gg", range(2), to(gg, ACT.Silu))
                yield
                proj("gg", range(2, 4), to(gg, ACT.Silu))
                yield

            def fox_proj():
                for n, x in (("fq", fq), ("fk", fk)):
                    proj(n, range(2), to(x))
                    yield
                    proj(n, range(2, 4), to(x))
                    yield
                project_tokens(f"fv{l}", h_pair, 512, to_tokens(fv, 512))
                yield

            def gla():
                la = t_a[:, 0:512].rearrange("p (a t) -> p a t", a=2)
                t2 = t_a[:, 512:1024].rearrange("p (a t) -> p a t", a=2)
                t3 = t_b[:, 0:512].rearrange("p (a t) -> p a t", a=2)
                b = take()
                for j in range(2):
                    mk = matmul(b.halves()[:, j, :], wa2[32:48, j * P:(j + 1) * P], rows[32:48, :],
                                True, True, act.last(), mark=True)
                for j in range(2):
                    m = TS(la[:, j, :], b.halves()[:, j, :], V(f"b_gla{l}", j), ALU.add, mk, act.last())
                b.free = [m]
                m = log_sigmoid(la, la, t3, t2, m)
                m = TS(la, la, 1.0 / 16.0, ALU.mult, m)
                cum = t2
                for j in range(2):
                    m2 = SCAN(cum[:, j, :], B("resets"), la[:, j, :], m)
                ends = small[:, 0:8].rearrange("p (a n) -> p a n", a=2)
                for j in range(2):
                    c4 = cum[:, j, :].rearrange("p (n i) -> p n i", n=4)
                    m = TTn(t3[:, j, :].rearrange("p (n i) -> p n i", n=4),
                            c4[:, :, CH - 1:CH].to_broadcast([P, 4, CH]), c4, ALU.subtract, m2)
                    m = A(ends[:, j, :].unsqueeze(2), c4[:, :, CH - 1:CH], ACT.Exp, m)
                m = A(t3, t3, ACT.Exp, m)
                yield
                m = TTn(kw[0], gk, t3, ALU.mult, m)
                for n in range(1, 4):
                    for j in range(2):
                        m2 = TS(kw[n][:, j, 0:n * CH], kw[n - 1][:, j, 0:n * CH], ends[:, j, n:n + 1],
                                ALU.mult, m)
                        m3 = TS(kw[n][:, j, n * CH:T], kw[0][:, j, n * CH:T], 1.0, ALU.mult, m)
                    m = m3
                yield
                mask = C("gla")
                for h in range(4):
                    j, lo = h // 2, (h % 2) * 64
                    b = take()
                    for n in range(4):
                        q_ = gq[lo:lo + 64, j, n * CH:(n + 1) * CH]
                        mk = matmul(b.t[:, n * CH:(n + 1) * CH], kw[n][lo:lo + 64, j, 0:P], q_,
                                    True, True, m, mark=n < 2)
                        if n >= 2:
                            c = T + (n - 2) * CH
                            mk = matmul(b.t[:, c:c + CH], kw[n][lo:lo + 64, j, P:T], q_, True, True,
                                        mark=True)
                    s = TTn(sc[:, h, :], b.t[:, 0:T + P], mask, ALU.mult, mk, act.last())
                    b.free = [s]
                    if h % 2:
                        yield
                o = four(t_a)
                marks = []

                def out(h, b, mk):
                    a = A(o[:, h:h + 2, :], b.halves(), ACT.Copy, mk, dve.last())
                    b.free = [a]
                    marks.append(a)
                values_times_scores(lambda h, t: gv[:, t, h * P:(h + 1) * P], sc, out, 4, s)
                yield
                finish(o, gg, lambda h: V(f"gla_g{l}", 0), branch[1], marks[-1], False, EPS,
                       (four(t_b), t_c))
                yield

            def fox():
                lf, t1 = t_a[0:4, 0:T], t_a[0:4, T:2 * T]
                m = TS(lf, rows[0:4, :], V(f"b_fox{l}", rows=4), ALU.add, act.last(), pe.last())
                m = log_sigmoid(lf, lf, t1, rows2[0:4, :], m)
                ones = t_b[0:4, 0:T]
                m = SET(ones, 1.0, m)
                cum, ncum = rows[0:4, :], rows2[0:4, :]
                m = SCAN(cum, ones, lf, m)
                c_m = TS(ncum, cum, -1.0, ALU.mult, m)
                yield
                for x, g, s in ((fq, f"q_g{l}", P ** -0.5), (fk, f"k_g{l}", 1.0)):
                    spread = head_norm(x, four(t_b), t_c, 4, EPS, sel, dve.last())
                    for h in range(0, 4, 2):
                        b, mk = spread(h)
                        m = STT(x[:, h:h + 2, :], x[:, h:h + 2, :], V(g), b.halves(), ALU.mult, ALU.mult, mk)
                        b.free = [m]
                    if s != 1.0:
                        m = TS(x, x, s, ALU.mult, m)
                    yield
                fence()
                for it in range(TT):
                    def scores(h, o, W, it=it):
                        for c in range(0, W, P):
                            w_ = slice(c, c + P)
                            matmul(o[:, w_], fq[:, h, it * P:(it + 1) * P], fk[:, h, w_], True, False, m, c_m)
                            matmul(o[:, w_], sel[0:4, h, :], ncum[:, w_], False, False)
                            mk = matmul(o[:, w_], cum[:, it * P:(it + 1) * P], sel[0:4, h, :],
                                        False, True, mark=True)
                        return mk

                    def bias(h0, per, W):
                        return bc(C("causal")[:, T - W:T], per)
                    yield from softmax_attention(4, it, scores, bias, 1.0, t_a, t_b, small, sc)
                o = four(t_a)

                def out(h, b, mk):
                    a = A(o[:, h:h + 2, :], b.halves(), ACT.Copy, mk, dve.last())
                    b.free = [a]
                    branch[2].split(o[:, h:h + 2, :], h, 2, a)
                values_times_scores(lambda h, t: fv[:, t, h * P:(h + 1) * P], sc, out, 4, act.last())
                yield

            def gate_proj(free):
                def out(two, b, mk):
                    for j, m in enumerate(two):
                        a = A(gates[:, m, :], b.halves()[:, j, :], ACT.Sigmoid, mk, free,
                              bias=V(f"b_mg{l}", m))
                    b.free = [a]
                for m in range(0, 24, 2):
                    proj("mg", range(m, m + 2), out)
                    modulate(l, ada_beside_gates(m))
                    yield
                modulated(l, 16, 32)

            weave(retention(), gla_proj())
            weave(gla(), fox_proj())
            weave(fox(), gate_proj([pe.last(), dve.last(), act.last()]))

            mixed = Pair(g_hi, g_lo, 12)
            for m in range(0, KD, 2):
                acc, t1 = four(t_a)[:, 0:2, :], four(t_a)[:, 2:4, :]
                for n in range(3):
                    def out(two, b, mk, n=n, m=m):
                        g = gates[:, n * KD + m:n * KD + m + 2, :]
                        dst = acc if n == 0 else t1
                        r = TTn(dst, b.halves(), g, ALU.mult, mk, dve.last(), act.last())
                        b.free = [r]
                        if n:
                            r = TTn(acc, acc, t1, ALU.add, r)
                        if n == 2:
                            mixed.split(acc, m, 2, r)
                    project(f"br{l}_{n}", branch[n], 4, range(m, m + 2), out)
            down(f"wo{l}", mixed, KD, add_gated(mod[:, 16:24]), sum_squares)

        def mixer_ab():
            fence()
            ar = Area()
            tab = ar.get(widths(TABA))
            ready = load_table(tab, ins["taba"])
            wg = ar.get(8, P)
            ready = load_table(wg, ins["rgw"])
            q, k, v = ar.get(4, T), ar.get(T), ar.get(2, P)
            bg = ar.get(4, T)
            pad = ar.get(4, T + 3)
            cv, ga, gi = ar.get(4, T), ar.get(4, T), ar.get(4, T)
            S, E, small, sc = ar.get(2048), ar.get(2048), ar.get(64), ar.get(8, 384)
            yb = Pair(g_hi, g_lo, 4)
            ya = Pair(g_hi, g_lo, 0)
            z = SET(pad[:, :, 0:3], 0.0)
            project("aq", h_pair, KD, range(4), to(q))
            project("ak", h_pair, KD, range(1), to(k.unsqueeze(1)))
            project_tokens("av", h_pair, P, to_tokens(v, P))
            flush()
            for e in (pe, act, dve):
                e.wait(ready)
            bias_t = tab.rearrange("p (h w) -> p h w", h=A_HEADS)
            vq = act.last()

            def attention():
                for it in range(TT):
                    def scores(h, o, W, it=it):
                        lo = (h // 4) * 64
                        return matmul(o, q[lo:lo + 64, h % 4, it * P:(it + 1) * P], k[lo:lo + 64, 0:W],
                                      True, True, vq, mark=True)

                    def bias(h0, per, W):
                        return bias_t[:, h0:h0 + per, T - W:T]
                    yield from softmax_attention(8, it, scores, bias, 64 ** -0.5, S, E, small, sc,
                                                 sink=V("sinks", 0, 8))
                val = S[:, 0:1024].rearrange("p (h t) -> p h t", h=4)

                def out(h, b, mk):
                    lo = (h // 4) * 64
                    a = A(val[lo:lo + 64, h % 4:h % 4 + 2, :], b.halves()[lo:lo + 64, :, :], ACT.Copy, mk,
                          dve.last())
                    b.free = [a]
                values_times_scores(lambda h, t: v[:, t, :], sc, out, 8, act.last())
                for h in range(0, 4, 2):
                    ya.split(val[:, h:h + 2, :], h, 2, act.last())
                yield

            def rg_out(two, b, mk):
                b.free = [A(pad[:, two[0]:two[0] + 2, 3:T + 3], b.halves(), ACT.Copy, mk, z)]

            def recurrence():
                project("abx", h_pair, KD, range(2), rg_out)
                yield
                project("abx", h_pair, KD, range(2, 4), rg_out)
                yield
                project("abg", h_pair, KD, range(2), to(bg, ACT.Gelu_apprx_tanh))
                yield
                project("abg", h_pair, KD, range(2, 4), to(bg, ACT.Gelu_apprx_tanh))
                yield
                flush()
                for j in range(4):
                    m = TS(cv[:, j, :], pad[:, j, 0:T], V("b_conv_w", j), ALU.mult, act.last(),
                           s2=V("b_conv_b", j), op1=ALU.add)
                    for t in range(1, 4):
                        m = STT(cv[:, j, :], pad[:, j, t:t + T], V("b_conv_w", 4 * t + j), cv[:, j, :],
                                ALU.mult, ALU.add, m)
                for w0, dst, bias in ((0, ga, "b_ba"), (4, gi, "b_bx")):
                    for j in range(0, 4, 2):
                        b = take()
                        for i in range(2):
                            mk = matmul(b.halves()[:, i, :], wg[:, w0 + j + i, :], cv[:, j + i, :],
                                        True, True, m, mark=True)
                        for i in range(2):
                            a = A(dst[:, j + i, :], b.halves()[:, i, :], ACT.Sigmoid, mk,
                                  bias=V(bias, j + i))
                        b.free = [a]
                    yield
                y, s_, s2, acc = (col[:, 24 + 4 * i:28 + 4 * i] for i in range(4))
                lam = V("b_lam", 0, 4)
                m = A(y, lam, ACT.Abs, m)
                m = A(y, y, ACT.Exp, m, scale=-1.0)
                m = TS(s_, y, 2.0, ALU.add, m)
                m = RCP(s_, s_, m)
                m = TTn(s_, s_, y, ALU.mult, m)
                m = TTn(s2, s_, s_, ALU.mult, m)
                m = SET(acc, 2.0 / 19, m)
                for n in range(17, 0, -2):
                    m = TTn(acc, acc, s2, ALU.mult, m)
                    m = TS(acc, acc, 2.0 / n, ALU.add, m)
                m = TTn(acc, acc, s_, ALU.mult, m)
                m = TS(y, lam, -1.0, ALU.mult, m, s2=0.0, op1=ALU.max)
                m = TTn(acc, acc, y, ALU.add, m)
                m = TS(acc, acc, 8.0, ALU.mult, m)
                yield
                for j in range(4):
                    m2 = TS(ga[:, j, :], ga[:, j, :], acc[:, j:j + 1], ALU.mult, m, act.last())
                th = pad[:, :, 0:T]
                m3 = A(th, ga, ACT.Tanh, m2)
                m2 = A(ga, ga, ACT.Exp, m3, scale=-1.0)
                m = TTn(gi, gi, cv, ALU.mult, m3)
                m = TS(cv, th, 1.0, ALU.add, m)
                m = RCP(cv, cv, m)
                m = TTn(cv, cv, th, ALU.mult, m)
                m = A(cv, cv, ACT.Sqrt, m, scale=2.0)
                m = TTn(gi, gi, cv, ALU.mult, m)
                for j in range(4):
                    m4 = SCAN(cv[:, j, :], ga[:, j, :], gi[:, j, :], m, m2)
                m = TTn(cv, cv, bg, ALU.mult, m4)
                for h in range(0, 4, 2):
                    yb.split(cv[:, h:h + 2, :], h, 2, m)
                yield

            weave(attention(), recurrence())
            both = Pair(g_hi, g_lo, 0)
            for i in range(4):
                both.ready[i], both.ready[4 + i] = ya.ready[i], yb.ready[i]
            down("abo", both, KD, add_scaled(1.0), sum_x)

        def mixer_c():
            fence()
            ar = Area()
            tab = ar.get(widths(TABC))
            ready = load_table(tab, ins["tabc"])
            at = columns(TABC)

            def C(name):
                a, w = at[name]
                return tab[:, a:a + w]

            qkv = [ar.get(8, T) for _ in range(3)]
            q, k, v = qkv
            rows = ar.get(4, T)
            cols = ar.get(48)
            st = ar.get(8, P)
            conv_at = ar.at
            pad = [ar.get(2, T + 3) for _ in range(2)]
            con = [ar.get(2, T) for _ in range(2)]
            rs = ar.get(8, T)
            sq = ar.get(8, T)
            sel = C("sel_c").rearrange("p (h w) -> p h w", h=8)
            zeroed = [SET(p[:, :, 0:3], 0.0) for p in pad][1]

            def small_out(two, b, mk):
                b.free = [A(rows[0:8, 0, :], b.t[0:8, 0:T], ACT.Sigmoid, mk)]
                e_ = A(rows[0:8, 1, :], b.t[32:40, 0:T], ACT.Copy)
                b.free = [e_]
                TS(rows[0:8, 1, :], rows[0:8, 1, :], V("c_dt", rows=8), ALU.add, e_)
            project("cab", h_pair, KD, range(1), small_out)
            for e in (pe, act, dve):
                e.wait(ready)
            n = 0
            free = [zeroed, zeroed]
            for part, sec in enumerate(("cq", "ck", "cv")):
                def out(two, b, mk, part=part):
                    i = (two[0] // 2) % 2
                    pd, cn, dst = pad[i], con[i], qkv[part]
                    a = A(pd[:, :, 3:T + 3], b.halves(), ACT.Copy, mk, free[i])
                    b.free = [a]
                    for j, f in enumerate(two):
                        c0 = part * 8 + f
                        m = A(cn[:, j, :], pd[:, j, 3:T + 3], ACT.Identity, a, scale=V("c_conv_w", 72 + c0))
                    for j, f in enumerate(two):
                        c0 = part * 8 + f
                        for t in range(2, -1, -1):
                            m = STT(cn[:, j, :], pd[:, j, t:t + T], V("c_conv_w", 24 * t + c0),
                                    cn[:, j, :], ALU.mult, ALU.add, m)
                    free[i] = A(dst[:, two[0]:two[0] + 2, :], cn, ACT.Silu, m)
                project(sec, h_pair, KD, range(KD), out)
            flush()
            a_, g_, t1, gc = rows[0:8, 1, :], rows[0:8, 2, :], rows[0:8, 3, :], rows[0:8, 1, :]
            m = A(g_, a_, ACT.Abs, dve.last())
            m = A(g_, g_, ACT.Exp, m, scale=-1.0)
            m = A(g_, g_, ACT.Ln, m, bias=const_col(1.0)[0][0:8, :])
            m1 = A(col[0:8, 40:41], V("c_a_log", rows=8), ACT.Exp)
            m = TS(t1, a_, 0.0, ALU.max, m, m1)
            m = TTn(g_, g_, t1, ALU.add, m)
            m = TS(g_, g_, col[0:8, 40:41], ALU.mult, m, s2=-1.0, op1=ALU.mult)
            m = SET(sq[0:8, 0, 0:P], 1.0, m)
            for t in range(TT):
                m = SCAN(gc[:, t * P:(t + 1) * P], sq[0:8, 0, 0:P], g_[:, t * P:(t + 1) * P], m)
            eg = rows[0:8, 2, :]
            m_eg = A(eg, gc, ACT.Exp, m)
            ngc = rows[0:8, 3, :]
            m_row = TS(ngc, gc, -1.0, ALU.mult, m)
            beta = rows[0:8, 0, :]
            for x, s in ((q, P ** -0.5), (k, 1.0)):
                spread = head_norm(x, sq, rs[:, 0, :], 8, EPS, sel, dve.last(), scale=float(P))
                for h in range(0, 8, 2):
                    b, mk = spread(h)
                    m_x = STT(x[:, h:h + 2, :], x[:, h:h + 2, :], s, b.halves(), ALU.mult, ALU.mult, mk)
                    b.free = [m_x]
            fence()
            ar.at = conv_at
            kb, dec, att, U, X, Xt, T1, vt = (ar.get(8, P) for _ in range(8))
            qg = ar.get(8, P)
            ekd = ar.get(P)
            levels = C("level").rearrange("p (n w) -> p n w", n=LEVELS)
            egc, bec, ekc = cols[:, 0:8], cols[:, 8:16], cols[:, 16:24]
            o_t = q

            def heads4(fn, consume, *after):
                marks = []
                for h0 in (0, 4):
                    b = take()
                    for h in range(h0, h0 + 4):
                        mk = fn(h, b.t[:, (h - h0) * P:(h - h0 + 1) * P], *after)
                    c = consume(slice(h0, h0 + 4), b.t[:, :].rearrange("p (h w) -> p h w", h=4), mk)
                    b.free = [c]
                    marks.append(c)
                return marks

            def mm(lhsT, rhs):
                return lambda h, o, *after: matmul(o, lhsT(h), rhs(h), True, True, *after, mark=True)

            for t in range(TT):
                tk = slice(t * P, (t + 1) * P)
                m = TS(ekd[0:8, :], gc[:, tk], gc[:, (t + 1) * P - 1:(t + 1) * P], ALU.subtract,
                       m_row, pe.last(), s2=-1.0, op1=ALU.mult)
                m = A(ekd[0:8, :], ekd[0:8, :], ACT.Exp, m)
                b = take()
                for i, src in enumerate((eg[:, tk], beta[:, tk], ekd[0:8, :])):
                    o = b.t[:, 8 * i:8 * i + 8]
                    mk = pe.do(lambda e, o=o, src=src: e.transpose(o, src, B("ident")[0:8, 0:8]), m, m_eg)
                m_c = A(cols[:, 0:24], b.t[:, 0:24], ACT.Copy, mk, dve.last())
                b.free = [m_c]
                ms = heads4(mm(lambda h: sel[0:8, h, :], lambda h: beta[:, tk]),
                            lambda s, p, mk: TTn(kb[:, s, :], k[:, s, tk], p, ALU.mult, mk), m_x)
                m_kb = ms[-1]
                def diff(h, o, *after):
                    matmul(o, sel[0:8, h, :], gc[:, tk], True, False, *after)
                    return matmul(o, ngc[:, tk], sel[0:8, h, :], False, True, mark=True)
                ms = heads4(diff, lambda s, p, mk: TTn(dec[:, s, :], p, bc(C("causal_t"), 4), ALU.add, mk),
                            m_row)
                m = A(dec, dec, ACT.Exp, ms[-1])
                heads4(mm(lambda h: k[:, h, tk], lambda h: q[:, h, tk]),
                       lambda s, p, mk: TTn(att[:, s, :], p, dec[:, s, :], ALU.mult, mk, m), m_kb)
                m_s = TTn(dec, dec, bc(C("strict"), 8), ALU.mult, dve.last())
                heads4(mm(lambda h: k[:, h, tk], lambda h: kb[:, h, :]),
                       lambda s, p, mk: TTn(U[:, s, :], p, dec[:, s, :], ALU.mult, mk, m_s), m_kb)
                m_att = dve.last()
                if t == 1:
                    heads4(mm(lambda h: sel[0:8, h, :], lambda h: eg[:, tk]),
                           lambda s, p, mk: TTn(qg[:, s, :], q[:, s, tk], p, ALU.mult, mk), m_eg)
                Um = dec
                m = TTn(Um, U, bc(levels[:, 0, :], 8), ALU.mult, m_att)
                m_xt = TTn(Xt, bc(B("ident"), 8), Um, ALU.subtract, m)

                def tr(src):
                    def fn(h, o, *after):
                        of = src(h)
                        return pe.do(lambda e: e.transpose(o, of, B("ident")), *after)
                    return fn
                m_X = heads4(tr(lambda h: Xt[:, h, :]),
                             lambda s, p, mk: A(X[:, s, :], p, ACT.Copy, mk, dve.last()), m_xt)[-1]
                for n in range(1, LEVELS):
                    m = TTn(Um, U, bc(levels[:, n, :], 8), ALU.mult, dve.last(), pe.last())
                    ms = heads4(mm(lambda h: Um[:, h, :], lambda h: X[:, h, :]),
                                lambda s, p, mk: A(T1[:, s, :], p, ACT.Copy, mk), m, m_X, dve.last())
                    if n < LEVELS - 1:
                        m_p = []
                        bs = []
                        for h0 in (0, 4):
                            b = take()
                            for h in range(h0, h0 + 4):
                                mk = matmul(b.t[:, (h - h0) * P:(h - h0 + 1) * P], Xt[:, h, :],
                                            T1[:, h, :], True, True, ms, m_xt, mark=True)
                            bs.append((b, mk))
                    m_xt2 = heads4(mm(lambda h: T1[:, h, :], lambda h: Xt[:, h, :]),
                                   lambda s, p, mk: TTn(Xt[:, s, :], Xt[:, s, :], p, ALU.subtract, mk),
                                   ms)
                    m_xt = m_xt2[-1]
                    if n < LEVELS - 1:
                        for i, (b, mk) in enumerate(bs):
                            s = slice(4 * i, 4 * i + 4)
                            m_X = TTn(X[:, s, :], X[:, s, :], b.t[:, :].rearrange("p (h w) -> p h w", h=4),
                                      ALU.subtract, mk)
                            b.free = [m_X]
                m_v = heads4(tr(lambda h: v[:, h, tk]),
                             lambda s, p, mk: A(vt[:, s, :], p, ACT.Copy, mk, dve.last()))[-1]
                if t == 1:
                    ms = heads4(mm(lambda h: k[:, h, tk], lambda h: st[:, h, :]),
                                lambda s, p, mk: TTn(T1[:, s, :], p, bl(egc[:, s], P), ALU.mult, mk, pe.last()),
                                m_st)
                    m_v = TTn(vt, vt, T1, ALU.subtract, ms[-1], m_v)
                m_v = TTn(vt, vt, bl(bec, P), ALU.mult, m_v)
                m_n = heads4(mm(lambda h: Xt[:, h, :], lambda h: vt[:, h, :]),
                             lambda s, p, mk: A(T1[:, s, :], p, ACT.Copy, mk, dve.last()), m_v, m_xt)[-1]
                if t == 0:
                    m_k = heads4(tr(lambda h: k[:, h, tk]),
                                 lambda s, p, mk: A(U[:, s, :], p, ACT.Copy, mk, dve.last()))[-1]
                    m = TTn(vt, T1, bl(ekc, P), ALU.mult, m_n, pe.last())
                    m_st = heads4(mm(lambda h: U[:, h, :], lambda h: vt[:, h, :]),
                                  lambda s, p, mk: A(st[:, s, :], p, ACT.Copy, mk), m_k, m)[-1]

                def outp(h, o, *after):
                    mk = matmul(o, T1[:, h, :], att[:, h, :], True, t == 0, *after, mark=t == 0)
                    if t == 1:
                        mk = matmul(o, st[:, h, :], qg[:, h, :], False, True, mark=True)
                    return mk
                heads4(outp, lambda s, p, mk: A(o_t[:, s, tk], p, ACT.Copy, mk), m_n, m_att, dve.last())
            fence()
            ar.at = conv_at
            rs, sq, zb = ar.get(T), ar.get(8, T), ar.get(8, T)
            spread = head_norm(o_t, sq, rs, 8, EPS, sel)
            for h in range(0, 8, 2):
                b, mk = spread(h)
                m = STT(o_t[:, h:h + 2, :], o_t[:, h:h + 2, :], V("c_g"), b.halves(), ALU.mult, ALU.mult, mk)
                b.free = [m]
            pair = Pair(g_hi, g_lo, 0)

            def z_out(two, b, mk):
                a = A(zb[:, two[0]:two[0] + 2, :], b.halves(), ACT.Silu, mk)
                b.free = [a]
                g = TTn(o_t[:, two[0]:two[0] + 2, :], o_t[:, two[0]:two[0] + 2, :],
                        zb[:, two[0]:two[0] + 2, :], ALU.mult, a, m)
                pair.split(o_t[:, two[0]:two[0] + 2, :], two[0], 2, g)
            project("cz", h_pair, KD, range(KD), z_out)
            down("cwo", pair, KD, add_scaled(1.0), sum_x)

        def per_layer(l):
            ar = Area(8192 + 2 * KD * T + T)
            pt, pv, sg = ar.get(2, T), ar.get(8, T), [ar.get(2, T) for _ in range(2)]

            def load():
                pool.wait(pe.last(), act.last(), dve.last())
                ready = load_table(pt, ins[f"p{l}"])
                h_pair.split(pt, 0, 2, ready, pe.last())

            def project_p():
                project(f"pp{l}", h_pair, 2, range(KD), to(pv))

            def finish(pair, last):
                def out(two, b, mk):
                    s = sg[(two[0] // 2) % 2]
                    for j, m in enumerate(two):
                        a = A(s[:, j, :], b.halves()[:, j, :], ACT.Sigmoid, mk, dve.last(),
                              bias=V(f"ple_b{l}", m))
                    b.free = [a]
                    x = x_t[:, two[0]:two[0] + 2, :]
                    r = TTn(s, s, pv[:, two[0]:two[0] + 2, :], ALU.mult, a)
                    r = TTn(x, x, s, ALU.add, r)
                    if not last:
                        pair_of_x(two, r)
                h_pair.ready.clear()
                project(f"pg{l}", pair, KD, range(KD), out)
            return load, project_p, finish

        plan = []
        for l in range(DEPTH):
            def first(l=l):
                if l == 0:
                    for k in range(0, KD, 2):
                        sum_squares([k, k + 1], None)
                    modulate(l, range(16))
                modulated(l, 0, 16)
                modulated_norm(col[:, 8:16], mod[:, 0:8])
                mixer_one(l)

            def second(l=l):
                modulated_norm(col[:, 16:24], mod[:, 24:32])
                conv_ffn(l, mod[:, 40:48], pair_of_x if l == DEPTH - 1 else sum_squares)
            plan += [first, second]
        x_pair_2 = Pair(g_hi, g_lo)
        for l in range(DEPTH):
            def ffn(l=l, f=1, i=0):
                load = project_p = finish = None
                if f == 2:
                    load, project_p, finish = per_layer(l)
                swiglu(f"f{f}g{l}", f"f{f}u{l}", f"f{f}d{l}", add_scaled(0.5), sum_x, load)
                layer_norm(l, i, h_pair if f == 1 else x_pair_2, ALPHA if f == 1 else 1.0, project_p)
                if f == 2:
                    finish(x_pair_2, l == DEPTH - 1)

            def mix(l=l):
                (mixer_ab if l == 0 else mixer_c)()
                layer_norm(l, 1, h_pair, ALPHA)
            plan += [ffn, mix, lambda l=l, ffn=ffn: ffn(l, 2, 2)]
        for step in plan[:stages]:
            step()
        flush()
        s_out = semaphore("output_written")
        sp.wait(dve.last(), act.last())
        sp.steps.append(("dma", lambda e: e.dma_start(out_ap, x_t[:, :, :]), s_out))
        sp.steps.append(("wait", s_out, 16))

        block = ctx.enter_context(nc.Block())

        @block.sync
        def _(e):
            sp.emit(e)

        @block.gpsimd
        def _(e):
            pool.emit(e)

        @block.scalar
        def _(e):
            act.emit(e)

        @block.vector
        def _(e):
            dve.emit(e)

        @block.tensor
        def _(e):
            pe.emit(e)


def pack_vectors(i):
    at, n = vector_columns()
    out = np.zeros((P, n), np.float32)

    def put(name, v):
        a, w = at[name]
        v = np.asarray(v).reshape(-1)
        if v.size < P:
            out[:v.size, a] = v
        else:
            out[:, a:a + w] = v.reshape(w, P).T
    for l in range(DEPTH):
        for name, src in (("b_ada", "b_ada"), ("norm1_g", "norm1_g"), ("norm2_g", "norm2_g"),
                          ("b_gla", "b_gla_a"), ("b_fox", "b_fox_f"), ("ret_g", "ret_norm_g"),
                          ("gla_g", "gla_norm_g"), ("q_g", "q_norm_g"), ("k_g", "k_norm_g"),
                          ("b_mg", "b_mg"), ("w_conv", "w_conv"), ("b_conv", "b_conv"),
                          ("ple_b", "ple_bg_2")):
            put(f"{name}{l}", i[src][l])
        for j in range(3):
            put(f"ln_g{l}{j}", i["ln_g_2"][l, j])
            put(f"ln_b{l}{j}", i["ln_b_2"][l, j])
    a, w = at["sinks"]
    out[:, a:a + w] = np.asarray(i["a_sinks_2"])[0]
    for name, src in (("b_conv_w", "b_conv_w_2"), ("b_conv_b", "b_conv_b_2"), ("b_ba", "b_ba_2"),
                      ("b_bx", "b_bx_2"), ("b_lam", "b_lam_2"), ("c_conv_w", "c_conv_w_2"),
                      ("c_a_log", "c_a_log_2"), ("c_dt", "c_dt_bias_2"), ("c_g", "c_norm_g_2")):
        put(name, i[src][0])
    return out


def matrices(i):
    out = {}
    splits = [512, 512, 512, 512, 256, 256, 512, 16, 512, 512, 512, 512, 4]
    edges = np.cumsum([0] + splits)
    for l in range(DEPTH):
        w = i["w_in"][l]
        parts = [w[:, a:b] for a, b in zip(edges[:-1], edges[1:])]
        for name, part in zip(("rq", "rk", "rv", "rg", "gq", "gk", "gv", "lr", "gg", "fq", "fk", "fv", "ff"), parts):
            out[f"{name}{l}"] = part
        small = np.zeros((D, P), np.float32)
        small[:, 0:4] = out[f"ff{l}"]
        small[:, 32:48] = out[f"lr{l}"]
        out[f"small{l}"] = small
        out[f"ada{l}"] = i["w_ada"][l]
        out[f"mg{l}"] = i["w_mg"][l]
        for n in range(3):
            out[f"br{l}_{n}"] = i["w_br"][l, n]
        out[f"wo{l}"], out[f"up{l}"], out[f"down{l}"] = i["w_o"][l], i["w_up"][l], i["w_down"][l]
        for f in (1, 2):
            out[f"f{f}g{l}"], out[f"f{f}u{l}"], out[f"f{f}d{l}"] = (
                i[f"ffn{f}_wg_2"][l], i[f"ffn{f}_wu_2"][l], i[f"ffn{f}_wd_2"][l])
        out[f"pg{l}"], out[f"pp{l}"] = i["ple_wg_2"][l], i["ple_wp_2"][l]
    w = i["ab_w_in_2"][0]
    heads = np.array([h for c in range(4) for h in (c, c + 4)])
    perm = (heads[:, None] * 64 + np.arange(64)[None, :]).reshape(-1)
    out["aq"], out["ak"], out["av"] = w[:, perm], w[:, 512:640], w[:, 640:768]
    out["abx"], out["abg"] = w[:, 768:1280], w[:, 1280:1792]
    out["abo"] = i["ab_w_out_2"][0][np.concatenate([perm, np.arange(512, 1024)])]
    w = i["c_w_in_2"][0]
    for n, name in enumerate(("cq", "ck", "cv", "cz")):
        out[name] = w[:, n * D:(n + 1) * D]
    small = np.zeros((D, P), np.float32)
    small[:, 0:8], small[:, 32:40] = w[:, 4096:4104], w[:, 4104:4112]
    out["cab"] = small
    out["cwo"] = i["c_w_out_2"][0]
    return out


def pack_stream(i):
    order, mats = weight_order(), matrices(i)
    out = np.zeros((len(order) // DMA_TILES, P, DMA_TILES, P), np.float32)
    for n, t in enumerate(order):
        if t is not None:
            name, k, m, split = t
            block = mats[name][k * P:(k + 1) * P, m * P:(m + 1) * P]
            out[n // DMA_TILES, :, n % DMA_TILES, :] = block if split else block.T
    return out


def lay(table, parts):
    out = np.zeros((P, widths(table)), np.float32)
    for name, (a, w) in columns(table).items():
        v = parts[name]
        out[:v.shape[0], a:a + w] = v.reshape(v.shape[0], w)
    return out


def tables():
    i, j, t = np.arange(P), np.arange(P), np.arange(T)
    eye = np.eye(P)
    base = lay(BASE, {"ident": eye, "mean_d": np.full((P, P), 1.0 / D), "pick": np.tile((np.arange(16) == 8) / P, (P, 1)),
                      "center": eye - 1.0 / P, "resets": np.tile((t % CH != 0) * 1.0, (P, 1))})
    half = P // 2
    freq = (10000.0 ** (-np.arange(half, dtype=np.float32) / half)).astype(np.float32)
    ang = (t.astype(np.float32)[None, :] * freq[:, None]).astype(np.float32)
    cos, sin = np.cos(ang), np.sin(ang)
    swap = np.zeros((P, P))
    swap[(i + half) % P, i] = 1.0
    decay = np.zeros((P, HEADS, 384))
    gla = np.zeros((P, 384))
    for jt in range(TT):
        key, qs = jt * P + i[:, None], t[None, jt * P:]
        seen = key // CH <= qs // CH
        at = slice(0, T) if jt == 0 else slice(T, 384)
        for h in range(HEADS):
            lg = np.log1p(-(2.0 ** (-5.0 - h)))
            decay[:, h, at] = np.where(seen, np.exp(np.abs(qs - key) * lg), 0.0)
        gla[:, at] = seen * 64 ** -0.5
    causal = np.concatenate([np.zeros((P, P)), np.where(i[:, None] >= j[None, :], 0.0, NEG)], 1)
    sel = np.zeros((P, C_HEADS, P))
    for h in range(C_HEADS):
        sel[h, h, :] = 1.0
    tab1 = lay(TAB1, {"swap": swap, "cos": np.concatenate([cos, cos]), "sin": np.concatenate([-sin, sin]),
                      "decay": decay, "gla": gla, "causal": causal, "sel": sel[:, :HEADS]})
    bias = np.zeros((P, A_HEADS, T))
    qi = P + i[:, None]
    kj = t[None, :]
    near = (kj // CH <= qi // CH) & (kj // CH >= qi // CH - 2)
    for h in range(A_HEADS):
        bias[:, h] = np.where(near, -(2.0 ** -(h + 1.0)) * np.abs(qi - kj), NEG)
    taba = lay(TABA, {"bias": bias})
    level = np.zeros((P, LEVELS, P))
    for n in range(LEVELS):
        s = 2 ** n
        level[:, n] = (j[None, :] // (2 * s) == i[:, None] // (2 * s)) & (i[:, None] % (2 * s) < s) & (
            j[None, :] % (2 * s) >= s)
    tabc = lay(TABC, {"causal_t": np.where(i[:, None] <= j[None, :], 0.0, NEG),
                      "strict": (i[:, None] < j[None, :]) * 1.0, "level": level, "sel_c": sel})
    return {"base": base, "tab1": tab1, "taba": taba, "tabc": tabc}


def arrays_of(i):
    out_c = np.ascontiguousarray(np.broadcast_to(i["c"].reshape(1, D), (P, D)))

    def blocks(x):
        f = x.shape[1]
        return np.ascontiguousarray(x.T.reshape(f // P, P, T).transpose(1, 0, 2))
    out = {"stream": pack_stream(i), "vec": pack_vectors(i), "xT": blocks(i["x"][0]), "c_row": out_c}
    out.update(tables())
    rgw = np.zeros((P, 8, P), np.float32)
    for n, name in enumerate(("b_wa_2", "b_wx_2")):
        w = i[name][0]
        for b in range(8):
            s = slice((b % 2) * 64, (b % 2) * 64 + 64)
            rgw[s, 4 * n + b // 2, s] = w[b]
    out["rgw"] = rgw
    for l in range(DEPTH):
        a = np.zeros((48, 256), np.float32)
        a[32:48] = i["w_gla_a2"][l]
        out[f"wa2_{l}"] = a
        out[f"p{l}"] = blocks(i["p_2"][l, 0])
    return out


def make(nc, arrays, stages=None):
    ins = {n: nc.dram_tensor(f"in_{n}", a.shape, F32, kind="ExternalInput").ap() for n, a in arrays.items()}
    out = nc.dram_tensor("out", (P, KD, T), F32, kind="ExternalOutput").ap()
    build(nc, ins, out, stages)


def kernel(**inputs):
    import concourse.bacc as _bacc
    from concourse.bass_utils import run_bass_kernel_spmd as _run
    arrays = arrays_of({n: np.asarray(a) for n, a in inputs.items()})
    nc = _bacc.Bacc("TRN2", target_bir_lowering=False, num_devices=1)
    make(nc, arrays)
    r = _run(nc, [{f"in_{n}": a for n, a in arrays.items()}], core_ids=[0])
    got = np.asarray(r.results[0]["out"])
    return np.ascontiguousarray(got.transpose(1, 0, 2).reshape(D, T).T).reshape(1, T, D)
```

```python
import math
from contextlib import ExitStack

import numpy as np
import concourse.bass as bass
from concourse import mybir

P = 128
T = 256
D = 1024
KD = D // P
DEPTH = 2
FF = 2816
KF = FF // P
HEADS = 4
CH = 64
TT = T // P
EPS = 1e-6
LN_EPS = 1e-5
ALPHA = (2.0 * DEPTH) ** 0.25
NEG = -1e30
A_HEADS = 8
C_HEADS = 8
LEVELS = 7

TILE = P * P
DMA_TILES = 16
CUT_TILES = 8
RAW_SLOTS = 3
CUT_SLOTS = 4
AHEAD = CUT_SLOTS - 2

F32 = mybir.dt.float32
F32R = mybir.dt.float32r
ACT = mybir.ActivationFunctionType
ALU = mybir.AluOpType
AX = mybir.AxisListType


ADA = 48
ADA_STEP = 2
ADA_BESIDE = ("rq", "rk", "rv", "rg", "gk", "gv", "gg", "fq", "fk", "fv")


def ada_beside(name):
    if name not in ADA_BESIDE:
        return range(0)
    at = 16 + ADA_STEP * ADA_BESIDE.index(name)
    return range(at, at + ADA_STEP)


def ada_in_gates(m):
    at = 16 + ADA_STEP * (len(ADA_BESIDE) + m // 4)
    return range(at, at + ADA_STEP) if m % 4 == 2 else range(0)


def ada_in_ffn(l, m):
    return range(m, m + 2) if l + 1 < DEPTH and m < 16 else range(0)


def sections():
    out = []
    for l in range(DEPTH):
        if l == 0:
            out.append((f"ada{l}", KD, range(0, 16), "raw"))
        for name, blocks, how in (("rq", 4, "k"), ("small", 1, "m"), ("rk", 4, "m"), ("rv", 4, "k"), ("rg", 4, "m"),
                                  ("gq", 2, "m"), ("gk", 2, "m"), ("gv", 4, "k"), ("gg", 4, "m"),
                                  ("fq", 4, "m"), ("fk", 4, "m"), ("fv", 4, "k")):
            out.append((f"{name}{l}", KD, range(blocks), how))
            out.append((f"ada{l}", KD, ada_beside(name), "raw"))
        for m in range(0, 24, 2):
            out.append((f"mg{l}", KD, range(m, m + 2), "m"))
            out.append((f"ada{l}", KD, ada_in_gates(m), "raw"))
        for m in range(0, KD, 2):
            for n in range(3):
                out.append((f"br{l}_{n}", 4, range(m, m + 2), "m"))
        out.append((f"wo{l}", KD, range(KD), "m"))
        for m in range(0, KF, 2):
            if m == 0:
                out.append((f"up_first{l}", KD, range(4), "k"))
            else:
                out.append((f"up{l}", KD, range(m, m + 2), "m"))
                out.append((f"up{l}", KD, range(KF + m, KF + m + 2), "m"))
            out.append((f"ada{l + 1}", KD, ada_in_ffn(l, m), "raw"))
        out.append((f"down{l}", KF, range(KD), "m"))
    for l in range(DEPTH):
        for f in (1, 2):
            out.append((f"f{f}_first{l}", KD, range(4), "k"))
            for m in range(2, KF, 2):
                out.append((f"f{f}g{l}", KD, range(m, m + 2), "m"))
                out.append((f"f{f}u{l}", KD, range(m, m + 2), "m"))
            out.append((f"f{f}d{l}", KF, range(KD), "m"))
            if f == 1 and l == 0:
                out.append(("aq", KD, range(4), "k"))
                out.append(("ak", KD, range(1), "m"))
                out.append(("av", KD, range(1), "k"))
                out.append(("abx", KD, range(4), "m"))
                out.append(("abg", KD, range(4), "m"))
                out.append(("abo", KD, range(KD), "m"))
            if f == 1 and l == 1:
                out.append(("cq", KD, range(4), "k"))
                out.append(("cab", KD, range(1), "m"))
                for n, m in (("ck", 0), ("cv", 0), ("cq", 4), ("ck", 4), ("cv", 4)):
                    out.append((n, KD, range(m, m + 4), "m"))
                out.append(("cz", KD, range(KD), "m"))
                out.append(("cwo", KD, range(KD), "m"))
        out.append((f"pp{l}", 2, range(KD), "m"))
        out.append((f"pg{l}", KD, range(4), "k"))
        out.append((f"pg{l}", KD, range(4, KD), "m"))
    return [x for x in out if len(x[2])]


def weight_order():
    order, raw = [], None
    for name, nk, ms, how in sections():
        if raw is not None and raw != (how == "raw"):
            order += [None] * (-len(order) % DMA_TILES)
        raw = how == "raw"
        if how == "k":
            order += [(name, k, m, True) for k in range(nk) for m in ms]
        else:
            order += [(name, k, m, not raw) for m in ms for k in range(nk)]
    return order + [None] * (-len(order) % DMA_TILES)


def vector_columns():
    sizes = []
    for l in range(DEPTH):
        sizes += [(f"b_ada{l}", 48), (f"norm1_g{l}", KD), (f"norm2_g{l}", KD), (f"b_gla{l}", 2),
                  (f"b_fox{l}", 1), (f"ret_g{l}", 4), (f"gla_g{l}", 1), (f"q_g{l}", 1),
                  (f"k_g{l}", 1), (f"b_mg{l}", 24), (f"w_conv{l}", 3 * KF), (f"b_conv{l}", KF),
                  (f"ple_b{l}", KD)]
        for i in range(3):
            sizes += [(f"ln_g{l}{i}", KD), (f"ln_b{l}{i}", KD)]
    sizes += [("sinks", A_HEADS), ("b_conv_w", 16), ("b_conv_b", 4), ("b_ba", 4), ("b_bx", 4),
              ("b_lam", 4), ("c_conv_w", 4 * 24), ("c_a_log", 1), ("c_dt", 1), ("c_g", 1)]
    out, at = {}, 0
    for n, s in sizes:
        out[n] = (at, s)
        at += s
    return out, at


BASE = [("ident", P), ("mean_d", P), ("pick", 16), ("center", P), ("resets", T)]
TAB1 = [("swap", P), ("cos", T), ("sin", T), ("decay", HEADS * 384), ("gla", 384), ("causal", T),
        ("sel", HEADS * P)]
TABA = [("bias", A_HEADS * T)]
TABC = [("causal_t", P), ("strict", P), ("level", LEVELS * P), ("sel_c", C_HEADS * P)]


def widths(table):
    return sum(w for _, w in table)


def columns(table):
    out, at = {}, 0
    for n, w in table:
        out[n] = (at, w)
        at += w
    return out


class Engine:

    def __init__(self, sem):
        self.sem, self.count, self.steps, self.passed = sem, 0, [], {}

    def wait(self, *marks):
        for mark in marks:
            if mark is None:
                continue
            if isinstance(mark, list):
                self.wait(*mark)
            elif self.passed.get(id(mark[0]), 0) < mark[1]:
                self.passed[id(mark[0])] = mark[1]
                self.steps.append(("wait", mark[0], mark[1]))

    def do(self, what, *after, mark=True):
        self.wait(*after)
        self.steps.append(("do", what, self.sem if mark else None))
        if mark:
            self.count += 1
            return (self.sem, self.count)
        return None

    def last(self):
        return (self.sem, self.count) if self.count else None

    def emit(self, eng):
        for kind, a, b in self.steps:
            if kind == "wait":
                eng.wait_ge(a, b)
            elif kind == "dma":
                a(eng).then_inc(b, 16)
            elif b is None:
                a(eng)
            else:
                a(eng).then_inc(b, 1)


def build(nc, ins, out_ap, stages):
    order = weight_order()
    vec_at, n_vec = vector_columns()
    ctx = ExitStack()
    with ctx:
        def sb(name, shape, dt=F32):
            return ctx.enter_context(nc.sbuf_tensor(name, shape, dt))

        def semaphore(name):
            return ctx.enter_context(nc.semaphore(name))

        pe, act, dve, pool, sp = (Engine(semaphore(f"{n}_done")) for n in ("pe", "act", "dve", "pool", "sp"))

        x_t = sb("x_t", [P, KD, T])
        h_hi = sb("h_hi", [P, KD, T], F32R)
        h_lo = sb("h_lo", [P, KD, T], F32R)
        g_hi = sb("g_hi", [P, KF, T], F32R)
        g_lo = sb("g_lo", [P, KF, T], F32R)
        raw = [sb(f"raw{i}", [P, DMA_TILES, P]) for i in range(RAW_SLOTS)]
        cut_hi = [sb(f"cut_hi{i}", [P, CUT_TILES, P], F32R) for i in range(CUT_SLOTS)]
        cut_lo = [sb(f"cut_lo{i}", [P, CUT_TILES, P], F32R) for i in range(CUT_SLOTS)]
        vec = sb("vec", [P, n_vec])
        base = sb("base", [P, widths(BASE)])
        mods = [sb(f"mod{l}", [P, ADA]) for l in range(2)]
        col = sb("col", [P, 64])
        WORK = 19900
        work = sb("work", [P, WORK])
        psum = [ctx.enter_context(nc.psum_tensor(f"psum{i}", [P, 512], F32)) for i in range(8)]

        base_at = columns(BASE)

        def B(name):
            a, w = base_at[name]
            return base[:, a:a + w]

        def V(name, i=0, n=1, rows=P):
            a, _ = vec_at[name]
            return vec[0:rows, a + i:a + i + n]

        class Bank:
            def __init__(self, t):
                self.t, self.free = t, []

            def halves(self):
                return self.t[:, :].rearrange("p (a t) -> p a t", a=2)

        banks = [Bank(t) for t in psum]
        turn = [0]

        def take():
            b = banks[turn[0] % len(banks)]
            turn[0] += 1
            marks, b.free = b.free, []
            pe.wait(marks)
            return b

        raw_ready = [semaphore(f"raw_ready{i}") for i in range(RAW_SLOTS)]
        n_loads = len(order) // DMA_TILES
        load_free = [None] * n_loads
        cut_mark = {}
        cut_free = {}
        state = {"loads": 0, "cuts": 0, "pos": 0}
        cuts_per_load = DMA_TILES // CUT_TILES
        stream = ins["stream"]

        def start_loads():
            while state["loads"] < n_loads:
                s = state["loads"]
                if s >= RAW_SLOTS:
                    if load_free[s - RAW_SLOTS] is None:
                        break
                    sp.wait(load_free[s - RAW_SLOTS])
                sp.steps.append(("dma", lambda e, s=s: e.dma_start(
                    raw[s % RAW_SLOTS][:, :, :], stream[s]), raw_ready[s % RAW_SLOTS]))
                state["loads"] += 1

        def load_mark(s):
            return (raw_ready[s % RAW_SLOTS], 16 * (s // RAW_SLOTS + 1))

        split_groups = [g for g in range(n_loads * cuts_per_load)
                        if any(t is not None and t[3] for t in order[g * CUT_TILES:(g + 1) * CUT_TILES])]
        place = {g: n for n, g in enumerate(split_groups)}

        def cut(n):
            s, half = divmod(split_groups[n], cuts_per_load)
            src = raw[s % RAW_SLOTS][:, half * CUT_TILES:(half + 1) * CUT_TILES, :]
            hi, lo = cut_hi[n % CUT_SLOTS], cut_lo[n % CUT_SLOTS]
            m = act.do(lambda e: e.activation(hi[:, :, :], src, ACT.Copy),
                       load_mark(s), cut_free.get(n - CUT_SLOTS))
            cut_mark[n] = dve.do(lambda e: e.tensor_tensor(
                lo[:, :, :], src, hi[:, :, :].bitcast(F32), ALU.subtract), m)
            if half == cuts_per_load - 1 or place.get(split_groups[n] + 1) is None:
                load_free[s] = cut_mark[n]
                start_loads()

        def cut_upto(n, need):
            while state["cuts"] <= min(n, len(split_groups) - 1):
                c = state["cuts"]
                if c > need and split_groups[c] // cuts_per_load >= state["loads"]:
                    break
                cut(c)
                state["cuts"] += 1

        class Weight:
            pass

        def weight(name, k, m, n=1):
            p = state["pos"]
            while order[p] is None:
                p += 1
            assert order[p][:3] == (name, k, m), (order[p], name, k, m)
            w = Weight()
            g = p // CUT_TILES
            s = p // DMA_TILES
            w.split = order[p][3]
            i = p % CUT_TILES
            w.load = s
            if w.split:
                w.group = place[g]
                cut_upto(w.group + AHEAD, w.group)
                w.hi = cut_hi[w.group % CUT_SLOTS][:, i:i + n, :].rearrange("p a b -> p (a b)")
                w.lo = cut_lo[w.group % CUT_SLOTS][:, i:i + n, :].rearrange("p a b -> p (a b)")
                w.ready = cut_mark[w.group]
            else:
                i = p % DMA_TILES
                w.raw = raw[s % RAW_SLOTS][:, i:i + n, :].rearrange("p a b -> p (a b)")
                w.ready = load_mark(s)
            nxt = p + n
            while nxt < len(order) and order[nxt] is None:
                nxt += 1
            w.ends_group = nxt // CUT_TILES != g
            w.ends_load = nxt // DMA_TILES != s
            state["pos"] = p + n
            return w

        def used(w, mark):
            if w.split and w.ends_group:
                cut_free[w.group] = mark
            if not w.split and w.ends_load:
                load_free[w.load] = mark
                start_loads()

        def matmul(out, lhsT, rhs, start, stop, *after, mark=False):
            return pe.do(lambda e: e.matmul(out, lhsT, rhs, start=start, stop=stop), *after, mark=mark)

        class Pair:

            def __init__(self, hi, lo, first=0):
                self.hi, self.lo, self.first, self.ready = hi, lo, first, {}

            def part(self, lo, k, a=0, b=T):
                t = self.lo if lo else self.hi
                return t[:, self.first + k, a:b]

            def split(self, value, k, n, *after):
                f = self.first + k
                hi, lo = self.hi[:, f:f + n, :], self.lo[:, f:f + n, :]
                m = A(hi, value, ACT.Copy, *after)
                m = TTn(lo, value, hi.bitcast(F32), ALU.subtract, m)
                for i in range(k, k + n):
                    self.ready[i] = m
                return m

        h_pair = Pair(h_hi, h_lo)

        def three(out, w, pair, k, start, stop, swap):
            parts = [(w.hi, 0), (w.hi, 1), (w.lo, 0)]
            for i, (wt, lo) in enumerate(parts):
                s, e_ = start and i == 0, stop and i == 2
                if swap is None:
                    yield wt, pair.part(lo, k), out, s, e_
                else:
                    yield pair.part(lo, k, swap * P, (swap + 1) * P), wt, out, s, e_

        late = []

        def flush(keep=0):
            while len(late) > keep:
                late.pop(0)()

        def project(sec, pair, nk, ms, evacuate):
            ms = list(ms)
            for i in range(0, len(ms), 2):
                two = ms[i:i + 2]
                b = take()
                for j, m in enumerate(two):
                    out = b.halves()[:, j, :]
                    for k in range(nk):
                        if k not in pair.ready:
                            flush()
                        w = weight(sec, k, m)
                        steps = list(three(out, w, pair, k, k == 0, k == nk - 1, None))
                        for n, (l, r, o, s, e_) in enumerate(steps):
                            end = n == 2 and (k == nk - 1 or w.ends_group)
                            mk = matmul(o, l, r, s, e_, w.ready, pair.ready[k], mark=end)
                        if mk is not None:
                            used(w, mk)
                flush()
                late.append(lambda two=two, b=b, mk=mk: evacuate(two, b, mk))

        def project_early(sec, pair, *evacuate):
            bs = [take() for _ in range(2)]
            flush()
            for k in range(KD):
                for m in range(4):
                    out = bs[m // 2].halves()[:, m % 2, :]
                    w = weight(sec, k, m)
                    steps = list(three(out, w, pair, k, k == 0 and m % 2 == 0,
                                       k == KD - 1 and m % 2 == 1, None))
                    for n, (l, r, o, s, e_) in enumerate(steps):
                        end = n == 2 and (k == KD - 1 or w.ends_group)
                        mk = matmul(o, l, r, s, e_, w.ready, pair.ready[k], mark=end)
                    if mk is not None:
                        used(w, mk)
                    if k == KD - 1:
                        bs[m // 2].done = mk
            for i, b in enumerate(bs):
                late.append(lambda i=i, b=b, mk=b.done: evacuate[i]([2 * i, 2 * i + 1], b, mk))

        def project_tokens(sec, pair, n_cols, evacuate):
            bs = [take() for _ in range(TT)]
            for k in range(KD):
                w = weight(sec, k, 0, n_cols // P)
                for t in range(TT):
                    steps = list(three(bs[t].t[:, 0:n_cols], w, pair, k, k == 0, k == KD - 1, t))
                    for n, (l, r, o, s, e_) in enumerate(steps):
                        mk = matmul(o, l, r, s, e_, w.ready, pair.ready[k],
                                    mark=n == 2 and (k == KD - 1 or t == TT - 1))
                    if k == KD - 1:
                        bs[t].done = mk
                used(w, mk)
            flush()
            for t in range(TT):
                late.append(lambda t=t: evacuate(t, bs[t], bs[t].done))

        def fence():
            flush()
            marks = [e.last() for e in (pe, act, dve, pool)]
            for e in (act, dve, pool):
                e.wait(*marks)

        class Area:
            def __init__(self, at=0):
                self.at = at

            def get(self, *shape):
                n = math.prod(shape)
                assert self.at + n <= WORK, (self.at, n)
                a = work[:, self.at:self.at + n]
                self.at += n
                if len(shape) == 2:
                    a = a.rearrange("p (a b) -> p a b", a=shape[0])
                if len(shape) == 3:
                    a = a.rearrange("p (a b c) -> p a b c", a=shape[0], b=shape[1])
                return a

        s_in = semaphore("inputs_ready")
        s_tab = semaphore("tables_ready")
        n_tab = [0]

        def load_in(dst, src):
            pool.steps.append(("dma", lambda e: e.dma_start(dst, src), s_in))

        c_row = work[:, WORK - D:WORK]
        s_c, s_x = semaphore("c_ready"), semaphore("x_ready")
        sp.steps.append(("dma", lambda e: e.dma_start(c_row, ins["c_row"]), s_c))
        load_in(vec[:, :], ins["vec"])
        load_in(base[:, :], ins["base"])
        start_loads()
        pool.steps.append(("dma", lambda e: e.dma_start(x_t[:, :, :], ins["xT"]), s_x))

        def load_table(dst, src):
            n_tab[0] += 16
            pool.steps.append(("dma", lambda e: e.dma_start(dst, src), s_tab))
            return (s_tab, n_tab[0])

        before = {}

        def behind(engine, what, *after):
            before[engine.sem.name] = m = engine.do(what, before.get(engine.sem.name), *after)
            return m

        def A(out, in_, f, *after, bias=0.0, scale=1.0):
            return behind(act, lambda e: e.activation(out, in_, f, bias=bias, scale=scale), *after)

        def TTn(out, a, b, op, *after):
            return behind(dve, lambda e: e.tensor_tensor(out, a, b, op), *after)

        def TS(out, a, s1, op0, *after, s2=None, op1=None):
            if op1 is None:
                return behind(dve, lambda e: e.tensor_scalar(out, a, s1, None, op0), *after)
            return behind(dve, lambda e: e.tensor_scalar(out, a, s1, s2, op0, op1), *after)

        def STT(out, a, s, b, op0, op1, *after):
            return behind(dve, lambda e: e.scalar_tensor_tensor(out, a, s, b, op0, op1), *after)

        def RED(out, in_, op, *after):
            return behind(dve, lambda e: e.tensor_reduce(out, in_, AX.X, op), *after)

        def RCP(out, in_, *after):
            return behind(dve, lambda e: e.reciprocal(out, in_), *after)

        def SCAN(out, a, b, *after):
            return behind(dve, lambda e: e.tensor_tensor_scan(out, a, b, 0.0, ALU.mult, ALU.add), *after)

        def SET(out, value, *after):
            return behind(dve, lambda e: e.memset(out, value), *after)

        eps_col = {}

        def const_col(value):
            if value not in eps_col:
                i = 60 + len(eps_col)
                eps_col[value] = (col[:, i:i + 1], SET(col[:, i:i + 1], value))
            return eps_col[value]

        for v in (EPS, LN_EPS, 1.0):
            const_col(v)
        act.wait(dve.last())

        def bc(ap, n):
            p, w = ap.shape
            return ap.unsqueeze(1).to_broadcast([p, n, w])

        def bl(ap, n):
            p, w = ap.shape
            return ap.unsqueeze(2).to_broadcast([p, w, n])

        stat = work[:, WORK - 2048:WORK - 1536].rearrange("p (a t) -> p a t", a=2)
        stat_sq = work[:, WORK - 1536:WORK - 1024].rearrange("p (a t) -> p a t", a=2)

        def sum_x(two, mark):
            x = x_t[:, two[0]:two[0] + 2, :]
            if two[0] == 0:
                TS(stat, x, 1.0, ALU.mult, mark)
            else:
                TTn(stat, stat, x, ALU.add, mark)

        def sum_squares(two, mark):
            x = x_t[:, two[0]:two[0] + 2, :]
            if two[0] == 0:
                A(stat, x, ACT.Square, mark, dve.last(), pe.last())
            else:
                m = A(stat_sq, x, ACT.Square, mark, dve.last())
                TTn(stat, stat, stat_sq, ALU.add, m)

        def pair_of_x(two, mark):
            x = x_t[:, two[0]:two[0] + 2, :]
            h_pair.split(x, two[0], 2, mark, pe.last())
            A(x, x, ACT.Copy, dve.last(), scale=ALPHA)

        def mean_of_stat():
            m = TTn(stat[:, 0, :], stat[:, 0, :], stat[:, 1, :], ALU.add, act.last())
            b = take()
            mk = matmul(b.t[:, 0:T], B("mean_d"), stat[:, 0, :], True, True, m, mark=True)
            return b, mk

        def inverse_root(b, out, mk, eps, meanwhile=None):
            m = A(out, b.t[:, 0:T], ACT.Sqrt, mk, bias=const_col(eps)[0])
            b.free = [m]
            if meanwhile is not None:
                meanwhile()
            return RCP(out, out, m)

        def norm_root(meanwhile=None):
            b, mk = mean_of_stat()
            return inverse_root(b, Area(8192).get(T), mk, EPS, meanwhile=meanwhile)

        def modulated_norm(gain, shift, r=None):
            fence()
            ar = Area(8192)
            rs, t1 = ar.get(T), ar.get(KD, T)
            if r is None:
                r = norm_root()
            for k in range(KD):
                m = STT(t1[:, k, :], x_t[:, k, :], gain[:, k:k + 1], rs, ALU.mult, ALU.mult, r)
                m = A(h_hi[:, k, :], t1[:, k, :], ACT.Identity, m, bias=shift[:, k:k + 1])
                h_pair.ready[k] = STT(h_lo[:, k, :], t1[:, k, :], shift[:, k:k + 1],
                                      h_hi[:, k, :].bitcast(F32), ALU.add, ALU.subtract, m)

        def layer_norm(l, i, pair, factor, meanwhile=None):
            flush()
            ar = Area(8192)
            xc, sq, rs = ar.get(KD, T), ar.get(KD, T), ar.get(T)
            b, mk = mean_of_stat()
            if meanwhile is not None:
                meanwhile()
            v = take()
            for k in range(0, KD, 2):
                m = TTn(xc[:, k:k + 2, :], x_t[:, k:k + 2, :], bc(b.t[:, 0:T], 2), ALU.subtract, mk,
                        act.last())
                sm = A(sq[:, k:k + 2, :], xc[:, k:k + 2, :], ACT.Square, m)
                for j in range(k, k + 2):
                    mv = matmul(v.t[:, 0:T], B("mean_d"), sq[:, j, :], j == 0, j == KD - 1, sm, mark=True)
            b.free = [m]
            flush()
            r = inverse_root(v, rs, mv, LN_EPS)
            gain, shift = (lambda k: V(f"ln_g{l}{i}", k)), (lambda k: V(f"ln_b{l}{i}", k))
            for k in range(KD):
                m = STT(xc[:, k, :], xc[:, k, :], gain(k), rs, ALU.mult, ALU.mult, r)
                hi, lo = pair.hi[:, pair.first + k, :], pair.lo[:, pair.first + k, :]
                m = A(hi, xc[:, k, :], ACT.Identity, m, pe.last(), bias=shift(k))
                pair.ready[k] = STT(lo, xc[:, k, :], shift(k), hi.bitcast(F32), ALU.add,
                                    ALU.subtract, m)
            if factor != 1.0:
                scaled = TS(col[:, 48:56], V(f"ln_b{l}{i}", 0, KD), factor, ALU.mult)
            for k in range(KD):
                bias = shift(k) if factor == 1.0 else col[:, 48 + k:49 + k]
                A(x_t[:, k, :], xc[:, k, :], ACT.Identity, dve.last(), bias=bias, scale=factor)

        def down(sec, pair, nk, residual, after):
            def evacuate(two, b, mk):
                m = residual(two, b, mk)
                b.free = [m]
                if after is not None:
                    after(two, m)
            if after is pair_of_x:
                h_pair.ready.clear()
            project(sec, pair, nk, range(KD), evacuate)

        def add_gated(gate):
            def residual(two, b, mk):
                for j, m in enumerate(two):
                    r = STT(x_t[:, m, :], b.halves()[:, j, :], gate[:, m:m + 1], x_t[:, m, :],
                            ALU.mult, ALU.add, mk)
                return r
            return residual

        def add_scaled(scale):
            def residual(two, b, mk):
                return STT(x_t[:, two[0]:two[0] + 2, :], b.halves(), scale,
                           x_t[:, two[0]:two[0] + 2, :], ALU.mult, ALU.add, mk, act.last())
            return residual

        def swiglu(sec_first, secg, secu, secd, residual, after, before_down=None):
            pair = Pair(g_hi, g_lo)
            ar = Area()
            silu = [ar.get(2, T) for _ in range(2)]
            val = [ar.get(2, T) for _ in range(2)]
            done = [None, None]
            for n, m in enumerate(range(0, KF, 2)):
                hold = {}

                def gate_out(two, b, mk, n=n, hold=hold):
                    hold["m"] = A(silu[n % 2], b.halves(), ACT.Silu, mk, done[n % 2])
                    b.free = [hold["m"]]

                def up_out(two, b, mk, n=n, m=m, hold=hold):
                    v = TTn(val[n % 2], silu[n % 2], b.halves(), ALU.mult, mk, hold["m"])
                    b.free = [v]
                    done[n % 2] = pair.split(val[n % 2], m, 2, v)

                if m == 0:
                    project_early(sec_first, h_pair, gate_out, up_out)
                else:
                    project(secg, h_pair, KD, range(m, m + 2), gate_out)
                    project(secu, h_pair, KD, range(m, m + 2), up_out)
            if before_down is not None:
                flush()
                before_down()
            down(secd, pair, KF, residual, after)

        def conv_ffn(l, gate, after):
            fence()
            pair = Pair(g_hi, g_lo)
            ar = Area()
            pad = [ar.get(2, T + 2) for _ in range(2)]
            con = [ar.get(2, T) for _ in range(2)]
            val = [ar.get(2, T) for _ in range(2)]
            zeroed = [SET(p[:, :, 0:2], 0.0) for p in pad]
            done = [zeroed[1], zeroed[1]]
            for n, m in enumerate(range(0, KF, 2)):
                hold = {}
                pd, cv, vl = pad[n % 2], con[n % 2], val[n % 2]

                def u_out(two, b, mk, n=n, pd=pd, cv=cv, hold=hold):
                    a = A(pd[:, :, 2:T + 2], b.halves(), ACT.Copy, mk, done[n % 2])
                    for j, f in enumerate(two):
                        b.free = [A(cv[:, j, :], b.halves()[:, j, :], ACT.Identity,
                                    bias=V(f"b_conv{l}", f), scale=V(f"w_conv{l}", 2 * KF + f))]
                    c = b.free[0]
                    for j, f in enumerate(two):
                        c1 = STT(cv[:, j, :], pd[:, j, 1:T + 1], V(f"w_conv{l}", KF + f), cv[:, j, :],
                                 ALU.mult, ALU.add, c)
                        c2 = STT(cv[:, j, :], pd[:, j, 0:T], V(f"w_conv{l}", f), cv[:, j, :],
                                 ALU.mult, ALU.add, c1)
                    hold["m"] = A(cv, cv, ACT.Silu, c2)

                def g_out(two, b, mk, n=n, m=m, cv=cv, vl=vl, hold=hold):
                    v = TTn(vl, cv, b.halves(), ALU.mult, mk, hold["m"])
                    b.free = [v]
                    done[n % 2] = pair.split(vl, m, 2, v)

                if m == 0:
                    project_early(f"up_first{l}", h_pair, u_out, g_out)
                else:
                    project(f"up{l}", h_pair, KD, range(m, m + 2), u_out)
                    project(f"up{l}", h_pair, KD, range(KF + m, KF + m + 2), g_out)
                if l + 1 < DEPTH:
                    modulate(l + 1, ada_in_ffn(l, m))
            if l + 1 < DEPTH:
                modulated(l + 1, 0, 16)
            down(f"down{l}", pair, KF, add_gated(gate), after)

        def to(out, f=ACT.Copy, bias=0.0, scale=1.0):
            def evacuate(two, b, mk):
                b.free = [A(out[:, two[0]:two[0] + len(two), :], b.halves()[:, 0:len(two), :], f, mk,
                            bias=bias, scale=scale)]
            return evacuate

        def to_tokens(out, n_cols):
            def evacuate(t, b, mk):
                b.free = [A(out[:, t, 0:n_cols], b.t[:, 0:n_cols], ACT.Copy, mk)]
            return evacuate

        finished = set()

        def weave(main, filler):
            for _ in main:
                finished.add(next(filler, None))

        def finish_filler(filler, name=None):
            while name is None or name not in finished:
                step = next(filler, "end")
                if step == "end":
                    break
                finished.add(step)
            flush()

        def run(steps):
            while True:
                try:
                    next(steps)
                except StopIteration as end:
                    return end.value

        def log_sigmoid(out, z, t1, t2, *after):
            m = A(t1, z, ACT.Abs, *after)
            m = A(t1, t1, ACT.Exp, m, scale=-1.0)
            m = A(t1, t1, ACT.Ln, m, bias=const_col(1.0)[0][0:t1.shape[0], :])
            m2 = TS(t2, z, 0.0, ALU.min)
            return TTn(out, t2, t1, ALU.subtract, m, m2)

        def head_norm(src, tmp, small, heads, eps, sel, *after, scale=1.0):
            m = A(tmp, src, ACT.Square, *after)
            yield
            b = take()
            for h in range(heads):
                mk = matmul(b.t[0:heads, 0:T], B("pick")[:, 8 - h:8 - h + heads], tmp[:, h, :],
                            h == 0, h == heads - 1, m, mark=True)
            rows = small[0:heads, 0:T]
            m = A(rows, b.t[0:heads, 0:T], ACT.Sqrt, mk, bias=const_col(eps)[0][0:heads, :], scale=scale)
            b.free = [m]
            m = RCP(rows, rows, m)
            yield

            def spread(h):
                b = take()
                for j in range(2):
                    mk = matmul(b.halves()[:, j, :], sel[0:heads, h + j, :], rows, True, True, m, mark=True)
                return b, mk
            return spread

        def values_times_scores(vals, sc, out, heads, *after):
            for h in range(heads):
                if h % 2 == 0:
                    b = take()
                o = b.halves()[:, h % 2, :]
                matmul(o, vals(h, 0), sc[:, h, 0:T], True, False, *after)
                mk = matmul(o[:, P:T], vals(h, 1), sc[:, h, T:T + P], False, True, mark=True)
                if h % 2 == 1:
                    out(h - 1, b, mk)

        def softmax_attention(heads, it, scores, bias, scale, S, E, small, sc, sink=None):
            W = P * (it + 1)
            per = 4 if it == 0 else 2
            Sv = S[:, 0:heads * W].rearrange("p (h w) -> p h w", h=heads)
            Ev = E[:, 0:heads * W].rearrange("p (h w) -> p h w", h=heads)
            for h0 in range(0, heads, per):
                b = take()
                v = b.t[:, :].rearrange("p (h w) -> p h w", h=per)
                for h in range(h0, h0 + per):
                    mk = scores(h, v[:, h - h0, :], W)
                m = STT(Sv[:, h0:h0 + per, :], v, scale, bias(h0, per, W), ALU.mult, ALU.add, mk,
                        act.last())
                b.free = [m]
                yield
            mx, sm, ex = (small[:, i * heads:(i + 1) * heads] for i in range(3))
            m = RED(mx, Sv, ALU.max, m)
            if sink is not None:
                m = TTn(mx, mx, sink, ALU.max, m)
                m1 = TTn(ex, sink, mx, ALU.subtract, m)
                mex = A(ex, ex, ACT.Exp, m1)
            m = TTn(Sv, Sv, bl(mx, W), ALU.subtract, m)
            m = A(Ev, Sv, ACT.Exp, m)
            yield
            m = RED(sm, Ev, ALU.add, m)
            if sink is not None:
                m = TTn(sm, sm, ex, ALU.add, m, mex)
            m = RCP(sm, sm, m)
            m = TTn(Ev, Ev, bl(sm, W), ALU.mult, m)
            yield
            pieces = [(h, jt) for jt in range(it + 1) for h in range(heads)]
            for i in range(0, len(pieces), 4):
                b = take()
                for n, (h, jt) in enumerate(pieces[i:i + 4]):
                    o, s_ = b.t[:, n * P:(n + 1) * P], Ev[:, h, jt * P:(jt + 1) * P]
                    mk = pe.do(lambda e, o=o, s_=s_: e.transpose(o, s_, B("ident")), m)
                h, jt = pieces[i]
                c0 = T if jt == 1 else it * P
                b.free = [A(sc[:, h:h + 4, c0:c0 + P], b.t[:, :].rearrange("p (h w) -> p h w", h=4),
                            ACT.Copy, mk)]
                yield

        c_ready = A(c_row, c_row, ACT.Silu, (s_c, 16))

        def modulate(l, blocks):
            mod = mods[l]
            for m in blocks:
                w = weight(f"ada{l}", 0, m, KD)
                mk = behind(dve, lambda e, w=w, m=m: e.tensor_tensor_reduce(
                    out=w.raw, in0=w.raw, in1=c_row, scale=1.0, scalar=0.0, op0=ALU.mult,
                    op1=ALU.add, accum_out=mod[:, m:m + 1]), w.ready, c_ready)
                used(w, mk)

        def modulated(l, first, n):
            mod = mods[l]
            m = TTn(mod[:, first:first + n], mod[:, first:first + n], V(f"b_ada{l}", first, n), ALU.add)
            if first == 0:
                STT(col[:, 8:16], mod[:, 8:16], 1.0, V(f"norm1_g{l}", 0, KD), ALU.add, ALU.mult, m)
            else:
                STT(col[:, 16:24], mod[:, 32:40], 1.0, V(f"norm2_g{l}", 0, KD), ALU.add, ALU.mult, m)

        def mixer_one(l):
            fence()
            ar = Area()
            tab = ar.get(widths(TAB1))
            ready = load_table(tab, ins["tab1"])
            at = columns(TAB1)

            def C(name):
                a, w = at[name]
                return tab[:, a:a + w]

            wa2 = ar.get(256)
            ready = load_table(wa2[0:48, :], ins[f"wa2_{l}"])
            r_at = ar.at
            rq, rk, rv, rg = ar.get(4, T), ar.get(4, T), ar.get(2, 512), ar.get(4, T)
            gq, gk, gv, gg = ar.get(2, T), ar.get(2, T), ar.get(2, 512), ar.get(4, T)
            kw_next = work[:, r_at:r_at + 3 * 512].rearrange("p (n a t) -> p n a t", n=3, a=2)
            kw = [gk] + [kw_next[:, n, :, :] for n in range(3)]
            r_end = ar.at
            fq, fk, fv = ar.get(4, T), ar.get(4, T), ar.get(2, 512)
            t_a, t_b, t_c = ar.get(1024), ar.get(1024), ar.get(1536)
            rows = ar.get(T)
            rows2 = ar.get(T)
            small = ar.get(64)
            ar2 = Area(r_at)
            gates = ar2.get(24, T)
            assert ar2.at <= r_end

            def four(x):
                return x[:, 0:1024].rearrange("p (h t) -> p h t", h=4)

            sel = C("sel").rearrange("p (h w) -> p h w", h=HEADS)
            branch = [Pair(g_hi, g_lo, 4 * n) for n in range(3)]
            sc = t_c.rearrange("p (h w) -> p h w", h=4)
            proj = lambda n, ms, ev: project(f"{n}{l}", h_pair, KD, ms, ev)

            def small_out(two, b, mk):
                b.free = [A(rows[0:48, :], b.t[0:48, 0:T], ACT.Copy, mk)]

            def pieces(name, blocks, out, f=ACT.Copy):
                for m in range(0, blocks, 2):
                    proj(name, range(m, m + 2), to(out, f))
                    if m + 2 < blocks:
                        yield
                modulate(l, ada_beside(name))
                yield name

            def token_pieces(name, out):
                project_tokens(f"{name}{l}", h_pair, 512, to_tokens(out, 512))
                modulate(l, ada_beside(name))
                yield name

            def filling():
                project_early(f"rq{l}", h_pair, to(rq), to(rq))
                modulate(l, ada_beside("rq"))
                proj("small", range(1), small_out)
                yield from pieces("rk", 4, rk)
                yield from token_pieces("rv", rv)
                yield from pieces("rg", 4, rg, ACT.Silu)
                yield from pieces("gq", 2, gq)
                yield from pieces("gk", 2, gk)
                yield from token_pieces("gv", gv)
                yield from pieces("gg", 4, gg, ACT.Silu)
                yield from pieces("fq", 4, fq)
                yield from pieces("fk", 4, fk)
                yield from token_pieces("fv", fv)
            finished.clear()
            filler = filling()
            finish_filler(filler, "rv")
            for e in (pe, act, dve):
                e.wait(ready)

            def finish(o, gate, gain, pair, src_mark, eps, bufs):
                tmp, rs = bufs
                flush()
                g_mark = act.last()
                spread = yield from head_norm(o, tmp, rs, 4, eps, sel, src_mark)
                for h in range(0, 4, 2):
                    b, mk = spread(h)
                    for j in range(2):
                        m = STT(o[:, h + j, :], o[:, h + j, :], gain(h + j), b.halves()[:, j, :],
                                ALU.mult, ALU.mult, mk)
                    b.free = [m]
                    m = TTn(o[:, h:h + 2, :], o[:, h:h + 2, :], gate[:, h:h + 2, :], ALU.mult, m, g_mark)
                    pair.split(o[:, h:h + 2, :], h, 2, m)

            def retention():
                t1 = four(t_a)
                for x, s in ((rq, 1.0), (rk, P ** -0.5)):
                    last = None
                    for h in range(0, 4, 2):
                        b = take()
                        mk = matmul(b.t[:, :], C("swap"), x[:, h:h + 2, :].rearrange("p a t -> p (a t)"),
                                    True, True, act.last(), mark=True)
                        m = STT(t1[:, h:h + 2, :], b.halves(), s, bc(C("sin"), 2), ALU.mult, ALU.mult, mk)
                        b.free = [m]
                        m = STT(x[:, h:h + 2, :], x[:, h:h + 2, :], s, bc(C("cos"), 2), ALU.mult, ALU.mult, m)
                        last = TTn(x[:, h:h + 2, :], x[:, h:h + 2, :], t1[:, h:h + 2, :], ALU.add, m)
                    yield
                dec = C("decay").rearrange("p (h w) -> p h w", h=4)
                for h in range(4):
                    b = take()
                    matmul(b.t[:, 0:T], rk[:, h, 0:P], rq[:, h, :], True, True, last)
                    mk = matmul(b.t[:, T:T + P], rk[:, h, P:T], rq[:, h, P:T], True, True, mark=True)
                    m = TTn(sc[:, h, :], b.t[:, 0:T + P], dec[:, h, :], ALU.mult, mk)
                    b.free = [m]
                    if h % 2:
                        yield
                o = four(t_a)
                marks = []

                def out(h, b, mk):
                    a = A(o[:, h:h + 2, :], b.halves(), ACT.Copy, mk, dve.last())
                    b.free = [a]
                    marks.append(a)
                values_times_scores(lambda h, t: rv[:, t, h * P:(h + 1) * P], sc, out, 4, m)
                yield
                for h in range(0, 4, 2):
                    b = take()
                    mk = matmul(b.t[:, :], B("center"), o[:, h:h + 2, :].rearrange("p a t -> p (a t)"),
                                True, True, marks[-1], mark=True)
                    a = A(o[:, h:h + 2, :], b.halves(), ACT.Copy, mk)
                    b.free = [a]
                yield
                yield from finish(o, rg, lambda h: V(f"ret_g{l}", h), branch[0], a, EPS,
                       (four(t_b), t_c))
                yield

            def gla():
                la = t_a[:, 0:512].rearrange("p (a t) -> p a t", a=2)
                t2 = t_a[:, 512:1024].rearrange("p (a t) -> p a t", a=2)
                t3 = t_b[:, 0:512].rearrange("p (a t) -> p a t", a=2)
                b = take()
                for j in range(2):
                    mk = matmul(b.halves()[:, j, :], wa2[32:48, j * P:(j + 1) * P], rows[32:48, :],
                                True, True, act.last(), mark=True)
                for j in range(2):
                    m = TS(la[:, j, :], b.halves()[:, j, :], V(f"b_gla{l}", j), ALU.add, mk, act.last())
                b.free = [m]
                m = log_sigmoid(la, la, t3, t2, m)
                m = TS(la, la, 1.0 / 16.0, ALU.mult, m)
                cum = t2
                for j in range(2):
                    m2 = SCAN(cum[:, j, :], B("resets"), la[:, j, :], m)
                ends = small[:, 0:8].rearrange("p (a n) -> p a n", a=2)
                for j in range(2):
                    c4 = cum[:, j, :].rearrange("p (n i) -> p n i", n=4)
                    m = TTn(t3[:, j, :].rearrange("p (n i) -> p n i", n=4),
                            c4[:, :, CH - 1:CH].to_broadcast([P, 4, CH]), c4, ALU.subtract, m2)
                    m = A(ends[:, j, :].unsqueeze(2), c4[:, :, CH - 1:CH], ACT.Exp, m)
                m = A(t3, t3, ACT.Exp, m)
                yield
                m = TTn(kw[0], gk, t3, ALU.mult, m)
                for n in range(1, 4):
                    for j in range(2):
                        m2 = TS(kw[n][:, j, 0:n * CH], kw[n - 1][:, j, 0:n * CH], ends[:, j, n:n + 1],
                                ALU.mult, m)
                        m3 = TS(kw[n][:, j, n * CH:T], kw[0][:, j, n * CH:T], 1.0, ALU.mult, m)
                    m = m3
                yield
                mask = C("gla")
                for h in range(4):
                    j, lo = h // 2, (h % 2) * 64
                    b = take()
                    for n in range(4):
                        q_ = gq[lo:lo + 64, j, n * CH:(n + 1) * CH]
                        mk = matmul(b.t[:, n * CH:(n + 1) * CH], kw[n][lo:lo + 64, j, 0:P], q_,
                                    True, True, m, mark=n < 2)
                        if n >= 2:
                            c = T + (n - 2) * CH
                            mk = matmul(b.t[:, c:c + CH], kw[n][lo:lo + 64, j, P:T], q_, True, True,
                                        mark=True)
                    s = TTn(sc[:, h, :], b.t[:, 0:T + P], mask, ALU.mult, mk, act.last())
                    b.free = [s]
                    if h % 2:
                        yield
                o = four(t_a)
                marks = []

                def out(h, b, mk):
                    a = A(o[:, h:h + 2, :], b.halves(), ACT.Copy, mk, dve.last())
                    b.free = [a]
                    marks.append(a)
                values_times_scores(lambda h, t: gv[:, t, h * P:(h + 1) * P], sc, out, 4, s)
                yield
                yield from finish(o, gg, lambda h: V(f"gla_g{l}", 0), branch[1], marks[-1], EPS,
                       (four(t_b), t_c))
                yield

            def fox():
                lf, t1 = t_a[0:4, 0:T], t_a[0:4, T:2 * T]
                m = TS(lf, rows[0:4, :], V(f"b_fox{l}", rows=4), ALU.add, act.last(), pe.last())
                m = log_sigmoid(lf, lf, t1, rows2[0:4, :], m)
                ones = t_b[0:4, 0:T]
                m = SET(ones, 1.0, m)
                cum, ncum = rows[0:4, :], rows2[0:4, :]
                m = SCAN(cum, ones, lf, m)
                c_m = TS(ncum, cum, -1.0, ALU.mult, m)
                yield
                for x, g, s in ((fq, f"q_g{l}", P ** -0.5), (fk, f"k_g{l}", 1.0)):
                    spread = yield from head_norm(x, four(t_b), t_c, 4, EPS, sel, dve.last())
                    for h in range(0, 4, 2):
                        b, mk = spread(h)
                        m = STT(x[:, h:h + 2, :], x[:, h:h + 2, :], V(g), b.halves(), ALU.mult, ALU.mult, mk)
                        b.free = [m]
                    if s != 1.0:
                        m = TS(x, x, s, ALU.mult, m)
                    yield
                fence()
                for it in range(TT):
                    def scores(h, o, W, it=it):
                        for c in range(0, W, P):
                            w_ = slice(c, c + P)
                            matmul(o[:, w_], fq[:, h, it * P:(it + 1) * P], fk[:, h, w_], True, False, m, c_m)
                            matmul(o[:, w_], sel[0:4, h, :], ncum[:, w_], False, False)
                            mk = matmul(o[:, w_], cum[:, it * P:(it + 1) * P], sel[0:4, h, :],
                                        False, True, mark=True)
                        return mk

                    def bias(h0, per, W):
                        return bc(C("causal")[:, T - W:T], per)
                    yield from softmax_attention(4, it, scores, bias, 1.0, t_a, t_b, small, sc)
                o = four(t_a)

                def out(h, b, mk):
                    a = A(o[:, h:h + 2, :], b.halves(), ACT.Copy, mk, dve.last())
                    b.free = [a]
                    branch[2].split(o[:, h:h + 2, :], h, 2, a)
                values_times_scores(lambda h, t: fv[:, t, h * P:(h + 1) * P], sc, out, 4, act.last())
                yield

            def gate_proj(free):
                def out(two, b, mk):
                    for j, m in enumerate(two):
                        a = A(gates[:, m, :], b.halves()[:, j, :], ACT.Sigmoid, mk, free,
                              bias=V(f"b_mg{l}", m))
                    b.free = [a]
                for m in range(0, 24, 2):
                    proj("mg", range(m, m + 2), out)
                    modulate(l, ada_in_gates(m))
                    yield

            weave(retention(), filler)
            finish_filler(filler, "gg")
            weave(gla(), filler)
            finish_filler(filler)
            filler = gate_proj([pe.last(), dve.last(), act.last()])
            weave(fox(), filler)
            finish_filler(filler)
            modulated(l, 16, 32)

            mixed = Pair(g_hi, g_lo, 12)
            for m in range(0, KD, 2):
                acc, t1 = four(t_a)[:, 0:2, :], four(t_a)[:, 2:4, :]
                for n in range(3):
                    def out(two, b, mk, n=n, m=m):
                        g = gates[:, n * KD + m:n * KD + m + 2, :]
                        dst = acc if n == 0 else t1
                        r = TTn(dst, b.halves(), g, ALU.mult, mk, dve.last(), act.last())
                        b.free = [r]
                        if n:
                            r = TTn(acc, acc, t1, ALU.add, r)
                        if n == 2:
                            mixed.split(acc, m, 2, r)
                    project(f"br{l}_{n}", branch[n], 4, range(m, m + 2), out)
            down(f"wo{l}", mixed, KD, add_gated(mods[l][:, 16:24]), sum_squares)

        def mixer_ab():
            fence()
            ar = Area()
            tab = ar.get(widths(TABA))
            ready = load_table(tab, ins["taba"])
            wg = ar.get(8, P)
            ready = load_table(wg, ins["rgw"])
            q, k, v = ar.get(4, T), ar.get(T), ar.get(2, P)
            bg = ar.get(4, T)
            pad = ar.get(4, T + 3)
            cv, ga, gi = ar.get(4, T), ar.get(4, T), ar.get(4, T)
            S, E, small, sc = ar.get(2048), ar.get(2048), ar.get(64), ar.get(8, 384)
            yb = Pair(g_hi, g_lo, 4)
            ya = Pair(g_hi, g_lo, 0)
            z = SET(pad[:, :, 0:3], 0.0)
            project_early("aq", h_pair, to(q), to(q))
            project("ak", h_pair, KD, range(1), to(k.unsqueeze(1)))
            project_tokens("av", h_pair, P, to_tokens(v, P))
            flush()
            for e in (pe, act, dve):
                e.wait(ready)
            bias_t = tab.rearrange("p (h w) -> p h w", h=A_HEADS)
            vq = act.last()

            def attention():
                for it in range(TT):
                    def scores(h, o, W, it=it):
                        lo = (h // 4) * 64
                        return matmul(o, q[lo:lo + 64, h % 4, it * P:(it + 1) * P], k[lo:lo + 64, 0:W],
                                      True, True, vq, mark=True)

                    def bias(h0, per, W):
                        return bias_t[:, h0:h0 + per, T - W:T]
                    yield from softmax_attention(8, it, scores, bias, 64 ** -0.5, S, E, small, sc,
                                                 sink=V("sinks", 0, 8))
                val = S[:, 0:1024].rearrange("p (h t) -> p h t", h=4)

                def out(h, b, mk):
                    lo = (h // 4) * 64
                    a = A(val[lo:lo + 64, h % 4:h % 4 + 2, :], b.halves()[lo:lo + 64, :, :], ACT.Copy, mk,
                          dve.last())
                    b.free = [a]
                values_times_scores(lambda h, t: v[:, t, :], sc, out, 8, act.last())
                for h in range(0, 4, 2):
                    ya.split(val[:, h:h + 2, :], h, 2, act.last())
                yield

            def rg_out(two, b, mk):
                b.free = [A(pad[:, two[0]:two[0] + 2, 3:T + 3], b.halves(), ACT.Copy, mk, z)]

            def recurrence():
                project("abx", h_pair, KD, range(2), rg_out)
                yield
                project("abx", h_pair, KD, range(2, 4), rg_out)
                yield
                project("abg", h_pair, KD, range(2), to(bg, ACT.Gelu_apprx_tanh))
                yield
                project("abg", h_pair, KD, range(2, 4), to(bg, ACT.Gelu_apprx_tanh))
                yield
                flush()
                for j in range(4):
                    m = TS(cv[:, j, :], pad[:, j, 0:T], V("b_conv_w", j), ALU.mult, act.last(),
                           s2=V("b_conv_b", j), op1=ALU.add)
                    for t in range(1, 4):
                        m = STT(cv[:, j, :], pad[:, j, t:t + T], V("b_conv_w", 4 * t + j), cv[:, j, :],
                                ALU.mult, ALU.add, m)
                for w0, dst, bias in ((0, ga, "b_ba"), (4, gi, "b_bx")):
                    for j in range(0, 4, 2):
                        b = take()
                        for i in range(2):
                            mk = matmul(b.halves()[:, i, :], wg[:, w0 + j + i, :], cv[:, j + i, :],
                                        True, True, m, mark=True)
                        for i in range(2):
                            a = A(dst[:, j + i, :], b.halves()[:, i, :], ACT.Sigmoid, mk,
                                  bias=V(bias, j + i))
                        b.free = [a]
                    yield
                y, s_, s2, acc = (col[:, 24 + 4 * i:28 + 4 * i] for i in range(4))
                lam = V("b_lam", 0, 4)
                m = A(y, lam, ACT.Abs, m)
                m = A(y, y, ACT.Exp, m, scale=-1.0)
                m = TS(s_, y, 2.0, ALU.add, m)
                m = RCP(s_, s_, m)
                m = TTn(s_, s_, y, ALU.mult, m)
                m = TTn(s2, s_, s_, ALU.mult, m)
                m = SET(acc, 2.0 / 19, m)
                for n in range(17, 0, -2):
                    m = TTn(acc, acc, s2, ALU.mult, m)
                    m = TS(acc, acc, 2.0 / n, ALU.add, m)
                m = TTn(acc, acc, s_, ALU.mult, m)
                m = TS(y, lam, -1.0, ALU.mult, m, s2=0.0, op1=ALU.max)
                m = TTn(acc, acc, y, ALU.add, m)
                m = TS(acc, acc, 8.0, ALU.mult, m)
                yield
                for j in range(4):
                    m2 = TS(ga[:, j, :], ga[:, j, :], acc[:, j:j + 1], ALU.mult, m, act.last())
                th = pad[:, :, 0:T]
                m3 = A(th, ga, ACT.Tanh, m2)
                m2 = A(ga, ga, ACT.Exp, m3, scale=-1.0)
                m = TTn(gi, gi, cv, ALU.mult, m3)
                m = TS(cv, th, 1.0, ALU.add, m)
                m = RCP(cv, cv, m)
                m = TTn(cv, cv, th, ALU.mult, m)
                m = A(cv, cv, ACT.Sqrt, m, scale=2.0)
                m = TTn(gi, gi, cv, ALU.mult, m)
                for j in range(4):
                    m4 = SCAN(cv[:, j, :], ga[:, j, :], gi[:, j, :], m, m2)
                m = TTn(cv, cv, bg, ALU.mult, m4)
                for h in range(0, 4, 2):
                    yb.split(cv[:, h:h + 2, :], h, 2, m)
                yield

            filler = recurrence()
            weave(attention(), filler)
            finish_filler(filler)
            both = Pair(g_hi, g_lo, 0)
            for i in range(4):
                both.ready[i], both.ready[4 + i] = ya.ready[i], yb.ready[i]
            down("abo", both, KD, add_scaled(1.0), sum_x)

        def mixer_c():
            fence()
            ar = Area()
            tab = ar.get(widths(TABC))
            ready = load_table(tab, ins["tabc"])
            at = columns(TABC)

            def C(name):
                a, w = at[name]
                return tab[:, a:a + w]

            q, k, v = (ar.get(8, T) for _ in range(3))
            rows = ar.get(4, T)
            cols = ar.get(TT, 24)
            buf = [ar.get(10 * 512) for _ in range(2)]
            z_part = ar.get(T)
            z_pair = Pair(g_hi, g_lo, 8)
            spare = buf[1]
            pad = [spare[:, i * 518:(i + 1) * 518].rearrange("p (a t) -> p a t", a=2) for i in range(2)]
            con = [spare[:, 1036 + i * 512:1548 + i * 512].rearrange("p (a t) -> p a t", a=2)
                   for i in range(2)]
            ekd, ones = spare[0:8, 2060:2060 + T], spare[0:8, 2060 + T:2060 + T + P]
            sel = C("sel_c").rearrange("p (h w) -> p h w", h=8)
            levels = C("level").rearrange("p (n w) -> p n w", n=LEVELS)
            zeroed = [SET(p[:, :, 0:3], 0.0) for p in pad][1]
            free = [zeroed, zeroed]
            h_mark = {}

            def small_out(two, b, mk):
                A(rows[0:8, 0, :], b.t[0:8, 0:T], ACT.Sigmoid, mk)
                e_ = A(rows[0:8, 1, :], b.t[32:40, 0:T], ACT.Copy)
                b.free = [e_]
                h_mark["rows"] = TS(rows[0:8, 1, :], rows[0:8, 1, :], V("c_dt", rows=8), ALU.add, e_)

            def conv_out(part, dst):
                def out(two, b, mk):
                    i = (two[0] // 2) % 2
                    pd, cn = pad[i], con[i]
                    a = A(pd[:, :, 3:T + 3], b.halves(), ACT.Copy, mk, free[i])
                    b.free = [a]
                    for j, f in enumerate(two):
                        c0 = part * 8 + f
                        m = A(cn[:, j, :], pd[:, j, 3:T + 3], ACT.Identity, a, scale=V("c_conv_w", 72 + c0))
                    for j, f in enumerate(two):
                        c0 = part * 8 + f
                        for t in range(2, -1, -1):
                            m = STT(cn[:, j, :], pd[:, j, t:t + T], V("c_conv_w", 24 * t + c0),
                                    cn[:, j, :], ALU.mult, ALU.add, m)
                    free[i] = A(dst[:, two[0]:two[0] + 2, :], cn, ACT.Silu, m)
                return out

            def z_out(two, b, mk):
                for j, m in enumerate(two):
                    a = A(z_part, b.halves()[:, j, :], ACT.Silu, mk, dve.last())
                    z_pair.split(z_part.unsqueeze(1), m, 1, a)
                b.free = [a]
            outs = {"cq": conv_out(0, q), "ck": conv_out(1, k), "cv": conv_out(2, v), "cz": z_out}

            def filling():
                for name, m0 in (("ck", 0), ("cv", 0), ("cq", 4), ("ck", 4), ("cv", 4), ("cz", 0), ("cz", 4)):
                    project(name, h_pair, KD, range(m0, m0 + 2), outs[name])
                    yield
                    project(name, h_pair, KD, range(m0 + 2, m0 + 4), outs[name])
                    yield name + str(m0)

            project_early("cq", h_pair, outs["cq"], outs["cq"])
            project("cab", h_pair, KD, range(1), small_out)
            finished.clear()
            filler = filling()
            next(filler)
            beta, gc, eg, ngc = (rows[0:8, i, :] for i in range(4))
            egc, bec, ekc = ([cols[:, t, 8 * i:8 * i + 8] for t in range(TT)] for i in range(3))

            def decays():
                a_, g_, t1 = gc, eg, ngc
                m = A(g_, a_, ACT.Abs, h_mark["rows"])
                m = A(g_, g_, ACT.Exp, m, scale=-1.0)
                m = A(g_, g_, ACT.Ln, m, bias=const_col(1.0)[0][0:8, :])
                m1 = A(col[0:8, 40:41], V("c_a_log", rows=8), ACT.Exp)
                yield
                m = TS(t1, a_, 0.0, ALU.max, m, m1)
                m = TTn(g_, g_, t1, ALU.add, m)
                m = TS(g_, g_, col[0:8, 40:41], ALU.mult, m, s2=-1.0, op1=ALU.mult)
                m = SET(ones, 1.0, m)
                for t in range(TT):
                    tk = slice(t * P, (t + 1) * P)
                    m = SCAN(gc[:, tk], ones, g_[:, tk], m)
                m_eg = A(eg, gc, ACT.Exp, m)
                h_mark["ngc"] = TS(ngc, gc, -1.0, ALU.mult, m)
                for t in range(TT):
                    tk = slice(t * P, (t + 1) * P)
                    m = TS(ekd[:, tk], gc[:, tk], gc[:, (t + 1) * P - 1:(t + 1) * P], ALU.subtract,
                           s2=-1.0, op1=ALU.mult)
                m = A(ekd, ekd, ACT.Exp, m)
                yield
                b = take()
                for t in range(TT):
                    for i, src in enumerate((eg, beta, ekd)):
                        o, s_ = b.t[:, 24 * t + 8 * i:24 * t + 8 * i + 8], src[:, t * P:(t + 1) * P]
                        mk = pe.do(lambda e, o=o, s_=s_: e.transpose(o, s_, B("ident")[0:8, 0:8]), m, m_eg)
                m = A(cols, b.t[:, 0:48].rearrange("p (a w) -> p a w", a=TT), ACT.Copy, mk)
                b.free = [m]
                h_mark["cols"] = m
                for e in (pe, act, dve):
                    e.wait(ready)
                yield

            def mm(lhsT, rhs):
                return lambda j, o, *after: matmul(o, lhsT(j), rhs(j), True, True, *after, mark=True)

            def tr(src):
                def fn(j, o, *after):
                    of = src(j)
                    return pe.do(lambda e: e.transpose(o, of, B("ident")), *after)
                return fn

            def four(fn, consume, *after):
                b = take()
                for j in range(4):
                    mk = fn(j, b.t[:, j * P:(j + 1) * P], *after)
                b.free = [consume(b.t[:, :].rearrange("p (h w) -> p h w", h=4), mk)]
                return b.free[0]

            pair = Pair(g_hi, g_lo, 0)

            def chain(half, buf):
                h0 = 4 * half
                hs = slice(h0, h0 + 4)
                kb, dec, att, U, X, Xt, T1, vt, qg, st = (
                    buf[:, i * 512:(i + 1) * 512].rearrange("p (h w) -> p h w", h=4) for i in range(10))
                sq, rs = buf[:, 0:4 * T].rearrange("p (h t) -> p h t", h=4), buf[:, 4 * T:5 * T]
                o_t = q
                for x, s, name in ((q, P ** -0.5, "cq"), (k, 1.0, "ck")):
                    if half == 0 and name == "ck":
                        finish_filler(filler, "ck0")
                    flush()
                    spread = yield from head_norm(x[:, hs, :], sq, rs, 4, EPS, sel, act.last(), dve.last(),
                                                  pe.last(), scale=float(P))
                    for j in range(0, 4, 2):
                        b, mk = spread(j)
                        xs = x[:, h0 + j:h0 + j + 2, :]
                        m_x = STT(xs, xs, s, b.halves(), ALU.mult, ALU.mult, mk)
                        b.free = [m_x]
                    yield
                if half == 0:
                    finish_filler(filler, "cv0")
                m_o = m_x
                for t in range(TT):
                    tk = slice(t * P, (t + 1) * P)

                    def column(c):
                        return bl(c[t][:, hs], P)
                    m_v = four(tr(lambda j: v[:, h0 + j, tk]), lambda p, mk: A(vt, p, ACT.Copy, mk, m_o),
                               act.last())
                    if t == 1:
                        m = four(mm(lambda j: k[:, h0 + j, tk], lambda j: st[:, j, :]),
                                 lambda p, mk: TTn(T1, p, column(egc), ALU.mult, mk), m_st)
                        m_v = TTn(vt, vt, T1, ALU.subtract, m, m_v)
                    m_v = TTn(vt, vt, column(bec), ALU.mult, m_v, h_mark["cols"])
                    m_kb = four(mm(lambda j: sel[0:8, h0 + j, :], lambda j: beta[:, tk]),
                                lambda p, mk: TTn(kb, k[:, hs, tk], p, ALU.mult, mk), m_x)

                    def diff(j, o, *after):
                        matmul(o, sel[0:8, h0 + j, :], gc[:, tk], True, False, *after)
                        return matmul(o, ngc[:, tk], sel[0:8, h0 + j, :], False, True, mark=True)
                    m = four(diff, lambda p, mk: TTn(dec, p, bc(C("causal_t"), 4), ALU.add, mk),
                             h_mark["ngc"])
                    m = A(dec, dec, ACT.Exp, m)
                    yield
                    four(mm(lambda j: k[:, h0 + j, tk], lambda j: q[:, h0 + j, tk]),
                         lambda p, mk: TTn(att, p, dec, ALU.mult, mk, m), m_kb)
                    m_s = TTn(dec, dec, bc(C("strict"), 4), ALU.mult)
                    m_u = four(mm(lambda j: k[:, h0 + j, tk], lambda j: kb[:, j, :]),
                               lambda p, mk: TTn(U, p, dec, ALU.mult, mk), m_kb)
                    if t == 1:
                        four(mm(lambda j: sel[0:8, h0 + j, :], lambda j: eg[:, tk]),
                             lambda p, mk: TTn(qg, q[:, hs, tk], p, ALU.mult, mk))
                    yield
                    Um = dec
                    m = TTn(Um, U, bc(levels[:, 0, :], 4), ALU.mult)
                    m_xt = TTn(Xt, bc(B("ident"), 4), Um, ALU.subtract)
                    m = TTn(Um, U, bc(levels[:, 1, :], 4), ALU.mult)
                    m_X = four(tr(lambda j: Xt[:, j, :]), lambda p, mk: A(X, p, ACT.Copy, mk), m_xt)
                    yield
                    for n in range(1, LEVELS):
                        m_t = four(mm(lambda j: Um[:, j, :], lambda j: X[:, j, :]),
                                   lambda p, mk: A(T1, p, ACT.Copy, mk), m, m_X, m_v)
                        if n < LEVELS - 1:
                            m = TTn(Um, U, bc(levels[:, n + 1, :], 4), ALU.mult, m_t)
                        yield
                        m_p = None
                        if n < LEVELS - 1:
                            b = take()
                            for j in range(4):
                                m_p = matmul(b.t[:, j * P:(j + 1) * P], Xt[:, j, :], T1[:, j, :],
                                             True, True, m_t, m_xt, mark=True)
                        m_xt = four(mm(lambda j: T1[:, j, :], lambda j: Xt[:, j, :]),
                                    lambda p, mk: TTn(Xt, Xt, p, ALU.subtract, mk), m_t, m_xt)
                        if m_p is not None:
                            m_X = TTn(X, X, b.t[:, :].rearrange("p (h w) -> p h w", h=4),
                                      ALU.subtract, m_p)
                            b.free = [m_X]
                        yield
                    m_n = four(mm(lambda j: Xt[:, j, :], lambda j: vt[:, j, :]),
                               lambda p, mk: A(T1, p, ACT.Copy, mk), m_v, m_xt)
                    yield
                    if t == 0:
                        m_k = four(tr(lambda j: k[:, h0 + j, tk]), lambda p, mk: A(U, p, ACT.Copy, mk, m_xt))
                        m = TTn(vt, T1, column(ekc), ALU.mult, m_n)
                        m_st = four(mm(lambda j: U[:, j, :], lambda j: vt[:, j, :]),
                                    lambda p, mk: A(st, p, ACT.Copy, mk), m_k, m)

                    def outp(j, o, *after):
                        mk = matmul(o, T1[:, j, :], att[:, j, :], True, t == 0, *after, mark=t == 0)
                        if t == 1:
                            mk = matmul(o, st[:, j, :], qg[:, j, :], False, True, mark=True)
                        return mk
                    m_o = four(outp, lambda p, mk: A(o_t[:, hs, tk], p, ACT.Copy, mk), m_n)
                    dve.wait(m_o)
                    yield
                spread = yield from head_norm(o_t[:, hs, :], sq, rs, 4, EPS, sel, m_o)
                finish_filler(filler, f"cz{h0}")
                for j in range(0, 4, 2):
                    b, mk = spread(j)
                    o = o_t[:, h0 + j:h0 + j + 2, :]
                    hi, lo = (g[:, 8 + h0 + j:10 + h0 + j, :].bitcast(F32) for g in (g_hi, g_lo))
                    z = sq[:, j:j + 2, :]
                    m = STT(o, o, V("c_g"), b.halves(), ALU.mult, ALU.mult, mk)
                    b.free = [m]
                    TTn(z, hi, lo, ALU.add)
                    m = TTn(o, o, z, ALU.mult)
                    pair.split(o, h0 + j, 2, m)
                yield

            chains = [chain(i, buf[i]) for i in range(2)]
            weave(decays(), filler)
            while "cv4" not in finished:
                next(chains[0], None)
                flush()
                finished.add(next(filler, None))
            flush()
            for _ in chains[1]:
                next(chains[0], None)
                flush()
            for _ in chains[0]:
                pass
            finish_filler(filler)
            down("cwo", pair, KD, add_scaled(1.0), sum_x)

        def per_layer(l):
            ar = Area(8192 + 2 * KD * T + T)
            pt, pv, sg = ar.get(2, T), ar.get(8, T), [ar.get(2, T) for _ in range(2)]

            def load():
                pool.wait(pe.last(), act.last(), dve.last())
                ready = load_table(pt, ins[f"p{l}"])
                h_pair.split(pt, 0, 2, ready, pe.last())

            def project_p():
                project(f"pp{l}", h_pair, 2, range(KD), to(pv))

            def finish(pair, last):
                def out(two, b, mk):
                    s = sg[(two[0] // 2) % 2]
                    for j, m in enumerate(two):
                        a = A(s[:, j, :], b.halves()[:, j, :], ACT.Sigmoid, mk, dve.last(),
                              bias=V(f"ple_b{l}", m))
                    b.free = [a]
                    x = x_t[:, two[0]:two[0] + 2, :]
                    r = TTn(s, s, pv[:, two[0]:two[0] + 2, :], ALU.mult, a)
                    r = TTn(x, x, s, ALU.add, r)
                    if not last:
                        pair_of_x(two, r)
                h_pair.ready.clear()
                project_early(f"pg{l}", pair, out, out)
                project(f"pg{l}", pair, KD, range(4, KD), out)
            return load, project_p, finish

        plan = []
        for l in range(DEPTH):
            def first(l=l):
                r = None
                if l == 0:
                    modulate(l, range(10))
                    for e in (pe, act, dve, pool):
                        e.wait((s_in, 32), (s_x, 16))
                    for k in range(0, KD, 2):
                        sum_squares([k, k + 1], None)
                    r = norm_root(lambda: modulate(l, range(10, 16)))
                    modulated(l, 0, 16)
                modulated_norm(col[:, 8:16], mods[l][:, 0:8], r)
                mixer_one(l)

            def second(l=l):
                modulated_norm(col[:, 16:24], mods[l][:, 24:32])
                conv_ffn(l, mods[l][:, 40:48], pair_of_x if l == DEPTH - 1 else sum_squares)
            plan += [first, second]
        x_pair_2 = Pair(g_hi, g_lo)
        for l in range(DEPTH):
            def ffn(l=l, f=1, i=0):
                load = project_p = finish = None
                if f == 2:
                    load, project_p, finish = per_layer(l)
                swiglu(f"f{f}_first{l}", f"f{f}g{l}", f"f{f}u{l}", f"f{f}d{l}", add_scaled(0.5), sum_x, load)
                layer_norm(l, i, h_pair if f == 1 else x_pair_2, ALPHA if f == 1 else 1.0, project_p)
                if f == 2:
                    finish(x_pair_2, l == DEPTH - 1)

            def mix(l=l):
                (mixer_ab if l == 0 else mixer_c)()
                layer_norm(l, 1, h_pair, ALPHA)
            plan += [ffn, mix, lambda l=l, ffn=ffn: ffn(l, 2, 2)]
        for step in plan[:stages]:
            step()
        flush()
        s_out = semaphore("output_written")
        sp.wait(dve.last(), act.last())
        sp.steps.append(("dma", lambda e: e.dma_start(out_ap, x_t[:, :, :]), s_out))
        sp.steps.append(("wait", s_out, 16))

        block = ctx.enter_context(nc.Block())

        @block.sync
        def _(e):
            sp.emit(e)

        @block.gpsimd
        def _(e):
            pool.emit(e)

        @block.scalar
        def _(e):
            act.emit(e)

        @block.vector
        def _(e):
            dve.emit(e)

        @block.tensor
        def _(e):
            pe.emit(e)


def pack_vectors(i):
    at, n = vector_columns()
    out = np.zeros((P, n), np.float32)

    def put(name, v):
        a, w = at[name]
        v = np.asarray(v).reshape(-1)
        if v.size < P:
            out[:v.size, a] = v
        else:
            out[:, a:a + w] = v.reshape(w, P).T
    for l in range(DEPTH):
        for name, src in (("b_ada", "b_ada"), ("norm1_g", "norm1_g"), ("norm2_g", "norm2_g"),
                          ("b_gla", "b_gla_a"), ("b_fox", "b_fox_f"), ("ret_g", "ret_norm_g"),
                          ("gla_g", "gla_norm_g"), ("q_g", "q_norm_g"), ("k_g", "k_norm_g"),
                          ("b_mg", "b_mg"), ("w_conv", "w_conv"), ("b_conv", "b_conv"),
                          ("ple_b", "ple_bg_2")):
            put(f"{name}{l}", i[src][l])
        for j in range(3):
            put(f"ln_g{l}{j}", i["ln_g_2"][l, j])
            put(f"ln_b{l}{j}", i["ln_b_2"][l, j])
    a, w = at["sinks"]
    out[:, a:a + w] = np.asarray(i["a_sinks_2"])[0]
    for name, src in (("b_conv_w", "b_conv_w_2"), ("b_conv_b", "b_conv_b_2"), ("b_ba", "b_ba_2"),
                      ("b_bx", "b_bx_2"), ("b_lam", "b_lam_2"), ("c_conv_w", "c_conv_w_2"),
                      ("c_a_log", "c_a_log_2"), ("c_dt", "c_dt_bias_2"), ("c_g", "c_norm_g_2")):
        put(name, i[src][0])
    return out


def matrices(i):
    out = {}
    splits = [512, 512, 512, 512, 256, 256, 512, 16, 512, 512, 512, 512, 4]
    edges = np.cumsum([0] + splits)
    def beside(a, b):
        return np.concatenate([a[:, :2 * P], b[:, :2 * P]], 1)
    for l in range(DEPTH):
        w = i["w_in"][l]
        parts = [w[:, a:b] for a, b in zip(edges[:-1], edges[1:])]
        for name, part in zip(("rq", "rk", "rv", "rg", "gq", "gk", "gv", "lr", "gg", "fq", "fk", "fv", "ff"), parts):
            out[f"{name}{l}"] = part
        small = np.zeros((D, P), np.float32)
        small[:, 0:4] = out[f"ff{l}"]
        small[:, 32:48] = out[f"lr{l}"]
        out[f"small{l}"] = small
        out[f"ada{l}"] = i["w_ada"][l]
        out[f"mg{l}"] = i["w_mg"][l]
        for n in range(3):
            out[f"br{l}_{n}"] = i["w_br"][l, n]
        out[f"wo{l}"], out[f"up{l}"], out[f"down{l}"] = i["w_o"][l], i["w_up"][l], i["w_down"][l]
        out[f"up_first{l}"] = beside(i["w_up"][l], i["w_up"][l][:, FF:])
        for f in (1, 2):
            out[f"f{f}g{l}"], out[f"f{f}u{l}"], out[f"f{f}d{l}"] = (
                i[f"ffn{f}_wg_2"][l], i[f"ffn{f}_wu_2"][l], i[f"ffn{f}_wd_2"][l])
            out[f"f{f}_first{l}"] = beside(i[f"ffn{f}_wg_2"][l], i[f"ffn{f}_wu_2"][l])
        out[f"pg{l}"], out[f"pp{l}"] = i["ple_wg_2"][l], i["ple_wp_2"][l]
    w = i["ab_w_in_2"][0]
    heads = np.array([h for c in range(4) for h in (c, c + 4)])
    perm = (heads[:, None] * 64 + np.arange(64)[None, :]).reshape(-1)
    out["aq"], out["ak"], out["av"] = w[:, perm], w[:, 512:640], w[:, 640:768]
    out["abx"], out["abg"] = w[:, 768:1280], w[:, 1280:1792]
    out["abo"] = i["ab_w_out_2"][0][np.concatenate([perm, np.arange(512, 1024)])]
    w = i["c_w_in_2"][0]
    for n, name in enumerate(("cq", "ck", "cv", "cz")):
        out[name] = w[:, n * D:(n + 1) * D]
    small = np.zeros((D, P), np.float32)
    small[:, 0:8], small[:, 32:40] = w[:, 4096:4104], w[:, 4104:4112]
    out["cab"] = small
    out["cwo"] = i["c_w_out_2"][0]
    return out


def pack_stream(i):
    order, mats = weight_order(), matrices(i)
    out = np.zeros((len(order) // DMA_TILES, P, DMA_TILES, P), np.float32)
    for n, t in enumerate(order):
        if t is not None:
            name, k, m, split = t
            block = mats[name][k * P:(k + 1) * P, m * P:(m + 1) * P]
            out[n // DMA_TILES, :, n % DMA_TILES, :] = block if split else block.T
    return out


def lay(table, parts):
    out = np.zeros((P, widths(table)), np.float32)
    for name, (a, w) in columns(table).items():
        v = parts[name]
        out[:v.shape[0], a:a + w] = v.reshape(v.shape[0], w)
    return out


def tables():
    i, j, t = np.arange(P), np.arange(P), np.arange(T)
    eye = np.eye(P)
    base = lay(BASE, {"ident": eye, "mean_d": np.full((P, P), 1.0 / D), "pick": np.tile((np.arange(16) == 8) / P, (P, 1)),
                      "center": eye - 1.0 / P, "resets": np.tile((t % CH != 0) * 1.0, (P, 1))})
    half = P // 2
    freq = (10000.0 ** (-np.arange(half, dtype=np.float32) / half)).astype(np.float32)
    ang = (t.astype(np.float32)[None, :] * freq[:, None]).astype(np.float32)
    cos, sin = np.cos(ang), np.sin(ang)
    swap = np.zeros((P, P))
    swap[(i + half) % P, i] = 1.0
    decay = np.zeros((P, HEADS, 384))
    gla = np.zeros((P, 384))
    for jt in range(TT):
        key, qs = jt * P + i[:, None], t[None, jt * P:]
        seen = key // CH <= qs // CH
        at = slice(0, T) if jt == 0 else slice(T, 384)
        for h in range(HEADS):
            lg = np.log1p(-(2.0 ** (-5.0 - h)))
            decay[:, h, at] = np.where(seen, np.exp(np.abs(qs - key) * lg), 0.0)
        gla[:, at] = seen * 64 ** -0.5
    causal = np.concatenate([np.zeros((P, P)), np.where(i[:, None] >= j[None, :], 0.0, NEG)], 1)
    sel = np.zeros((P, C_HEADS, P))
    for h in range(C_HEADS):
        sel[h, h, :] = 1.0
    tab1 = lay(TAB1, {"swap": swap, "cos": np.concatenate([cos, cos]), "sin": np.concatenate([-sin, sin]),
                      "decay": decay, "gla": gla, "causal": causal, "sel": sel[:, :HEADS]})
    bias = np.zeros((P, A_HEADS, T))
    qi = P + i[:, None]
    kj = t[None, :]
    near = (kj // CH <= qi // CH) & (kj // CH >= qi // CH - 2)
    for h in range(A_HEADS):
        bias[:, h] = np.where(near, -(2.0 ** -(h + 1.0)) * np.abs(qi - kj), NEG)
    taba = lay(TABA, {"bias": bias})
    level = np.zeros((P, LEVELS, P))
    for n in range(LEVELS):
        s = 2 ** n
        level[:, n] = (j[None, :] // (2 * s) == i[:, None] // (2 * s)) & (i[:, None] % (2 * s) < s) & (
            j[None, :] % (2 * s) >= s)
    tabc = lay(TABC, {"causal_t": np.where(i[:, None] <= j[None, :], 0.0, NEG),
                      "strict": (i[:, None] < j[None, :]) * 1.0, "level": level, "sel_c": sel})
    return {"base": base, "tab1": tab1, "taba": taba, "tabc": tabc}


def arrays_of(i):
    out_c = np.ascontiguousarray(np.broadcast_to(i["c"].reshape(1, D), (P, D)))

    def blocks(x):
        f = x.shape[1]
        return np.ascontiguousarray(x.T.reshape(f // P, P, T).transpose(1, 0, 2))
    out = {"stream": pack_stream(i), "vec": pack_vectors(i), "xT": blocks(i["x"][0]), "c_row": out_c}
    out.update(tables())
    rgw = np.zeros((P, 8, P), np.float32)
    for n, name in enumerate(("b_wa_2", "b_wx_2")):
        w = i[name][0]
        for b in range(8):
            s = slice((b % 2) * 64, (b % 2) * 64 + 64)
            rgw[s, 4 * n + b // 2, s] = w[b]
    out["rgw"] = rgw
    for l in range(DEPTH):
        a = np.zeros((48, 256), np.float32)
        a[32:48] = i["w_gla_a2"][l]
        out[f"wa2_{l}"] = a
        out[f"p{l}"] = blocks(i["p_2"][l, 0])
    return out


def make(nc, arrays, stages=None):
    ins = {n: nc.dram_tensor(f"in_{n}", a.shape, F32, kind="ExternalInput").ap() for n, a in arrays.items()}
    out = nc.dram_tensor("out", (P, KD, T), F32, kind="ExternalOutput").ap()
    build(nc, ins, out, stages)


def kernel(**inputs):
    import concourse.bacc as _bacc
    from concourse.bass_utils import run_bass_kernel_spmd as _run
    arrays = arrays_of({n: np.asarray(a) for n, a in inputs.items()})
    nc = _bacc.Bacc("TRN2", target_bir_lowering=False, num_devices=1)
    make(nc, arrays)
    r = _run(nc, [{f"in_{n}": a for n, a in arrays.items()}], core_ids=[0])
    got = np.asarray(r.results[0]["out"])
    return np.ascontiguousarray(got.transpose(1, 0, 2).reshape(D, T).T).reshape(1, T, D)
```
